# Optimizing a Trainium2 kernel written in Bass

```python
import jax, jax.numpy as jnp
from jax import lax
import numpy as np

D_MODEL = 1024
BATCH = 1
SEQ = 128
DEPTH = 2
DEC_BATCH = 1
DEC_SEQ = 256
PAST_LEN = 128

GRID_W = 64
N_HEADS = 8
N_KV_HEADS = 2
HEAD_DIM = 64
GQA_GROUP = N_HEADS // N_KV_HEADS
AXIS_ROPE_DIM = HEAD_DIM // 2
ROPE_THETA = 10000.0
Q_BLOCK = 128
ATT_Q = N_HEADS * HEAD_DIM
ATT_KV = N_KV_HEADS * HEAD_DIM
CONV_CH = 512
CONV_K = 31
FOURIER_GROUPS = 4
FOURIER_GROUP_CH = 128
FOURIER_CH = FOURIER_GROUPS * FOURIER_GROUP_CH
SGU_GROUPS = 4
SGU_GROUP_CH = 128
SGU_CH = SGU_GROUPS * SGU_GROUP_CH
CHUNK = 128
FFN_DIM = 2816
N_SUBLAYERS = 3
N_MOD = 3 * N_SUBLAYERS
EVEN_IN = ATT_Q + 2 * ATT_KV + 2 * CONV_CH
EVEN_OUT = ATT_Q + CONV_CH
ODD_IN = FOURIER_CH + 2 * SGU_CH
ODD_OUT = FOURIER_CH + SGU_CH
N_EVEN = (DEPTH + 1) // 2
N_ODD = DEPTH // 2
RMS_EPS = 1e-6
LN_EPS = 1e-5

kernel_name = 'hybrid_diffusion_prefix_trunk_step'

def rms_norm(x, g):
    xf = x.astype(jnp.float32)
    y = xf * lax.rsqrt(jnp.mean(xf * xf, axis=-1, keepdims=True) + RMS_EPS)
    return (y * g.astype(jnp.float32)).astype(x.dtype)

def layer_norm(x, g, b):
    xf = x.astype(jnp.float32)
    mu = jnp.mean(xf, axis=-1, keepdims=True)
    xc = xf - mu
    var = jnp.mean(xc * xc, axis=-1, keepdims=True)
    return (xc * lax.rsqrt(var + LN_EPS) * g.astype(jnp.float32) + b.astype(jnp.float32)).astype(x.dtype)

def adaln(cond, w, b):
    return (jax.nn.silu(cond) @ w + b).reshape(cond.shape[0], N_MOD, D_MODEL)

def modulate(x, g, shift, scale):
    return rms_norm(x, g) * (1 + scale) + shift

def swiglu(h, w_in, w_out):
    gate, up = jnp.split(h @ w_in, 2, axis=-1)
    return (jax.nn.silu(gate) * up) @ w_out

def rope_tables(rows):
    t = jnp.arange(rows * GRID_W)
    row = (t // GRID_W).astype(jnp.float32)
    col = (t % GRID_W).astype(jnp.float32)
    inv_freq = 1.0 / (ROPE_THETA ** (jnp.arange(0, AXIS_ROPE_DIM, 2, dtype=jnp.float32) / AXIS_ROPE_DIM))
    ang = jnp.concatenate([row[:, None] * inv_freq, col[:, None] * inv_freq], axis=-1)
    return jnp.cos(ang), jnp.sin(ang)

def apply_rope(x, cos, sin):
    xf = x.astype(jnp.float32).reshape(*x.shape[:-1], HEAD_DIM // 2, 2)
    x0, x1 = xf[..., 0], xf[..., 1]
    cs = cos[None, :, None, :]
    sn = sin[None, :, None, :]
    out = jnp.stack([x0 * cs - x1 * sn, x0 * sn + x1 * cs], axis=-1)
    return out.reshape(x.shape).astype(x.dtype)

def block_attention(q, k, v):
    bsz, lq = q.shape[0], q.shape[1]
    nb = lq // Q_BLOCK
    qb = q.reshape(bsz, nb, Q_BLOCK, N_KV_HEADS, GQA_GROUP, HEAD_DIM).swapaxes(0, 1)
    scale = HEAD_DIM ** -0.5

    def one_block(qblk):
        s = jnp.einsum('bqkgd,bskd->bkgqs', qblk, k).astype(jnp.float32) * scale
        p = jax.nn.softmax(s, axis=-1).astype(v.dtype)
        return jnp.einsum('bkgqs,bskd->bqkgd', p, v)

    out = lax.map(one_block, qb)
    return out.swapaxes(0, 1).reshape(bsz, lq, ATT_Q)

def depthwise_conv(x, w, b):
    y = lax.conv_general_dilated(
        x, w[:, None, :], window_strides=(1,), padding=[(CONV_K // 2, CONV_K // 2)],
        dimension_numbers=('NWC', 'WIO', 'NWC'), feature_group_count=x.shape[-1])
    return y + b

def even_mixer(h, w_in, w_out, q_g, k_g, conv_w, conv_b, cn_g, cn_b, rope, ctx_kv):
    bsz, length, _ = h.shape
    q, k, v, a = jnp.split(h @ w_in, [ATT_Q, ATT_Q + ATT_KV, ATT_Q + 2 * ATT_KV], axis=-1)
    q = rms_norm(q.reshape(bsz, length, N_HEADS, HEAD_DIM), q_g)
    k = rms_norm(k.reshape(bsz, length, N_KV_HEADS, HEAD_DIM), k_g)
    v = v.reshape(bsz, length, N_KV_HEADS, HEAD_DIM)
    if ctx_kv is None:
        own_kv = (k, v)
        attn = block_attention(q, k, v)
    else:
        cos, sin = rope
        ck, cv = ctx_kv
        attn = block_attention(apply_rope(q, cos, sin),
                               jnp.concatenate([ck, apply_rope(k, cos, sin)], axis=1),
                               jnp.concatenate([cv, v], axis=1))
        own_kv = None
    glu = a[..., :CONV_CH] * jax.nn.sigmoid(a[..., CONV_CH:])
    conv = jax.nn.silu(layer_norm(depthwise_conv(glu, conv_w, conv_b), cn_g, cn_b))
    return jnp.concatenate([attn, conv], axis=-1) @ w_out, own_kv

def odd_mixer(h, w_in, w_out, sn_g, sn_b, w_s, b_s):
    bsz, length, _ = h.shape
    f, u, v = jnp.split(h @ w_in, [FOURIER_CH, FOURIER_CH + SGU_CH], axis=-1)
    f = f.reshape(bsz, length, FOURIER_GROUPS, FOURIER_GROUP_CH).astype(jnp.float32)
    four = jnp.fft.fft2(f, axes=(1, 3), norm='ortho').real.astype(h.dtype).reshape(bsz, length, FOURIER_CH)
    v = layer_norm(v, sn_g, sn_b).reshape(bsz, length // CHUNK, CHUNK, SGU_GROUPS, SGU_GROUP_CH)
    v = jnp.einsum('gpq,bnqgc->bnpgc', w_s, v) + jnp.swapaxes(b_s, 0, 1)[:, :, None]
    sgu = u * v.reshape(bsz, length, SGU_CH)
    return jnp.concatenate([four, sgu], axis=-1) @ w_out, None

def macaron_layer(x, mod, norm_g, ffn_in, ffn_out, mixer):
    m = mod[:, :, None, :]
    x = x + 0.5 * m[:, 2] * swiglu(modulate(x, norm_g[0], m[:, 0], m[:, 1]), ffn_in[0], ffn_out[0])
    mixed, own_kv = mixer(modulate(x, norm_g[1], m[:, 3], m[:, 4]))
    x = x + m[:, 5] * mixed
    x = x + 0.5 * m[:, 8] * swiglu(modulate(x, norm_g[2], m[:, 6], m[:, 7]), ffn_in[1], ffn_out[1])
    return x, own_kv

def run_stream(x, cond, rope, ctx_k, ctx_v, w_mod, b_mod, norm_g, ffn_w_in, ffn_w_out,
               ev_w_in, ev_w_out, q_norm_g, k_norm_g, conv_w, conv_b, conv_norm_g, conv_norm_b,
               od_w_in, od_w_out, sgu_norm_g, sgu_norm_b, sgu_w, sgu_b):
    ks, vs = [], []
    for layer in range(DEPTH):
        mod = adaln(cond, w_mod[layer], b_mod[layer])
        j = layer // 2
        if layer % 2 == 0:
            ctx_kv = None if ctx_k is None else (ctx_k[:, j], ctx_v[:, j])

            def mixer(h):
                return even_mixer(h, ev_w_in[j], ev_w_out[j], q_norm_g[j], k_norm_g[j], conv_w[j],
                                  conv_b[j], conv_norm_g[j], conv_norm_b[j], rope, ctx_kv)
        else:
            def mixer(h):
                return odd_mixer(h, od_w_in[j], od_w_out[j], sgu_norm_g[j], sgu_norm_b[j],
                                 sgu_w[j], sgu_b[j])
        x, own_kv = macaron_layer(x, mod, norm_g[layer], ffn_w_in[layer], ffn_w_out[layer], mixer)
        if own_kv is not None:
            ks.append(own_kv[0])
            vs.append(own_kv[1])
    return x, ks, vs

def setup_inputs(seed: int = 0) -> dict:
    key = jax.random.key(seed)
    ks = jax.random.split(key, 25)

    def nrm(k, shape, s):
        return jax.random.normal(k, shape, jnp.float32) * s

    return {
        'x_prompt': nrm(ks[0], (BATCH, SEQ, D_MODEL), 1.0),
        'x_sample': nrm(ks[1], (DEC_BATCH, DEC_SEQ, D_MODEL), 1.0),
        'cache_k': nrm(ks[2], (DEC_BATCH, N_EVEN, PAST_LEN, N_KV_HEADS, HEAD_DIM), 1.0),
        'cache_v': nrm(ks[3], (DEC_BATCH, N_EVEN, PAST_LEN, N_KV_HEADS, HEAD_DIM), 1.0),
        'c': nrm(ks[4], (DEC_BATCH, D_MODEL), 1.0),
        'c_ctx': nrm(ks[5], (D_MODEL,), 1.0),
        'w_mod': nrm(ks[6], (DEPTH, D_MODEL, N_MOD * D_MODEL), 0.3 * D_MODEL ** -0.5),
        'b_mod': nrm(ks[7], (DEPTH, N_MOD * D_MODEL), 0.01),
        'norm_g': 1.0 + nrm(ks[8], (DEPTH, N_SUBLAYERS, D_MODEL), 0.05),
        'ffn_w_in': nrm(ks[9], (DEPTH, 2, D_MODEL, 2 * FFN_DIM), D_MODEL ** -0.5),
        'ffn_w_out': nrm(ks[10], (DEPTH, 2, FFN_DIM, D_MODEL), FFN_DIM ** -0.5),
        'ev_w_in': nrm(ks[11], (N_EVEN, D_MODEL, EVEN_IN), D_MODEL ** -0.5),
        'ev_w_out': nrm(ks[12], (N_EVEN, EVEN_OUT, D_MODEL), EVEN_OUT ** -0.5),
        'q_norm_g': 1.0 + nrm(ks[13], (N_EVEN, HEAD_DIM), 0.05),
        'k_norm_g': 1.0 + nrm(ks[14], (N_EVEN, HEAD_DIM), 0.05),
        'conv_w': nrm(ks[15], (N_EVEN, CONV_K, CONV_CH), CONV_K ** -0.5),
        'conv_b': nrm(ks[16], (N_EVEN, CONV_CH), 0.01),
        'conv_norm_g': 1.0 + nrm(ks[17], (N_EVEN, CONV_CH), 0.05),
        'conv_norm_b': nrm(ks[18], (N_EVEN, CONV_CH), 0.01),
        'od_w_in': nrm(ks[19], (N_ODD, D_MODEL, ODD_IN), D_MODEL ** -0.5),
        'od_w_out': nrm(ks[20], (N_ODD, ODD_OUT, D_MODEL), ODD_OUT ** -0.5),
        'sgu_norm_g': 1.0 + nrm(ks[21], (N_ODD, SGU_CH), 0.05),
        'sgu_norm_b': nrm(ks[22], (N_ODD, SGU_CH), 0.01),
        'sgu_w': nrm(ks[23], (N_ODD, SGU_GROUPS, CHUNK, CHUNK), CHUNK ** -0.5),
        'sgu_b': 1.0 + nrm(ks[24], (N_ODD, SGU_GROUPS, CHUNK), 0.01),
    }

def reference(x_prompt, x_sample, cache_k, cache_v, c, c_ctx, w_mod, b_mod, norm_g, ffn_w_in,
              ffn_w_out, ev_w_in, ev_w_out, q_norm_g, k_norm_g, conv_w, conv_b, conv_norm_g,
              conv_norm_b, od_w_in, od_w_out, sgu_norm_g, sgu_norm_b, sgu_w, sgu_b):
    weights = (w_mod, b_mod, norm_g, ffn_w_in, ffn_w_out, ev_w_in, ev_w_out, q_norm_g, k_norm_g,
               conv_w, conv_b, conv_norm_g, conv_norm_b, od_w_in, od_w_out, sgu_norm_g,
               sgu_norm_b, sgu_w, sgu_b)
    y_prompt, ctx_ks, ctx_vs = run_stream(x_prompt, c_ctx[None, :], None, None, None, *weights)
    new_cache_k = jnp.stack(ctx_ks, axis=1)
    new_cache_v = jnp.stack(ctx_vs, axis=1)
    rows = x_sample.shape[1] // GRID_W
    rope = rope_tables(rows)
    y_sample, _, _ = run_stream(x_sample, c, rope, cache_k, cache_v, *weights)
    return (y_prompt, y_sample, new_cache_k, new_cache_v)


_drawn_inputs = setup_inputs


def setup_inputs(seed=0):
    import zlib

    import numpy as np

    out = dict(_drawn_inputs(seed))
    spreads = {}
    factors = {'cache_k': 8.0,
     'cache_v': 8.0,
     'b_mod': 3.836,
     'q_norm_g': 8.0,
     'conv_b': 8.0,
     'conv_norm_g': 8.0,
     'conv_norm_b': 8.0,
     'sgu_norm_g': 8.0,
     'sgu_norm_b': 8.0,
     'sgu_b': 8.0}
    for name, (base, spread) in spreads.items():
        noise = np.random.default_rng([zlib.crc32(name.encode()), seed]).standard_normal(out[name].shape)
        drawn = base * np.exp(spread * noise) if base else spread * noise
        out[name] = __import__('jax').numpy.asarray(drawn.astype(out[name].dtype))
    for name, factor in factors.items():
        out[name] = (out[name] * factor).astype(out[name].dtype)
    return out
```

```python
from contextlib import ExitStack

import numpy as np

import concourse.bass as bass
import concourse.mybir as mybir

FP32 = mybir.dt.float32
F32R = mybir.dt.float32r
ALU = mybir.AluOpType
ACT = mybir.ActivationFunctionType
AX = mybir.AxisListType

P = 128
D_MODEL, CTX, LAT, PAST = 1024, 128, 256, 128
TOK = CTX + LAT
TT = TOK // P
SEGS = [(0, 0, CTX), (1, CTX, TOK)]
KT = D_MODEL // P
FFN = 2816
FT = FFN // P
HEADS, KV_HEADS, HD = 8, 2, 64
QT = HEADS * HD // P
GRID_W, THETA = 64, 10000.0
CONV_CH, CONV_K = 512, 31
CT = CONV_CH // P
PADW = CONV_K // 2
PAD_AT = [PADW, 2 * PADW + CTX]
PAD_N = 3 * PADW + TOK
CONV_N = PAD_N - (CONV_K - 1)
CONV_AT = [0, CTX + PADW]
N_MOD = 9
N_SUB = 6
MODT = N_MOD * KT
RMS_EPS, LN_EPS = 1e-6, 1e-5

RING = 3
UNIT = 2048
HALF = UNIT // 2
FFN_OUT_UNITS = FT // 2
FFN_UNITS = FT + FFN_OUT_UNITS
M0_UNITS, M1_UNITS = 11, 10
_sizes = [FFN_UNITS, M0_UNITS, FFN_UNITS, FFN_UNITS, M1_UNITS, FFN_UNITS]
UNIT0 = [sum(_sizes[:i]) for i in range(6)]
UNITS = sum(_sizes)

PAIRS_FIRST = 8
LOOPS = (FT - 1) // RING
MOD_LOOPS = {0: LOOPS, 2: LOOPS, 3: 5, 5: 0}
MOD_EXTRA = {0: 4, 2: 3, 3: 0, 5: 0}
PAIR0, _p = {}, PAIRS_FIRST
for _s in (0, 2, 3, 5):
    PAIR0[_s] = _p
    _p += RING * MOD_LOOPS[_s] + MOD_EXTRA[_s]
assert _p == 2 * MODT // 2
LAYER_PAIRS = MODT // 2

A_BMOD, A_NORM_G, A_ROWS = 0, MODT, MODT + N_SUB * KT
B_BMOD, B_C, B_CCTX = 0, MODT, MODT + KT
B_CONV_B = MODT + 2 * KT
B_CN_G, B_CN_B, B_SN_G, B_SN_B = (B_CONV_B + CT * i for i in range(1, 5))
B_QG = B_CONV_B + 5 * CT
B_KG, B_ROWS = B_QG + 1, B_QG + 2

R_SWAP, R_COS, R_SIN, R_N = 0, P, P + LAT, P + 2 * LAT
F_CH, F_LAT, F_CTX, F_N = 0, 2 * P, 2 * P + 4 * LAT, 2 * P + 4 * LAT + 2 * P


def shape_constants():
    ident = np.eye(P, dtype=np.float32)
    swap = ident.reshape(P // 2, 2, P)[:, ::-1].reshape(P, P)
    t = np.arange(LAT)
    row, col = (t // GRID_W).astype(np.float32), (t % GRID_W).astype(np.float32)
    half = HD // 2
    freq = (1.0 / np.float32(THETA) ** (np.arange(0, half, 2, dtype=np.float32) / np.float32(half))).astype(np.float32)
    ang = np.concatenate([row[:, None] * freq, col[:, None] * freq], axis=-1)
    cos = np.repeat(np.cos(ang), 2, axis=1).T
    sin = np.repeat(np.sin(ang), 2, axis=1).T * np.tile([-1.0, 1.0], half)[:, None]
    rope = np.concatenate([swap, np.tile(cos, (2, 1)), np.tile(sin, (2, 1))], axis=1)

    def dft(n):
        a = 2 * np.pi * (np.outer(np.arange(n), np.arange(n)) % n) / n
        return np.cos(a), np.sin(a)

    cc, cs = dft(P)
    lc, ls = dft(LAT)
    lat = np.concatenate([lc[0:P], -ls[0:P], lc[P:], -ls[P:]], axis=1)
    fourier = np.concatenate([cc, cs, lat, cc, -cs], axis=1)
    return (ident, np.ascontiguousarray(rope, dtype=np.float32), np.ascontiguousarray(fourier, dtype=np.float32))


def build(nc, x_prompt, x_sample, cache_k, cache_v, c, c_ctx, w_mod, b_mod, norm_g, ffn_w_in, ffn_w_out,
          ev_w_in, ev_w_out, q_norm_g, k_norm_g, conv_w, conv_b, conv_norm_g, conv_norm_b, od_w_in, od_w_out,
          sgu_norm_g, sgu_norm_b, sgu_w, sgu_b, k_ident, k_rope, k_fourier,
          y_prompt, y_sample, new_cache_k, new_cache_v):
    ctx = ExitStack()
    with ctx:
        def sb(name, shape, dt=FP32, stack=ctx):
            return stack.enter_context(nc.sbuf_tensor(name, shape, dt))

        def sem(name):
            return ctx.enter_context(nc.semaphore(name))

        w_raw = sb("w_raw", [P, RING, UNIT])
        w_hi = sb("w_hi", [P, RING, UNIT], F32R)
        w_lo = sb("w_lo", [P, RING, UNIT], F32R)
        m_raw = sb("m_raw", [P, RING, HALF])
        x = sb("x", [P, KT, TOK])
        a_hi = sb("a_hi", [P, KT, TOK], F32R)
        a_lo = sb("a_lo", [P, KT, TOK], F32R)
        ident = sb("ident", [P, P])
        ones = sb("ones", [P, P])
        ones_mean = sb("ones_mean", [P, P])
        vec_a = sb("vec_a", [P, A_ROWS])
        vec_b = sb("vec_b", [P, B_ROWS])
        conv_wt = sb("conv_wt", [P, CT, CONV_K])
        cond = sb("cond", [P, KT, 32])
        mod_pick = sb("mod_pick", [P, 2])
        mod_part = sb("mod_part", [P, 2 * P])
        mod_cols = sb("mod_cols", [P, 2 * MODT, 2])
        m_shift = sb("m_shift", [P, N_SUB, KT, 2])
        m_scale = sb("m_scale", [P, N_SUB, KT, 2])
        m_gate = sb("m_gate", [P, N_SUB, KT, 2])
        stat = sb("stat", [P, 32])
        stat_row = sb("stat_row", [P, 32])
        diag = sb("diag", [P, TT, P])
        glu = sb("glu", [P, RING, TOK])

        r = ExitStack()
        h_hi = sb("h_hi", [P, FT, TOK], F32R, r)
        h_lo = sb("h_lo", [P, FT, TOK], F32R, r)
        r.close()
        r = ExitStack()
        n_sq = sb("n_sq", [P, KT, TOK], stack=r)
        n_full = sb("n_full", [P, KT, TOK], stack=r)
        rows = sb("rows", [P, 2, P], stack=r)
        conv_rows = sb("conv_rows", [CONV_K, CONV_CH], stack=r)
        x_nat = sb("x_nat", [P, TT, D_MODEL], stack=r)
        r.close()
        r = ExitStack()
        padded = sb("padded", [P, CT, PAD_N], stack=r)
        conv = sb("conv", [P, CT, CONV_N], stack=r)
        e_sig = sb("e_sig", [P, 2, TOK], stack=r)
        qk = sb("qk", [P, QT + 1, TOK], stack=r)
        qk_sq = sb("qk_sq", [P, QT + 1, TOK], stack=r)
        qk_wide = sb("qk_wide", [P, 2 * TT * (QT + 1), HD], stack=r)
        v_raw = sb("v_raw", [P, TOK], stack=r)
        rope = sb("rope", [P, R_N], stack=r)
        pick_half = sb("pick_half", [P, 2], stack=r)
        rot = sb("rot", [P, QT + 1, LAT], stack=r)
        kdup = sb("kdup", [P, KV_HEADS, TOK + PAST], stack=r)
        ck_nat = sb("ck_nat", [P, P], stack=r)
        v_nat = sb("v_nat", [P, TT + 1, P], stack=r)
        k_nat = sb("k_nat", [P, P], stack=r)
        prob = sb("prob", [P, 2, TOK], stack=r)
        prob_t = sb("prob_t", [P, 2, TOK], stack=r)
        smax = sb("smax", [P, HEADS * TT], stack=r)
        smaxn = sb("smaxn", [P, HEADS * TT], stack=r)
        ssum = sb("ssum", [P, HEADS * TT], stack=r)
        srec = sb("srec", [P, HEADS * TT], stack=r)
        r.close()
        r = ExitStack()
        o_v = sb("o_v", [P, CT, TOK], stack=r)
        o_f = sb("o_f", [P, CT, TOK], stack=r)
        o_u = sb("o_u", [P, CT, TOK], stack=r)
        o_sq = sb("o_sq", [P, CT, TOK], stack=r)
        o_vn = sb("o_vn", [P, TT, CONV_CH], stack=r)
        o_z = sb("o_z", [P, TT, 2 * CONV_CH], stack=r)
        fourier = sb("fourier", [P, F_N], stack=r)
        ws_nat = sb("ws_nat", [P, CT, P], stack=r)
        ws_t = sb("ws_t", [P, CT, P], stack=r)
        bs = sb("bs", [P, CT, P], stack=r)
        r.close()

        ps = ctx.enter_context(nc.psum_tensor("ps", [P, 8, 512], FP32))

        raw_in = [sem(f"raw_in{i}") for i in range(RING)]
        hi_done = sem("hi_done")
        lo_done = sem("lo_done")
        unit_done = sem("unit_done")
        mod_in = [sem(f"mod_in{i}") for i in range(RING)]
        mod_used = sem("mod_used")
        part_copied = sem("part_copied")
        cols_done = sem("cols_done")
        cols_copied = sem("cols_copied")
        const_in, rows_in, x_in = sem("const_in"), sem("rows_in"), sem("x_in")
        setup = sem("setup")
        pick_ready = sem("pick_ready")
        rows_t, rows_c = sem("rows_t"), sem("rows_c")
        cond_ready = sem("cond_ready")
        x_t = sem("x_t")
        x_ready = sem("x_ready")
        y_done = sem("y_done")
        sq_done, stat_done, ms_done, root_done, diag_done, bc_done = (
            sem(n) for n in ("sq_done", "stat_done", "ms_done", "root_done", "diag_done", "bc_done"))
        full_done, a_hi_done, a_ready = sem("full_done"), sem("a_hi_done"), sem("a_ready")
        dve_self = sem("dve_self")
        silu_done, h_hi_done = sem("silu_done"), sem("h_hi_done")
        prod_done, h_ready = sem("prod_done"), sem("h_ready")
        out_in, out_t, out_c, out_done = sem("out_in"), sem("out_t"), sem("out_c"), sem("out_done")
        e_in, e_zero, sig_done, glu_done, conv_done = (
            sem(n) for n in ("e_in", "e_zero", "sig_done", "glu_done", "conv_done"))
        qk_copied, qk_sq_done, qk_stat, qk_ms, qk_root, qk_wide_done, qk_bc, qk_normed = (
            sem(n) for n in ("qk_copied", "qk_sq_done", "qk_stat", "qk_ms", "qk_root", "qk_wide_done",
                             "qk_bc", "qk_normed"))
        swap_done, roped, e_t, e_tc, kdup_done, cache_out = (
            sem(n) for n in ("swap_done", "roped", "e_t", "e_tc", "kdup_done", "cache_out"))
        score_done, max_done, exp_done, prob_done, pt_done, pt_copied, pv_done = (
            sem(n) for n in ("score_done", "max_done", "exp_done", "prob_done", "pt_done", "pt_copied", "pv_done"))
        mix_hi, mix_ready = sem("mix_hi"), sem("mix_ready")
        ln_mean_done, ln_meanc, ln_xc, ln_sq, ln_stat, ln_ms, ln_root, ln_diag, ln_bc, ln_y = (
            sem(n) for n in ("ln_mean_done", "ln_meanc", "ln_xc", "ln_sq", "ln_stat", "ln_ms", "ln_root",
                             "ln_diag", "ln_bc", "ln_y"))
        ln_out = sem("ln_out")
        o_in, o_copied, o_t, o_tc, o_z_done, o_z_copied, o_sgu, o_bias, o_four = (
            sem(n) for n in ("o_in", "o_copied", "o_t", "o_tc", "o_z_done", "o_z_copied", "o_sgu", "o_bias",
                             "o_four"))

        block = ctx.enter_context(nc.Block())

        def slot(u):
            return u % RING

        def half(tile, u, h):
            return tile[:, slot(u), h * HALF:(h + 1) * HALF]

        def ffn_of(s):
            return (0, 0) if s == 0 else (0, 1) if s == 2 else (1, 0) if s == 3 else (1, 1)

        @block.sync
        def _(sp):
            def load_unit(u, i, halves):
                sp.wait_ge(lo_done, u + 1 + RING * i)
                for h, src in enumerate(halves):
                    dst = half(w_raw, u, h).rearrange("p (a b) -> p a b", a=src.shape[1])
                    sp.dma_start(dst, src).then_inc(raw_in[slot(u)], 16)

            def cols(w, start, n=P):
                return w.rearrange("(k p) n -> p k n", p=P)[:, :, bass.ds(start, n)]

            def load_pair(pair, i, layer):
                w = w_mod[layer]
                for q in range(2):
                    n = 2 * pair + q
                    sp.wait_ge(mod_used, n + 1 + 2 * RING * i)
                    sp.dma_start(m_raw[:, n % RING, :].rearrange("p (a b) -> p a b", a=KT),
                                 cols(w, (n - layer * MODT) * P + i * 2 * RING * P)).then_inc(mod_in[n % RING], 16)

            def load_ffn(s):
                layer, which = ffn_of(s)
                win, wout = ffn_w_in[layer, which], ffn_w_out[layer, which]
                u0, p0 = UNIT0[s], PAIR0[s]

                def in_unit(u, t, i):
                    load_unit(u, i, [cols(win, h * FFN + t * P + i * RING * P) for h in range(2)])

                def out_unit(u, t, i):
                    load_unit(u, i, [wout[bass.ds((2 * t + h) * P + i * 2 * RING * P, P), :]
                                     .rearrange("p (a n) -> p a n", a=1) for h in range(2)])

                in_unit(u0, 0, 0)
                if s == 0:
                    for pair in range(1, PAIRS_FIRST):
                        load_pair(pair, 0, 0)
                in_unit(u0 + 1, 1, 0)
                in_unit(u0 + 2, 2, 0)
                mods = MOD_LOOPS[s]
                rounds = min(mods, LOOPS - 1)
                first = max(0, min(rounds, (LAYER_PAIRS - p0) // RING))
                parts = [(first, 0), (rounds - first, 1), (LOOPS - 1 - rounds, None)]
                done = 0
                for n, mod_layer in parts:
                    if n > 0:
                        with sp.Fori(0, n) as i:
                            for b in range(RING):
                                t = 1 + RING * done + b
                                in_unit(u0 + t + 2, t + 2, i)
                                if mod_layer is not None:
                                    load_pair(p0 + RING * done + b, i, mod_layer)
                        done += n
                for b in range(RING):
                    t = 1 + RING * done + b
                    if t + 2 < FT:
                        in_unit(u0 + t + 2, t + 2, 0)
                    else:
                        out_unit(u0 + t + 2, t + 2 - FT, 0)
                    if mods == LOOPS:
                        pair = p0 + RING * done + b
                        load_pair(pair, 0, pair // LAYER_PAIRS)
                for b in range(MOD_EXTRA[s]):
                    pair = p0 + RING * mods + b
                    load_pair(pair, 0, pair // LAYER_PAIRS)
                with sp.Fori(0, (FFN_OUT_UNITS - 2) // RING) as i:
                    for b in range(RING):
                        out_unit(u0 + FT + 2 + b, 2 + b, i)

            def load_proj_out(u, w, kt0, d0):
                load_unit(u, 0, [w[(kt0 + 2 * h) * P:(kt0 + 2 * h + 2) * P, d0 * P:(d0 + 4) * P]
                                 .rearrange("(k p) n -> p k n", p=P) for h in range(2)])

            sp.dma_start(ident[:], k_ident).then_inc(const_in, 16)
            for dst, src in (
                    (rows[0:MODT, 0, :], b_mod[0].rearrange("(r n) -> r n", n=P)),
                    (rows[A_NORM_G:A_ROWS, 0, :], norm_g.rearrange("l s (r n) -> (l s r) n", n=P)),
                    (rows[0:MODT, 1, :], b_mod[1].rearrange("(r n) -> r n", n=P)),
                    (rows[B_C:B_C + KT, 1, :], c[0].rearrange("(r n) -> r n", n=P)),
                    (rows[B_CCTX:B_CCTX + KT, 1, :], c_ctx.rearrange("(r n) -> r n", n=P)),
                    (rows[B_CONV_B:B_CONV_B + CT, 1, :], conv_b[0].rearrange("(r n) -> r n", n=P)),
                    (rows[B_CN_G:B_CN_G + CT, 1, :], conv_norm_g[0].rearrange("(r n) -> r n", n=P)),
                    (rows[B_CN_B:B_CN_B + CT, 1, :], conv_norm_b[0].rearrange("(r n) -> r n", n=P)),
                    (rows[B_SN_G:B_SN_G + CT, 1, :], sgu_norm_g[0].rearrange("(r n) -> r n", n=P)),
                    (rows[B_SN_B:B_SN_B + CT, 1, :], sgu_norm_b[0].rearrange("(r n) -> r n", n=P)),
                    (rows[B_QG:B_QG + 1, 1, 0:HD], q_norm_g), (rows[B_QG:B_QG + 1, 1, HD:P], q_norm_g),
                    (rows[B_KG:B_KG + 1, 1, 0:HD], k_norm_g), (rows[B_KG:B_KG + 1, 1, HD:P], k_norm_g),
                    (conv_rows[:, :], conv_w[0])):
                sp.dma_start(dst, src).then_inc(rows_in, 16)
            load_pair(0, 0, 0)
            sp.dma_start(x_nat[:, 0, :], x_prompt[0]).then_inc(x_in, 16)
            sp.dma_start(x_nat[:, 1:TT, :], x_sample[0].rearrange("(a p) n -> p a n", p=P)).then_inc(x_in, 16)
            load_ffn(0)
            u = UNIT0[1]
            a0 = (HEADS + 2 * KV_HEADS) * HD
            for j in range(CT):
                load_unit(u + j, 0, [cols(ev_w_in[0], a0 + h * CONV_CH + j * P) for h in range(2)])
            sp.wait_ge(a_ready, 2 * KT)
            sp.wait_ge(unit_done, RING + UNIT0[1])
            for dst, src in ((rope[:], k_rope), (ck_nat[:], cache_k[0, 0].rearrange("t g d -> t (g d)")),
                             (v_nat[:, TT, :], cache_v[0, 0].rearrange("t g d -> t (g d)"))):
                sp.dma_start(dst, src).then_inc(e_in, 16)
            for j in range(3):
                load_unit(u + CT + j, 0, [cols(ev_w_in[0], (2 * j + h) * P) for h in range(2)])
            for j, (kt0, d0) in enumerate(((0, 0), (0, 4), (4, 0), (4, 4))):
                load_proj_out(u + CT + 3 + j, ev_w_out[0], kt0, d0)
            load_ffn(2)
            load_ffn(3)
            u = UNIT0[4]
            for j, base in enumerate((8, 10, 0, 2, 4, 6)):
                load_unit(u + j, 0, [cols(od_w_in[0], (base + h) * P) for h in range(2)])
                if j == 3:
                    sp.wait_ge(a_ready, 5 * KT)
                    sp.wait_ge(unit_done, RING + u)
                    for dst, src in ((fourier[:], k_fourier), (ws_nat[:], sgu_w[0].rearrange("g p q -> p g q"))):
                        sp.dma_start(dst, src).then_inc(o_in, 16)
                    for g in range(CT):
                        sp.dma_start(bs[:, g, :], sgu_b[0, g:g + 1, :].to_broadcast([P, P])).then_inc(o_in, 16)
            for j, (kt0, d0) in enumerate(((0, 0), (0, 4), (4, 0), (4, 4))):
                load_proj_out(u + 6 + j, od_w_out[0], kt0, d0)
            load_ffn(5)
            for tt in range(TT):
                sp.wait_ge(out_c, tt + 1)
                dst = y_prompt[0] if tt == 0 else y_sample[0, (tt - 1) * P:tt * P, :]
                sp.dma_start(dst, x_nat[:, tt, :]).then_inc(out_done, 16)
            sp.wait_ge(out_done, 16 * TT)
            sp.wait_ge(cache_out, 32)

        @block.gpsimd
        def _(pool):
            nc.gpsimd.memset(ones[:], 1.0).then_inc(setup, 1)
            nc.gpsimd.memset(cond[:], 0.0).then_inc(setup, 1)
            nc.gpsimd.memset(ones_mean[:], 1.0 / CONV_CH).then_inc(setup, 1)
            pool.wait_ge(unit_done, RING + UNIT0[1])
            pool.wait_ge(a_ready, 2 * KT)
            nc.gpsimd.memset(padded[:], 0.0).then_inc(e_zero, 1)
            nc.gpsimd.memset(pick_half[:], 0.0).then_inc(e_zero, 1)
            pool.wait_ge(e_zero, 2)
            nc.gpsimd.memset(pick_half[0:HD, 0:1], 1.0).then_inc(e_zero, 1)
            nc.gpsimd.memset(pick_half[HD:P, 1:2], 1.0).then_inc(e_zero, 1)

        @block.scalar
        def _(act):
            def split(u, i=0):
                act.wait_ge(raw_in[slot(u)], 32 * (u // RING + 1) + 32 * i)
                act.wait_ge(unit_done, u + 1 + RING * i)
                nc.scalar.activation(w_hi[:, slot(u), :], w_raw[:, slot(u), :], ACT.Copy).then_inc(hi_done, 1)

            def norm(n):
                for d in range(KT):
                    act.wait_ge(x_ready, KT * n + d + 1)
                    nc.scalar.activation(n_sq[:, d, :], x[:, d, :], ACT.Square).then_inc(sq_done, 1)
                act.wait_ge(ms_done, n + 1)
                nc.scalar.activation(stat[:, 4:4 + TT], stat[:, 0:TT], ACT.Sqrt).then_inc(root_done, 1)
                for d in range(KT):
                    act.wait_ge(full_done, KT * n + d + 1)
                    nc.scalar.activation(a_hi[:, d, :], n_full[:, d, :], ACT.Copy).then_inc(a_hi_done, 1)

            def ffn(s):
                u0, f = UNIT0[s], FFN_AT[s]

                def step(t, b, i):
                    split(u0 + t + 2, i)
                    act.wait_ge(unit_done, RING + u0 + t + 1 + RING * i)
                    act.wait_ge(h_ready, FT * f + t + 1 + RING * i)
                    nc.scalar.activation(glu[:, b, :], ps[:, 2 * b, 0:TOK], ACT.Silu).then_inc(silu_done, 1)
                    act.wait_ge(prod_done, RING + FT * f + t + 1 + RING * i)
                    nc.scalar.activation(h_hi[:, bass.ds(t + RING * i, 1), :], glu[:, b:b + 1, :],
                                         ACT.Copy).then_inc(h_hi_done, 1)

                step(0, 0, 0)
                with act.Fori(0, LOOPS) as i:
                    for b in range(RING):
                        step(1 + b, (1 + b) % RING, i)
                split(u0 + FT + 2)
                ahead = min(FFN_UNITS - FT - 2, UNITS - (u0 + FT + 3))
                with act.Fori(0, ahead // RING) as i:
                    for b in range(RING):
                        split(u0 + FT + 3 + b, i)
                for b in range(ahead // RING * RING, ahead):
                    split(u0 + FT + 3 + b)
                if s < 5:
                    split(u0 + FFN_UNITS + 1)

            for v in range(2):
                act.wait_ge(rows_t, v + 1)
                nc.scalar.activation((vec_a, vec_b)[v][:], ps[:, v, 0:(A_ROWS, B_ROWS)[v]], ACT.Copy).then_inc(rows_c, 1)
            act.wait_ge(rows_t, 3)
            nc.scalar.activation(conv_wt[:], ps[:, 2, 0:CT * CONV_K].rearrange("p (a b) -> p a b", a=CT),
                                 ACT.Copy).then_inc(rows_c, 1)
            act.wait_ge(rows_c, 2)
            act.wait_ge(setup, 3)
            for i, col in enumerate((B_CCTX, B_C)):
                nc.scalar.activation(cond[:, :, i:i + 1], vec_b[:, col:col + KT].unsqueeze(2), ACT.Silu).then_inc(cond_ready, 1)
            split(0)
            norm(0)
            split(1)
            ffn(0)

            norm(1)
            u = UNIT0[1]
            for j in range(CT):
                split(u + j + 2)
                act.wait_ge(unit_done, RING + u + j + 1)
                if j >= 2:
                    act.wait_ge(glu_done, j - 1)
                nc.scalar.activation(e_sig[:, j % 2, :], ps[:, 2 * j + 1, 0:TOK], ACT.Sigmoid).then_inc(sig_done, 1)
            for j in range(3):
                split(u + CT + j + 2)
                act.wait_ge(unit_done, RING + u + CT + j + 1)
                for h in range(2):
                    dst = qk[:, 2 * j + h, :] if 2 * j + h <= QT else v_raw[:]
                    nc.scalar.activation(dst, ps[:, 2 * j + h, 0:TOK], ACT.Copy).then_inc(qk_copied, 1)
                    if 2 * j + h <= QT:
                        act.wait_ge(qk_copied, 2 * j + h + 1)
                        nc.scalar.activation(qk_sq[:, 2 * j + h, :], dst, ACT.Square).then_inc(qk_sq_done, 1)
            split(u + 9)
            act.wait_ge(qk_ms, 1)
            nc.scalar.activation(stat_row[:, 0:30], stat[:, 0:30], ACT.Sqrt).then_inc(qk_root, 1)
            act.wait_ge(e_t, 1)
            nc.scalar.activation(v_nat[:, 0:TT, :], ps[:, 7, 0:TOK].rearrange("p (a b) -> p a b", a=TT),
                                 ACT.Copy).then_inc(e_tc, 1)
            for g in range(KV_HEADS):
                for o in range(2):
                    nc.scalar.activation(kdup[o * HD:(o + 1) * HD, g, TOK:], ps[g * HD:(g + 1) * HD, 5, 0:PAST],
                                         ACT.Copy).then_inc(kdup_done, 1)
            act.wait_ge(e_t, 2)
            nc.scalar.activation(k_nat[:], ps[:, 6, 0:P], ACT.Copy).then_inc(e_tc, 1)
            act.wait_ge(e_tc, 2)
            act.dma_start(new_cache_k[0, 0].rearrange("t g d -> t (g d)"), k_nat[:]).then_inc(cache_out, 16)
            act.dma_start(new_cache_v[0, 0].rearrange("t g d -> t (g d)"), v_nat[:, 0, :]).then_inc(cache_out, 16)
            N = HEADS * TT
            for n in range(N + 1):
                if n < N:
                    width = CTX if n % TT == 0 else LAT + PAST
                    act.wait_ge(max_done, n + 1)
                    if n >= 2:
                        act.wait_ge(pt_done, n - 1)
                    nc.scalar.activation(prob[:, n % 2, 0:width], ps[:, 4 + n % 2, 0:width], ACT.Exp,
                                         bias=smaxn[:, n:n + 1], scale=HD ** -0.5,
                                         accum_out=ssum[:, n:n + 1]).then_inc(exp_done, 1)
                if n >= 1:
                    m = n - 1
                    width = CTX if m % TT == 0 else LAT + PAST
                    act.wait_ge(pt_done, m + 1)
                    if m >= 2:
                        act.wait_ge(pv_done, m - 1)
                    nc.scalar.activation(prob_t[:, m % 2, 0:width], ps[:, 6 + m % 2, 0:width], ACT.Copy).then_inc(pt_copied, 1)
            act.wait_ge(pv_done, N)
            for j in range(QT):
                nc.scalar.activation(a_hi[:, j, :], ps[:, j, 0:TOK], ACT.Copy).then_inc(mix_hi, 1)

            def layer_norm_root(m, src):
                for j in range(CT):
                    act.wait_ge(ln_xc, CT * m + j + 1)
                    nc.scalar.activation(qk_sq[:, j, :] if m == 0 else o_sq[:, j, :], src[:, j, :],
                                         ACT.Square).then_inc(ln_sq, 1)
                act.wait_ge(ln_ms, m + 1)
                nc.scalar.activation(stat_row[:, 0:TT], stat[:, 0:TT], ACT.Sqrt).then_inc(ln_root, 1)

            layer_norm_root(0, qk)
            split(u + 10)
            for j in range(CT):
                act.wait_ge(ln_y, j + 1)
                nc.scalar.activation(qk[:, j, :], qk_sq[:, j, :], ACT.Silu, bias=vec_b[:, B_CN_B + j:B_CN_B + j + 1],
                                     scale=vec_b[:, B_CN_G + j:B_CN_G + j + 1]).then_inc(ln_out, 1)
                act.wait_ge(ln_out, j + 1)
                nc.scalar.activation(a_hi[:, QT + j, :], qk[:, j, :], ACT.Copy).then_inc(mix_hi, 1)
            split(u + 11)
            split(u + 12)
            act.wait_ge(cache_out, 32)
            norm(2)
            ffn(2)
            norm(3)
            ffn(3)

            norm(4)
            u = UNIT0[4]
            for j in range(6):
                split(u + j + 2)
                act.wait_ge(unit_done, RING + u + j + 1)
                for h in range(2):
                    n = 2 * j + h
                    dst = (o_v, o_f, o_u)[n // CT][:, n % CT, :]
                    nc.scalar.activation(dst, ps[:, O_BANK[j] + h, 0:TOK], ACT.Copy).then_inc(o_copied, 1)
                if j == 2:
                    for k in range(CT):
                        act.wait_ge(ln_xc, CT + k + 1)
                        nc.scalar.activation(o_sq[:, k, :], o_v[:, k, :], ACT.Square).then_inc(ln_sq, 1)
                if j == 4:
                    act.wait_ge(ln_ms, 2)
                    nc.scalar.activation(stat_row[:, 0:TT], stat[:, 0:TT], ACT.Sqrt).then_inc(ln_root, 1)
            split(u + 8)
            for j in range(CT):
                act.wait_ge(ln_y, CT + j + 1)
                nc.scalar.activation(o_v[:, j, :], o_sq[:, j, :], ACT.Identity, bias=vec_b[:, B_SN_B + j:B_SN_B + j + 1],
                                     scale=vec_b[:, B_SN_G + j:B_SN_G + j + 1]).then_inc(ln_out, 1)
            act.wait_ge(o_t, 1)
            nc.scalar.activation(ws_t[:], ps[:, 0, :].rearrange("p (a b) -> p a b", a=CT), ACT.Copy).then_inc(o_tc, 1)
            for tt in range(TT):
                act.wait_ge(o_t, tt + 2)
                nc.scalar.activation(o_vn[:, tt, :], ps[:, 1 + tt, :], ACT.Copy).then_inc(o_tc, 1)
            for tt in range(TT):
                for h in range(2):
                    n = 2 * tt + h
                    act.wait_ge(o_z_done, n + 1)
                    nc.scalar.activation(o_z[:, tt, h * 512:(h + 1) * 512], ps[:, O_ZBANK[n], :], ACT.Copy).then_inc(o_z_copied, 1)
            for g in range(CT):
                act.wait_ge(o_four, g + 1)
                for _, lo, hi in SEGS:
                    nc.scalar.activation(a_hi[:, g, lo:hi], ps[:, 4 + g, lo:hi], ACT.Copy,
                                         scale=float((hi - lo) * P) ** -0.5).then_inc(mix_hi, 1)
            for g in range(CT):
                act.wait_ge(o_bias, g + 1)
                nc.scalar.activation(a_hi[:, CT + g, :], o_sq[:, g, :], ACT.Copy).then_inc(mix_hi, 1)
            split(u + 9)
            split(u + 10)
            split(u + 11)
            norm(5)
            ffn(5)
            for tt in range(TT):
                act.wait_ge(out_t, tt + 1)
                nc.scalar.activation(x_nat[:, tt, :].rearrange("p (a b) -> p a b", a=2), ps[:, 2 * tt:2 * tt + 2, :],
                                     ACT.Copy).then_inc(out_c, 1)

        @block.vector
        def _(dve):
            self_n = [0]

            def mark(ins):
                ins.then_inc(dve_self, 1)
                self_n[0] += 1
                return self_n[0]

            def split(u, i=0):
                dve.wait_ge(hi_done, u + 1 + RING * i)
                nc.vector.tensor_tensor(w_lo[:, slot(u), :], w_raw[:, slot(u), :], w_hi[:, slot(u), :].bitcast(FP32),
                                        ALU.subtract).then_inc(lo_done, 1)

            def part_copy(pair, i=0):
                dve.wait_ge(mod_used, RING + 2 * pair + 2 + 2 * RING * i)
                if pair:
                    dve.wait_ge(cols_done, pair + RING * i)
                nc.vector.tensor_copy(mod_part[:], ps[:, 6, 0:2 * P]).then_inc(part_copied, 1)

            def cols_copy(pair, i=0):
                dve.wait_ge(cols_done, pair + 1 + RING * i)
                nc.vector.tensor_copy(mod_cols[:, bass.ds(2 * pair + 2 * RING * i, 2), :],
                                      ps[:, 7, 0:4].rearrange("p (a b) -> p a b", a=2)).then_inc(cols_copied, 1)

            def bias(s, which):
                layer, m = s // 3, 3 * (s % 3) + which
                v, base = (vec_a, A_BMOD) if layer == 0 else (vec_b, B_BMOD)
                return v[:, base + m * KT:base + (m + 1) * KT].unsqueeze(2).to_broadcast([P, KT, 2])

            def raw_mod(s, which):
                t = (s // 3) * MODT + (3 * (s % 3) + which) * KT
                return mod_cols[:, t:t + KT, :]

            def modulation_in(s):
                dve.wait_ge(rows_c, 2)
                dve.wait_ge(cols_copied, 1 + 12 * s + 8)
                mark(nc.vector.tensor_tensor(m_shift[:, s], raw_mod(s, 0), bias(s, 0), ALU.add))
                dve.wait_ge(dve_self, mark(nc.vector.tensor_tensor(m_scale[:, s], raw_mod(s, 1), bias(s, 1), ALU.add)))
                g = vec_a[:, A_NORM_G + s * KT:A_NORM_G + (s + 1) * KT].unsqueeze(2).to_broadcast([P, KT, 2])
                dve.wait_ge(dve_self, mark(nc.vector.scalar_tensor_tensor(
                    m_scale[:, s], m_scale[:, s], 1.0, g, ALU.add, ALU.mult)))

            def modulation_gate(s):
                dve.wait_ge(cols_copied, 1 + 12 * (s + 1))
                n = mark(nc.vector.tensor_tensor(m_gate[:, s], raw_mod(s, 2), bias(s, 2), ALU.add))
                dve.wait_ge(dve_self, n)
                if s % 3 != 1:
                    dve.wait_ge(dve_self, mark(nc.vector.tensor_scalar(m_gate[:, s], m_gate[:, s], 0.5, None, ALU.mult)))

            def residual(s, d):
                for cnd, lo, hi in SEGS:
                    ins = nc.vector.scalar_tensor_tensor(x[:, d, lo:hi], ps[:, d, lo:hi], m_gate[:, s, d, cnd:cnd + 1],
                                                         x[:, d, lo:hi], ALU.mult, ALU.add)
                ins.then_inc(x_ready, 1)

            def norm(n):
                dve.wait_ge(stat_done, n + 1)
                nc.vector.tensor_scalar(stat[:, 0:TT], ps[:, 0, 0:TT], 1.0 / D_MODEL, RMS_EPS,
                                        ALU.mult, ALU.add).then_inc(ms_done, 1)
                dve.wait_ge(root_done, n + 1)
                dve.wait_ge(dve_self, mark(nc.vector.reciprocal(stat[:, 8:8 + TT], stat[:, 4:4 + TT])))
                for tt in range(TT):
                    ins = nc.vector.tensor_scalar(diag[:, tt, :], ident[:], stat[:, 8 + tt:9 + tt], None, ALU.mult)
                ins.then_inc(diag_done, 1)
                dve.wait_ge(bc_done, n + 1)
                at = {}
                for d in range(KT + 2):
                    if d < KT:
                        at[d] = mark(nc.vector.tensor_tensor(n_full[:, d, :], x[:, d, :], ps[:, 7, 0:TOK], ALU.mult))
                    if 1 <= d <= KT:
                        e = d - 1
                        dve.wait_ge(dve_self, at[e])
                        for cnd, lo, hi in SEGS:
                            ins = nc.vector.tensor_scalar(n_full[:, e, lo:hi], n_full[:, e, lo:hi],
                                                          m_scale[:, n, e, cnd:cnd + 1], m_shift[:, n, e, cnd:cnd + 1],
                                                          ALU.mult, ALU.add)
                        ins.then_inc(full_done, 1)
                    if d >= 2:
                        e = d - 2
                        dve.wait_ge(a_hi_done, KT * n + e + 1)
                        nc.vector.tensor_tensor(a_lo[:, e, :], n_full[:, e, :], a_hi[:, e, :].bitcast(FP32),
                                                ALU.subtract).then_inc(a_ready, 1)

            def ffn(s):
                u0, f, p0 = UNIT0[s], FFN_AT[s], PAIR0[s]

                def step(t, b, i, pair):
                    split(u0 + t + 2, i)
                    if pair is not None:
                        part_copy(pair, i)
                    dve.wait_ge(silu_done, FT * f + t + 1 + RING * i)
                    nc.vector.tensor_tensor(glu[:, b, :], glu[:, b, :], ps[:, 2 * b + 1, 0:TOK],
                                            ALU.mult).then_inc(prod_done, 1)
                    dve.wait_ge(h_hi_done, FT * f + t + 1 + RING * i)
                    nc.vector.tensor_tensor(h_lo[:, bass.ds(t + RING * i, 1), :], glu[:, b:b + 1, :],
                                            h_hi[:, bass.ds(t + RING * i, 1), :].bitcast(FP32),
                                            ALU.subtract).then_inc(h_ready, 1)
                    if pair is not None:
                        cols_copy(pair, i)

                step(0, 0, 0, None)
                done = 0
                for n, mod in ((MOD_LOOPS[s], True), (LOOPS - MOD_LOOPS[s], False)):
                    if n:
                        with dve.Fori(0, n) as i:
                            for b in range(RING):
                                t = 1 + RING * done + b
                                step(t, (1 + b) % RING, i, p0 + b if mod else None)
                        done += n
                for b in range(MOD_EXTRA[s]):
                    part_copy(p0 + RING * MOD_LOOPS[s] + b)
                    cols_copy(p0 + RING * MOD_LOOPS[s] + b)
                split(u0 + FT + 2)
                ahead = min(FFN_UNITS - FT - 2, UNITS - (u0 + FT + 3))
                with dve.Fori(0, ahead // RING) as i:
                    for b in range(RING):
                        split(u0 + FT + 3 + b, i)
                for b in range(ahead // RING * RING, ahead):
                    split(u0 + FT + 3 + b)
                if s < 5:
                    modulation_in(s + 1)
                modulation_gate(s)
                if s < 5:
                    split(u0 + FFN_UNITS + 1)
                for d in range(KT):
                    if d < KT - 1:
                        dve.wait_ge(y_done, (KT - 1) * f + M_Y[s] + d + 1)
                    else:
                        dve.wait_ge(unit_done, RING + u0 + FFN_UNITS)
                    residual(s, d)

            dve.sem_inc(lo_done, RING)
            dve.sem_inc(part_copied, 1)
            dve.sem_inc(cols_copied, 1)
            dve.sem_inc(prod_done, RING)
            dve.sem_inc(h_ready, RING)
            dve.wait_ge(const_in, 16)
            nc.vector.tensor_reduce(mod_pick[:], ident[:].rearrange("p (a b) -> p b a", a=4)[:, 0:2, :], axis=AX.X,
                                    op=ALU.add).then_inc(pick_ready, 1)
            for d in range(KT):
                dve.wait_ge(x_t, d + 1)
                nc.vector.tensor_copy(x[:, d, :], ps[:, d % 6, 0:TOK]).then_inc(x_ready, 1)
            split(0)
            for pair in range(PAIRS_FIRST):
                part_copy(pair)
                cols_copy(pair)
            modulation_in(0)
            norm(0)
            split(1)
            ffn(0)

            norm(1)
            u = UNIT0[1]
            tap_at = {}

            def taps(pair, k0, k1):
                for k in range(k0, k1):
                    for j in (2 * pair, 2 * pair + 1):
                        if k == 0:
                            ins = nc.vector.tensor_scalar(conv[:, j, :], padded[:, j, 0:CONV_N], conv_wt[:, j, 0:1],
                                                          vec_b[:, B_CONV_B + j:B_CONV_B + j + 1], ALU.mult, ALU.add)
                        else:
                            dve.wait_ge(dve_self, tap_at[j])
                            ins = nc.vector.scalar_tensor_tensor(conv[:, j, :], padded[:, j, k:k + CONV_N],
                                                                 conv_wt[:, j, k:k + 1], conv[:, j, :], ALU.mult, ALU.add)
                        if k < CONV_K - 1:
                            tap_at[j] = mark(ins)
                        else:
                            ins.then_inc(conv_done, 1)

            def glu_mul(j):
                dve.wait_ge(sig_done, j + 1)
                dve.wait_ge(e_zero, 1)
                for sgm, lo, hi in SEGS:
                    ins = nc.vector.tensor_tensor(padded[:, j, PAD_AT[sgm]:PAD_AT[sgm] + hi - lo],
                                                  e_sig[:, j % 2, lo:hi], ps[:, 2 * j, lo:hi], ALU.mult)
                ins.then_inc(glu_done, 1)

            for j in range(CT):
                split(u + j + 2)
                glu_mul(j)
                if j == 2:
                    dve.wait_ge(glu_done, 2)
                    dve.wait_ge(rows_c, 3)
                    taps(0, 0, 7)
            taps(0, 7, 10)
            split(u + 6)
            taps(0, 10, 20)
            split(u + 7)
            taps(0, 20, CONV_K)
            split(u + 8)
            NS = 2 * TT * (QT + 1)
            dve.wait_ge(qk_stat, 1)
            nc.vector.tensor_scalar(stat[:, 0:NS], ps[:, 6, 256:256 + NS], 1.0 / HD, RMS_EPS, ALU.mult, ALU.add).then_inc(qk_ms, 1)
            split(u + 9)
            dve.wait_ge(qk_root, 1)
            dve.wait_ge(dve_self, mark(nc.vector.reciprocal(stat_row[:, 0:NS], stat_row[:, 0:NS])))
            nc.vector.tensor_copy(qk_wide[:], stat_row[:, 0:NS].unsqueeze(2).to_broadcast([P, NS, HD])).then_inc(qk_wide_done, 1)
            for j in range(QT + 1):
                dve.wait_ge(qk_bc, j + 1)
                col = B_QG if j < QT else B_KG
                nc.vector.scalar_tensor_tensor(qk[:, j, :], qk[:, j, :], vec_b[:, col:col + 1], ps[:, j, 0:TOK],
                                               ALU.mult, ALU.mult).then_inc(qk_normed, 1)
            dve.wait_ge(e_in, 48)
            dve.wait_ge(qk_normed, QT + 1)
            a = mark(nc.vector.tensor_tensor(rot[:], qk[:, :, CTX:], rope[:, R_COS:R_COS + LAT].unsqueeze(1)
                                             .to_broadcast([P, QT + 1, LAT]), ALU.mult))
            dve.wait_ge(dve_self, a)
            dve.wait_ge(swap_done, 1)
            a = mark(nc.vector.tensor_tensor(qk[:, 0:4, CTX:], ps[:, 0:2, :].rearrange("p a (c b) -> p (a c) b", c=2),
                                             rope[:, R_SIN:R_SIN + LAT].unsqueeze(1).to_broadcast([P, 4, LAT]), ALU.mult))
            a = mark(nc.vector.tensor_tensor(qk[:, 4, CTX:], ps[:, 2, 0:LAT], rope[:, R_SIN:R_SIN + LAT], ALU.mult))
            dve.wait_ge(dve_self, a)
            nc.vector.tensor_tensor(qk[:, :, CTX:], qk[:, :, CTX:], rot[:], ALU.add).then_inc(roped, 1)
            dve.wait_ge(roped, 1)
            for g in range(KV_HEADS):
                for o in range(2):
                    nc.vector.tensor_copy(kdup[o * HD:(o + 1) * HD, g, 0:TOK], qk[g * HD:(g + 1) * HD, QT, :]).then_inc(roped, 1)

            def attention(n):
                width = CTX if n % TT == 0 else LAT + PAST
                dve.wait_ge(score_done, n + 1)
                a = mark(nc.vector.tensor_reduce(smax[:, n:n + 1], ps[:, 4 + n % 2, 0:width], axis=AX.X, op=ALU.max))
                dve.wait_ge(dve_self, a)
                nc.vector.tensor_scalar(smaxn[:, n:n + 1], smax[:, n:n + 1], -(HD ** -0.5), None, ALU.mult).then_inc(max_done, 1)

            def normalize(n):
                width = CTX if n % TT == 0 else LAT + PAST
                dve.wait_ge(exp_done, n + 1)
                dve.wait_ge(dve_self, mark(nc.vector.reciprocal(srec[:, n:n + 1], ssum[:, n:n + 1])))
                nc.vector.tensor_scalar(prob[:, n % 2, 0:width], prob[:, n % 2, 0:width], srec[:, n:n + 1], None,
                                        ALU.mult).then_inc(prob_done, 1)

            N = HEADS * TT
            dve.wait_ge(glu_done, CT)
            attention(0)
            k = 0
            for n in range(N):
                if n + 1 < N:
                    attention(n + 1)
                normalize(n)
                m = 2 if n < CONV_K - N else 1
                taps(1, k, k + m)
                k += m

            def layer_norm(m, src, dst, sq, at):
                dve.wait_ge(ln_mean_done, m + 1)
                for j in range(CT):
                    for sgm, lo, hi in SEGS:
                        ins = nc.vector.tensor_tensor(dst[:, j, lo:hi], src[:, j, at[sgm]:at[sgm] + hi - lo],
                                                      ps[:, 4, lo:hi], ALU.subtract)
                    ins.then_inc(ln_xc, 1)

            def layer_norm_scale(m):
                dve.wait_ge(ln_stat, m + 1)
                nc.vector.tensor_scalar(stat[:, 0:TT], ps[:, 5, 0:TT], 1.0 / CONV_CH, LN_EPS, ALU.mult, ALU.add).then_inc(ln_ms, 1)
                dve.wait_ge(ln_root, m + 1)
                dve.wait_ge(dve_self, mark(nc.vector.reciprocal(stat[:, 8:8 + TT], stat_row[:, 0:TT])))
                for tt in range(TT):
                    ins = nc.vector.tensor_scalar(diag[:, tt, :], ident[:], stat[:, 8 + tt:9 + tt], None, ALU.mult)
                ins.then_inc(ln_diag, 1)

            def mix_low(j, src):
                dve.wait_ge(mix_hi, j + 1)
                nc.vector.tensor_tensor(a_lo[:, j, :], src, a_hi[:, j, :].bitcast(FP32), ALU.subtract).then_inc(mix_ready, 1)

            for j in range(QT):
                mix_low(j, ps[:, j, 0:TOK])
            layer_norm(0, conv, qk, qk_sq, CONV_AT)
            layer_norm_scale(0)
            split(u + 10)
            dve.wait_ge(ln_bc, 1)
            for j in range(CT):
                nc.vector.tensor_tensor(qk_sq[:, j, :], qk[:, j, :], ps[:, 5, 0:TOK], ALU.mult).then_inc(ln_y, 1)
            for j in range(CT):
                mix_low(QT + j, qk[:, j, :])
            modulation_in(2)
            modulation_gate(1)
            split(u + 11)
            split(u + 12)
            for d in range(KT):
                if d % 4 < 3:
                    dve.wait_ge(y_done, (KT - 1) + (d // 4) * 3 + d % 4 + 1)
                else:
                    dve.wait_ge(unit_done, RING + u + 10 + d // 4)
                residual(1, d)
            norm(2)
            ffn(2)
            norm(3)
            ffn(3)

            norm(4)
            u = UNIT0[4]
            split(u + 2)
            split(u + 3)
            split(u + 4)
            layer_norm(1, o_v, o_v, o_sq, [0, CTX])
            split(u + 5)
            split(u + 6)
            layer_norm_scale(1)
            split(u + 7)
            dve.wait_ge(ln_bc, 2)
            for j in range(CT):
                nc.vector.tensor_tensor(o_sq[:, j, :], o_v[:, j, :], ps[:, 5, 0:TOK], ALU.mult).then_inc(ln_y, 1)
            split(u + 8)
            for g in range(CT):
                dve.wait_ge(mix_hi, 2 * QT + 2 * g + 2)
                for _, lo, hi in SEGS:
                    ins = nc.vector.scalar_tensor_tensor(a_lo[:, g, lo:hi], ps[:, 4 + g, lo:hi], float((hi - lo) * P) ** -0.5,
                                                         a_hi[:, g, lo:hi].bitcast(FP32), ALU.mult, ALU.subtract)
                ins.then_inc(mix_ready, 1)
            dve.wait_ge(o_in, 16 * (2 + CT))
            dve.wait_ge(ln_out, 2 * CT)
            for g in range(CT):
                dve.wait_ge(o_sgu, g + 1)
                a = mark(nc.vector.tensor_tensor(o_sq[:, g, :].rearrange("p (a b) -> p a b", a=TT),
                                                 ps[:, g, 0:TOK].rearrange("p (a b) -> p a b", a=TT),
                                                 bs[:, g:g + 1, :].to_broadcast([P, TT, P]), ALU.add))
                dve.wait_ge(dve_self, a)
                dve.wait_ge(o_copied, 12)
                nc.vector.tensor_tensor(o_sq[:, g, :], o_sq[:, g, :], o_u[:, g, :], ALU.mult).then_inc(o_bias, 1)
            for g in range(CT):
                dve.wait_ge(mix_hi, 2 * QT + 2 * CT + g + 1)
                nc.vector.tensor_tensor(a_lo[:, CT + g, :], o_sq[:, g, :], a_hi[:, CT + g, :].bitcast(FP32),
                                        ALU.subtract).then_inc(mix_ready, 1)
            modulation_in(5)
            modulation_gate(4)
            split(u + 9)
            split(u + 10)
            split(u + 11)
            for d in range(KT):
                if d % 4 < 3:
                    dve.wait_ge(y_done, 3 * (KT - 1) + 6 + (d // 4) * 3 + d % 4 + 1)
                else:
                    dve.wait_ge(unit_done, RING + u + 9 + d // 4)
                residual(4, d)
            norm(5)
            ffn(5)

        @block.tensor
        def _(pe):
            mm = nc.tensor.matmul

            def three(out, whi, wlo, mhi, mlo, start, stop):
                mm(out, whi, mhi, start=start, stop=False)
                mm(out, whi, mlo, start=False, stop=False)
                return mm(out, wlo, mhi, start=False, stop=stop)

            def tile_of(w, u, n):
                return w[:, slot(u), n * P:(n + 1) * P]

            def in_unit(u, banks, n=None, i=0):
                pe.wait_ge(lo_done, RING + u + 1 + RING * i)
                for k in range(KT):
                    if n is not None:
                        pe.wait_ge(a_ready, KT * n + k + 1)
                    for h in range(2):
                        ins = three(ps[:, banks + h, 0:TOK], tile_of(w_hi, u, h * KT + k), tile_of(w_lo, u, h * KT + k),
                                    a_hi[:, k, :], a_lo[:, k, :], k == 0, k == KT - 1)
                ins.then_inc(unit_done, 1)

            def mod_sums(pair, i=0):
                pe.wait_ge(part_copied, pair + 1 + RING * i)
                for q in range(2):
                    n = 2 * pair + q
                    pe.wait_ge(mod_in[n % RING], 16 * (n // RING + 1) + 32 * i)
                    for k in range(KT):
                        j = k % 4
                        ins = mm(ps[32 * j:32 * j + 32, 6, q * P:(q + 1) * P], cond[:, k, :],
                                 m_raw[:, n % RING, k * P:(k + 1) * P], start=k < 4, stop=k >= 4)
                    ins.then_inc(mod_used, 1)

            def mod_columns(pair, i=0):
                pe.wait_ge(part_copied, pair + 2 + RING * i)
                pe.wait_ge(cols_copied, pair + 1 + RING * i)
                for q in range(2):
                    ins = mm(ps[:, 7, 2 * q:2 * q + 2], mod_part[:, q * P:(q + 1) * P], mod_pick[:], start=True, stop=True)
                ins.then_inc(cols_done, 1)

            def token_sums(out, src, k, last):
                for tt in range(TT):
                    ins = mm(out[:, tt:tt + 1], src[:, tt * P:(tt + 1) * P], ones[:, 0:1], start=(k == 0 and tt == 0),
                             stop=last, skip_group_check=True)
                return ins

            def spread(bank):
                for tt in range(TT):
                    ins = mm(ps[:, bank, tt * P:(tt + 1) * P], ones[:], diag[:, tt, :], start=True, stop=True)
                return ins

            def norm(n):
                for d in range(KT):
                    pe.wait_ge(sq_done, KT * n + d + 1)
                    ins = token_sums(ps[:, 0, :], n_sq[:, d, :], d, d == KT - 1)
                ins.then_inc(stat_done, 1)
                pe.wait_ge(diag_done, n + 1)
                spread(7).then_inc(bc_done, 1)

            def ffn(s):
                u0, f, p0 = UNIT0[s], FFN_AT[s], PAIR0[s]

                def step(t, b, i, pair, n=None):
                    if pair is not None:
                        mod_sums(pair, i)
                    pe.wait_ge(prod_done, FT * f + t + 1 + RING * i)
                    in_unit(u0 + t, 2 * b, n, i)
                    if pair is not None:
                        mod_columns(pair, i)

                step(0, 0, 0, None, s)
                done = 0
                for n, mod in ((MOD_LOOPS[s], True), (LOOPS - MOD_LOOPS[s], False)):
                    if n:
                        with pe.Fori(0, n) as i:
                            for b in range(RING):
                                t = 1 + RING * done + b
                                step(t, (1 + b) % RING, i, p0 + b if mod else None)
                        done += n
                for b in range(MOD_EXTRA[s]):
                    mod_sums(p0 + RING * MOD_LOOPS[s] + b)
                    mod_columns(p0 + RING * MOD_LOOPS[s] + b)

                def out_unit(u, t, i, first=False):
                    pe.wait_ge(lo_done, RING + u + 1 + RING * i)
                    for h in range(2):
                        fm = bass.ds(2 * t + h + 2 * RING * i, 1)
                        mhi, mlo = h_hi[:, fm, :], h_lo[:, fm, :]
                        for d in (6, 7, 2, 3, 4, 5, 0, 1) if first else range(KT):
                            if first and h == 0 and d in (2, 4, 0):
                                pe.wait_ge(prod_done, RING + FT * f + FT - {2: 2, 4: 1, 0: 0}[d])
                            ins = three(ps[:, d:d + 1, 0:TOK], tile_of(w_hi, u, h * KT + d), tile_of(w_lo, u, h * KT + d),
                                        mhi, mlo, first and h == 0, False)
                    ins.then_inc(unit_done, 1)

                pe.wait_ge(h_ready, RING + FT * f + 2)
                if MOD_LOOPS[s]:
                    pe.wait_ge(cols_copied, 1 + p0 + RING * MOD_LOOPS[s] + MOD_EXTRA[s])
                out_unit(u0 + FT, 0, 0, True)
                pe.wait_ge(h_ready, RING + FT * (f + 1))
                with pe.Fori(0, (FFN_OUT_UNITS - 2) // RING) as i:
                    for b in range(RING):
                        out_unit(u0 + FT + 1 + b, 1 + b, i)
                u = u0 + FFN_UNITS - 1
                pe.wait_ge(lo_done, RING + u + 1)
                for d in range(KT):
                    for h in range(2):
                        ft = FT - 2 + h
                        ins = three(ps[:, d, 0:TOK], tile_of(w_hi, u, h * KT + d), tile_of(w_lo, u, h * KT + d),
                                    h_hi[:, ft, :], h_lo[:, ft, :], False, h == 1)
                    ins.then_inc(y_done if d < KT - 1 else unit_done, 1)

            def proj_out(u, kt0, d0, last, ready):
                pe.wait_ge(lo_done, RING + u + 1)
                for d in range(4):
                    for k in range(4):
                        if d == 0:
                            pe.wait_ge(mix_ready, ready + k + 1)
                        n = k * 4 + d
                        ins = three(ps[:, d0 + d, 0:TOK], tile_of(w_hi, u, n), tile_of(w_lo, u, n),
                                    a_hi[:, kt0 + k, :], a_lo[:, kt0 + k, :], not last and k == 0, last and k == 3)
                    if last and d < 3:
                        ins.then_inc(y_done, 1)
                ins.then_inc(unit_done, 1)

            pe.sem_inc(unit_done, RING)
            pe.sem_inc(mod_used, RING)

            pe.wait_ge(const_in, 16)
            pe.wait_ge(rows_in, 16 * 15)
            for v in range(2):
                n = (A_ROWS, B_ROWS)[v]
                nc.tensor.transpose(ps[:, v, 0:n], rows[0:n, v, :], ident[0:n, 0:n]).then_inc(rows_t, 1)
            for j in range(CT):
                ins = nc.tensor.transpose(ps[:, 2, j * CONV_K:(j + 1) * CONV_K], conv_rows[:, j * P:(j + 1) * P],
                                          ident[0:CONV_K, 0:CONV_K])
            ins.then_inc(rows_t, 1)
            pe.wait_ge(x_in, 32)
            pe.wait_ge(rows_c, 3)
            for d in range(KT):
                if d >= 6:
                    pe.wait_ge(x_ready, d - 5)
                for tt in range(TT):
                    ins = nc.tensor.transpose(ps[:, d % 6, tt * P:(tt + 1) * P], x_nat[:, tt, d * P:(d + 1) * P], ident[:])
                ins.then_inc(x_t, 1)
            pe.wait_ge(cond_ready, 2)
            pe.wait_ge(setup, 3)
            pe.wait_ge(pick_ready, 1)
            pe.wait_ge(x_ready, KT)
            for pair in range(PAIRS_FIRST):
                mod_sums(pair)
                mod_columns(pair)
            norm(0)
            ffn(0)

            norm(1)
            u = UNIT0[1]
            for j in range(CT):
                in_unit(u + j, 2 * j, 1 if j == 0 else None)
            for j in range(3):
                pe.wait_ge(glu_done, j + 1)
                in_unit(u + CT + j, 2 * j)
            pe.wait_ge(glu_done, CT)
            pe.wait_ge(e_zero, 4)
            first = True
            for j in range(QT + 1):
                pe.wait_ge(qk_sq_done, j + 1)
                for tt in range(TT):
                    n = 2 * (TT * j + tt)
                    ins = mm(ps[:, 6, 256 + n:258 + n], qk_sq[:, j, tt * P:(tt + 1) * P], pick_half[:], start=True, stop=True)
            ins.then_inc(qk_stat, 1)
            pe.wait_ge(e_in, 48)
            pe.wait_ge(qk_copied, QT + 2)
            nc.tensor.transpose(ps[:, 5, 0:P], ck_nat[:], ident[:])
            for tt in range(TT):
                ins = nc.tensor.transpose(ps[:, 7, tt * P:(tt + 1) * P], v_raw[:, tt * P:(tt + 1) * P], ident[:])
            ins.then_inc(e_t, 1)
            pe.wait_ge(qk_wide_done, 1)
            for j in range(QT + 1):
                for tt in range(TT):
                    n = 2 * (TT * j + tt)
                    ins = mm(ps[:, j, tt * P:(tt + 1) * P], qk_wide[:, n:n + 2, :].rearrange("p a b -> p (a b)"), ident[:],
                             start=True, stop=True)
                ins.then_inc(qk_bc, 1)
            pe.wait_ge(qk_normed, QT + 1)
            for j in range(QT + 1):
                ins = mm(ps[:, j // 2, (j % 2) * LAT:(j % 2 + 1) * LAT], rope[:, R_SWAP:R_SWAP + P], qk[:, j, CTX:],
                         start=True, stop=True)
            ins.then_inc(swap_done, 1)
            nc.tensor.transpose(ps[:, 6, 0:P], qk[:, QT, 0:CTX], ident[:]).then_inc(e_t, 1)
            pe.wait_ge(roped, 5)
            pe.wait_ge(kdup_done, 4)
            pe.wait_ge(e_tc, 2)
            N = HEADS * TT

            def scores(n):
                head, tt = n // TT, n % TT
                j, o, g = head // 2, (head % 2) * HD, head // (HEADS // KV_HEADS)
                keys = slice(0, CTX) if tt == 0 else slice(CTX, TOK + PAST)
                if n >= 2:
                    pe.wait_ge(exp_done, n - 1)
                mm(ps[:, 4 + n % 2, 0:keys.stop - keys.start], qk[o:o + HD, j, tt * P:(tt + 1) * P],
                   kdup[o:o + HD, g, keys], start=True, stop=True).then_inc(score_done, 1)

            def flip(n):
                pe.wait_ge(prob_done, n + 1)
                if n >= 2:
                    pe.wait_ge(pt_copied, n - 1)
                for k in range(1 if n % TT == 0 else 3):
                    ins = nc.tensor.transpose(ps[:, 6 + n % 2, k * P:(k + 1) * P], prob[:, n % 2, k * P:(k + 1) * P], ident[:])
                ins.then_inc(pt_done, 1)

            def values(n):
                head, tt = n // TT, n % TT
                j, o, g = head // 2, (head % 2) * HD, head // (HEADS // KV_HEADS)
                tiles = [0] if tt == 0 else [1, 2, 3]
                pe.wait_ge(pt_copied, n + 1)
                for k, v in enumerate(tiles):
                    ins = mm(ps[o:o + HD, j, tt * P:(tt + 1) * P], v_nat[:, v, g * HD:(g + 1) * HD],
                             prob_t[:, n % 2, k * P:(k + 1) * P], start=k == 0, stop=k == len(tiles) - 1)
                ins.then_inc(pv_done, 1)

            scores(0)
            for n in range(N):
                if n + 1 < N:
                    scores(n + 1)
                flip(n)
                if n:
                    values(n - 1)
            values(N - 1)

            def means(m, src, at, ready):
                for sgm, lo, hi in SEGS:
                    for j in range(CT):
                        ins = mm(ps[:, 4, lo:hi], ones_mean[:], src[:, j, at[sgm]:at[sgm] + hi - lo],
                                 start=j == 0, stop=j == CT - 1)
                ins.then_inc(ln_mean_done, 1)

            def variances(m, sq):
                for j in range(CT):
                    pe.wait_ge(ln_sq, CT * m + j + 1)
                    ins = token_sums(ps[:, 5, :], sq[:, j, :], j, j == CT - 1)
                ins.then_inc(ln_stat, 1)

            pe.wait_ge(conv_done, CT)
            means(0, conv, CONV_AT, 0)
            proj_out(u + 7, 0, 0, False, 0)
            variances(0, qk_sq)
            pe.wait_ge(ln_diag, 1)
            spread(5).then_inc(ln_bc, 1)
            pe.wait_ge(ln_y, CT)
            proj_out(u + 8, 0, 4, False, 0)
            proj_out(u + 9, 4, 0, True, QT)
            proj_out(u + 10, 4, 4, True, QT)
            norm(2)
            ffn(2)
            norm(3)
            ffn(3)

            norm(4)
            u = UNIT0[4]
            in_unit(u, O_BANK[0], 4)
            in_unit(u + 1, O_BANK[1])
            in_unit(u + 2, O_BANK[2])
            pe.wait_ge(o_copied, 4)
            means(1, o_v, [0, CTX], 0)
            in_unit(u + 3, O_BANK[3])
            variances(1, o_sq)
            in_unit(u + 4, O_BANK[4])
            pe.wait_ge(ln_diag, 2)
            spread(5).then_inc(ln_bc, 1)
            pe.wait_ge(o_copied, 6)
            in_unit(u + 5, O_BANK[5])
            pe.wait_ge(o_in, 16 * (2 + CT))
            pe.wait_ge(o_copied, 8)
            for g in range(CT):
                ins = nc.tensor.transpose(ps[:, 0, g * P:(g + 1) * P], ws_nat[:, g, :], ident[:])
            ins.then_inc(o_t, 1)
            pe.wait_ge(o_copied, 10)
            pe.wait_ge(ln_out, 2 * CT)
            for tt in range(TT):
                for j in range(CT):
                    ins = nc.tensor.transpose(ps[:, 1 + tt, j * P:(j + 1) * P], o_v[:, j, tt * P:(tt + 1) * P], ident[:])
                ins.then_inc(o_t, 1)
            pe.wait_ge(o_copied, 12)
            pe.wait_ge(ln_y, 2 * CT)
            for tt in range(TT):
                for h in range(2):
                    n = 2 * tt + h
                    if n >= 4:
                        pe.wait_ge(o_z_copied, n - 3)
                    for gg in range(2):
                        ins = mm(ps[:, O_ZBANK[n], gg * 2 * P:(gg + 1) * 2 * P], o_f[:, 2 * h + gg, tt * P:(tt + 1) * P],
                                 fourier[:, F_CH:F_CH + 2 * P], start=True, stop=True)
                    ins.then_inc(o_z_done, 1)
            pe.wait_ge(o_tc, 1 + TT)
            for g in range(CT):
                for tt in range(TT):
                    ins = mm(ps[:, g, tt * P:(tt + 1) * P], o_vn[:, tt, g * P:(g + 1) * P], ws_t[:, g, :], start=True, stop=True)
                ins.then_inc(o_sgu, 1)
            pe.wait_ge(o_z_copied, 6)
            for g in range(CT):
                for cs in range(2):
                    z = slice(g * 2 * P + cs * P, g * 2 * P + (cs + 1) * P)
                    mm(ps[:, 4 + g, 0:CTX], o_z[:, 0, z], fourier[:, F_CTX + cs * P:F_CTX + (cs + 1) * P],
                       start=cs == 0, stop=cs == 1)
                for cs in range(2):
                    z = slice(g * 2 * P + cs * P, g * 2 * P + (cs + 1) * P)
                    for lt in range(2):
                        at = F_LAT + (2 * lt + cs) * LAT
                        ins = mm(ps[:, 4 + g, CTX:TOK], o_z[:, 1 + lt, z], fourier[:, at:at + LAT],
                                 start=cs == 0 and lt == 0, stop=cs == 1 and lt == 1)
                ins.then_inc(o_four, 1)
            pe.wait_ge(o_bias, CT)
            proj_out(u + 6, 0, 0, False, 2 * QT)
            proj_out(u + 7, 0, 4, False, 2 * QT)
            proj_out(u + 8, 4, 0, True, 3 * QT)
            proj_out(u + 9, 4, 4, True, 3 * QT)
            norm(5)
            ffn(5)
            pe.wait_ge(x_ready, KT * (N_SUB + 1))
            for tt in range(TT):
                for d in range(KT):
                    ins = nc.tensor.transpose(ps[:, 2 * tt + d // 4, (d % 4) * P:(d % 4 + 1) * P],
                                              x[:, d, tt * P:(tt + 1) * P], ident[:])
                ins.then_inc(out_t, 1)


FFN_AT = {0: 0, 2: 1, 3: 2, 5: 3}
M_Y = {0: 0, 2: 6, 3: 6, 5: 12}
O_BANK = [0, 2, 6, 0, 2, 6]
O_ZBANK = [4, 5, 6, 7, 4, 5]

_INS = ["x_prompt", "x_sample", "cache_k", "cache_v", "c", "c_ctx", "w_mod", "b_mod", "norm_g", "ffn_w_in",
        "ffn_w_out", "ev_w_in", "ev_w_out", "q_norm_g", "k_norm_g", "conv_w", "conv_b", "conv_norm_g",
        "conv_norm_b", "od_w_in", "od_w_out", "sgu_norm_g", "sgu_norm_b", "sgu_w", "sgu_b"]
_OUTS = [(1, CTX, D_MODEL), (1, LAT, D_MODEL), (1, 1, CTX, KV_HEADS, HD), (1, 1, CTX, KV_HEADS, HD)]


def kernel(**inputs):
    import concourse.bacc as bacc
    from concourse.bass_utils import run_bass_kernel_spmd

    nc = bacc.Bacc("TRN2", target_bir_lowering=False, num_devices=1)
    named = {n: np.ascontiguousarray(inputs[n]) for n in _INS}
    named.update(zip(("k_ident", "k_rope", "k_fourier"), shape_constants()))
    arrays, args = {}, []
    for name, a in named.items():
        arrays[f"in_{name}"] = a
        args.append(nc.dram_tensor(f"in_{name}", a.shape, mybir.dt.from_np(a.dtype), kind="ExternalInput").ap())
    for i, shape in enumerate(_OUTS):
        args.append(nc.dram_tensor(f"out_{i}", shape, FP32, kind="ExternalOutput").ap())
    build(nc, *args)
    result = run_bass_kernel_spmd(nc, [arrays], core_ids=[0])
    return tuple(result.results[0][f"out_{i}"] for i in range(len(_OUTS)))
```

```python
from contextlib import ExitStack

import numpy as np

import concourse.bass as bass
import concourse.mybir as mybir

FP32 = mybir.dt.float32
F32R = mybir.dt.float32r
ALU = mybir.AluOpType
ACT = mybir.ActivationFunctionType
AX = mybir.AxisListType

P = 128
D_MODEL, CTX, LAT, PAST = 1024, 128, 256, 128
TOK = CTX + LAT
TT = TOK // P
SEGS = [(0, 0, CTX), (1, CTX, TOK)]
KT = D_MODEL // P
FFN = 2816
FT = FFN // P
HEADS, KV_HEADS, HD = 8, 2, 64
QT = HEADS * HD // P
GRID_W, THETA = 64, 10000.0
CONV_CH, CONV_K = 512, 31
CT = CONV_CH // P
PADW = CONV_K // 2
PAD_AT = [PADW, 2 * PADW + CTX]
PAD_N = 3 * PADW + TOK
CONV_N = PAD_N - (CONV_K - 1)
CONV_AT = [0, CTX + PADW]
N_MOD = 9
N_SUB = 6
MODT = N_MOD * KT
RMS_EPS, LN_EPS = 1e-6, 1e-5
EARLY_TAPS = 7
POOL_TILES, TAP_BUFS = [0, 3], 2
DVE_TILES = [1, 2]

RING = 3
MRING = 3
UNIT = 2048
HALF = UNIT // 2
FFN_OUT_UNITS = FT // 2
FFN_UNITS = FT + FFN_OUT_UNITS
M0_UNITS, M1_UNITS = 11, 10
_sizes = [FFN_UNITS, M0_UNITS, FFN_UNITS, FFN_UNITS, M1_UNITS, FFN_UNITS]
UNIT0 = [sum(_sizes[:i]) for i in range(6)]
UNITS = sum(_sizes)

PAIR = 2 * P
PAIR_TILES = 2
GROUPS_FIRST = 3
LOOPS = (FT - 1) // RING
MOD_LOOPS = {0: LOOPS, 2: LOOPS, 3: LOOPS - 1, 5: 0}
MOD_EXTRA = {0: 1, 2: 0, 3: 0, 5: 0}
GROUP0, _p = {}, GROUPS_FIRST
for _s in (0, 2, 3, 5):
    GROUP0[_s] = _p
    _p += MOD_LOOPS[_s] + MOD_EXTRA[_s]
assert _p * MRING == 2 * MODT // PAIR_TILES
LAYER_PAIRS = MODT // PAIR_TILES
LAYER_GROUPS = LAYER_PAIRS // MRING
COND_ROWS = 32
COND_AT = 2 * (MRING - 1)

A_BMOD, A_NORM_G, A_ROWS = 0, MODT, MODT + N_SUB * KT
B_BMOD, B_CONV_B = 0, MODT
B_CN_G, B_CN_B, B_SN_G, B_SN_B = (B_CONV_B + CT * i for i in range(1, 5))
B_QG = B_CONV_B + 5 * CT
B_KG, B_ROWS = B_QG + 1, B_QG + 2

R_SWAP, R_COS, R_SIN, R_N = 0, P, P + LAT, P + 2 * LAT
F_CH, F_LAT, F_CTX, F_N = 0, 2 * P, 2 * P + 4 * LAT, 2 * P + 4 * LAT + 2 * P


def shape_constants():
    ident = np.eye(P, dtype=np.float32)
    swap = ident.reshape(P // 2, 2, P)[:, ::-1].reshape(P, P)
    t = np.arange(LAT)
    row, col = (t // GRID_W).astype(np.float32), (t % GRID_W).astype(np.float32)
    half = HD // 2
    freq = (1.0 / np.float32(THETA) ** (np.arange(0, half, 2, dtype=np.float32) / np.float32(half))).astype(np.float32)
    ang = np.concatenate([row[:, None] * freq, col[:, None] * freq], axis=-1)
    cos = np.repeat(np.cos(ang), 2, axis=1).T
    sin = np.repeat(np.sin(ang), 2, axis=1).T * np.tile([-1.0, 1.0], half)[:, None]
    rope = np.concatenate([swap, np.tile(cos, (2, 1)), np.tile(sin, (2, 1))], axis=1)

    def dft(n):
        a = 2 * np.pi * (np.outer(np.arange(n), np.arange(n)) % n) / n
        return np.cos(a), np.sin(a)

    cc, cs = dft(P)
    lc, ls = dft(LAT)
    lat = np.concatenate([lc[0:P], -ls[0:P], lc[P:], -ls[P:]], axis=1)
    fourier = np.concatenate([cc, cs, lat, cc, -cs], axis=1)
    return (ident, np.ascontiguousarray(rope, dtype=np.float32), np.ascontiguousarray(fourier, dtype=np.float32))


def build(nc, x_prompt, x_sample, cache_k, cache_v, c, c_ctx, w_mod, b_mod, norm_g, ffn_w_in, ffn_w_out,
          ev_w_in, ev_w_out, q_norm_g, k_norm_g, conv_w, conv_b, conv_norm_g, conv_norm_b, od_w_in, od_w_out,
          sgu_norm_g, sgu_norm_b, sgu_w, sgu_b, k_ident, k_rope, k_fourier,
          y_prompt, y_sample, new_cache_k, new_cache_v):
    ctx = ExitStack()
    with ctx:
        def sb(name, shape, dt=FP32, stack=ctx):
            return stack.enter_context(nc.sbuf_tensor(name, shape, dt))

        def sem(name):
            return ctx.enter_context(nc.semaphore(name))

        w_raw = sb("w_raw", [P, RING, UNIT])
        w_hi = sb("w_hi", [P, RING, UNIT], F32R)
        w_lo = sb("w_lo", [P, RING, UNIT], F32R)
        m_raw = sb("m_raw", [P, MRING, UNIT])
        x = sb("x", [P, KT, TOK])
        a_hi = sb("a_hi", [P, KT, TOK], F32R)
        a_lo = sb("a_lo", [P, KT, TOK], F32R)
        ident = sb("ident", [P, P])
        ones = sb("ones", [P, P])
        ones_mean = sb("ones_mean", [P, P])
        vec_a = sb("vec_a", [P, A_ROWS])
        vec_b = sb("vec_b", [P, B_ROWS])
        conv_wt = sb("conv_wt", [P, CT, CONV_K])
        cond = sb("cond", [P, KT, COND_AT + COND_ROWS])
        mod_pick = sb("mod_pick", [P, 2 * MRING])
        mod_part = sb("mod_part", [P, PAIR])
        mod_cols = sb("mod_cols", [P, 2 * MODT, 2])
        m_shift = sb("m_shift", [P, N_SUB, KT, 2])
        m_scale = sb("m_scale", [P, N_SUB, KT, 2])
        m_gate = sb("m_gate", [P, N_SUB, KT, 2])
        stat = sb("stat", [P, 32])
        stat_row = sb("stat_row", [P, 32])
        warm = sb("warm", [P, 16])
        glu = sb("glu", [P, 1, TOK])

        r = ExitStack()
        h_hi = sb("h_hi", [P, FT, TOK], F32R, r)
        h_lo = sb("h_lo", [P, FT, TOK], F32R, r)
        r.close()
        r = ExitStack()
        n_sq = sb("n_sq", [P, KT, TOK], stack=r)
        n_diag = sb("n_diag", [P, TT, P], stack=r)
        n_acc = sb("n_acc", [P, TOK], stack=r)
        n_full = sb("n_full", [P, KT, TOK], stack=r)
        cond_rows = sb("cond_rows", [2 * KT, P], stack=r)
        rows = sb("rows", [P, 2, P], stack=r)
        conv_rows = sb("conv_rows", [CONV_K, CONV_CH], stack=r)
        x_nat = sb("x_nat", [P, TT, D_MODEL], stack=r)
        r.close()
        r = ExitStack()
        e_diag = sb("e_diag", [P, TT, P], stack=r)
        taps_buf = sb("taps_buf", [P, TAP_BUFS, CONV_N], stack=r)
        padded = sb("padded", [P, CT, PAD_N], stack=r)
        conv = sb("conv", [P, CT, CONV_N], stack=r)
        e_sig = sb("e_sig", [P, 2, TOK], stack=r)
        qk = sb("qk", [P, QT + 1, TOK], stack=r)
        qk_sq = sb("qk_sq", [P, QT + 1, TOK], stack=r)
        qk_wide = sb("qk_wide", [P, 2 * TT * (QT + 1), HD], stack=r)
        v_raw = sb("v_raw", [P, TOK], stack=r)
        rope = sb("rope", [P, R_N], stack=r)
        pick_half = sb("pick_half", [P, 2], stack=r)
        rot = sb("rot", [P, QT + 1, LAT], stack=r)
        kdup = sb("kdup", [P, KV_HEADS, TOK + PAST], stack=r)
        ck_nat = sb("ck_nat", [P, P], stack=r)
        v_nat = sb("v_nat", [P, TT + 1, P], stack=r)
        k_nat = sb("k_nat", [P, P], stack=r)
        prob = sb("prob", [P, 2, TOK], stack=r)
        prob_t = sb("prob_t", [P, 2, TOK], stack=r)
        smax = sb("smax", [P, HEADS * TT], stack=r)
        smaxn = sb("smaxn", [P, HEADS * TT], stack=r)
        ssum = sb("ssum", [P, HEADS * TT], stack=r)
        srec = sb("srec", [P, HEADS * TT], stack=r)
        r.close()
        r = ExitStack()
        o_diag = sb("o_diag", [P, TT, P], stack=r)
        o_v = sb("o_v", [P, CT, TOK], stack=r)
        o_f = sb("o_f", [P, CT, TOK], stack=r)
        o_u = sb("o_u", [P, CT, TOK], stack=r)
        o_sq = sb("o_sq", [P, CT, TOK], stack=r)
        o_vn = sb("o_vn", [P, TT, CONV_CH], stack=r)
        o_z = sb("o_z", [P, TT, 2 * CONV_CH], stack=r)
        fourier = sb("fourier", [P, F_N], stack=r)
        ws_nat = sb("ws_nat", [P, CT, P], stack=r)
        ws_t = sb("ws_t", [P, CT, P], stack=r)
        bs = sb("bs", [P, CT, P], stack=r)
        r.close()

        ps = ctx.enter_context(nc.psum_tensor("ps", [P, 8, 512], FP32))

        raw_in = [sem(f"raw_in{i}") for i in range(RING)]
        hi_done = sem("hi_done")
        lo_done = sem("lo_done")
        unit_done = sem("unit_done")
        mod_in = [sem(f"mod_in{i}") for i in range(MRING)]
        mod_used = sem("mod_used")
        part_copied = sem("part_copied")
        cols_done = sem("cols_done")
        cols_copied = sem("cols_copied")
        const_in, cond_in, x_in = sem("const_in"), sem("cond_in"), sem("x_in")
        cond_t = sem("cond_t")
        vectors_in = sem("vectors_in")
        setup = sem("setup")
        pick_ready = sem("pick_ready")
        rows_t, rows_c = sem("rows_t"), sem("rows_c")
        cond_ready = sem("cond_ready")
        x_t = sem("x_t")
        x_ready = sem("x_ready")
        y_done = sem("y_done")
        sq_done, stat_done, ms_done, root_done, diag_done, bc_done = (
            sem(n) for n in ("sq_done", "stat_done", "ms_done", "root_done", "diag_done", "bc_done"))
        full_done, a_hi_done, a_ready = sem("full_done"), sem("a_hi_done"), sem("a_ready")
        dve_self = sem("dve_self")
        acc_done = sem("acc_done")
        silu_done, h_hi_done = sem("silu_done"), sem("h_hi_done")
        prod_done, h_ready = sem("prod_done"), sem("h_ready")
        out_in, out_t, out_c, out_done = sem("out_in"), sem("out_t"), sem("out_c"), sem("out_done")
        e_in, e_zero, sig_done, glu_done, conv_done = (
            sem(n) for n in ("e_in", "e_zero", "sig_done", "glu_done", "conv_done"))
        qk_copied, qk_sq_done, qk_stat, qk_ms, qk_root, qk_wide_done, qk_bc, qk_normed = (
            sem(n) for n in ("qk_copied", "qk_sq_done", "qk_stat", "qk_ms", "qk_root", "qk_wide_done",
                             "qk_bc", "qk_normed"))
        swap_done, roped, e_t, e_tc, kdup_done, cache_out = (
            sem(n) for n in ("swap_done", "roped", "e_t", "e_tc", "kdup_done", "cache_out"))
        score_done, max_done, exp_done, prob_done, pt_done, pt_copied, pv_done = (
            sem(n) for n in ("score_done", "max_done", "exp_done", "prob_done", "pt_done", "pt_copied", "pv_done"))
        mix_hi, mix_ready = sem("mix_hi"), sem("mix_ready")
        tap_ready, tap_added = sem("tap_ready"), sem("tap_added")
        ln_mean_done, ln_meanc, ln_xc, ln_sq, ln_stat, ln_ms, ln_root, ln_diag, ln_bc, ln_y = (
            sem(n) for n in ("ln_mean_done", "ln_meanc", "ln_xc", "ln_sq", "ln_stat", "ln_ms", "ln_root",
                             "ln_diag", "ln_bc", "ln_y"))
        ln_out = sem("ln_out")
        o_in, o_copied, o_t, o_tc, o_z_done, o_z_copied, o_sgu, o_bias, o_four = (
            sem(n) for n in ("o_in", "o_copied", "o_t", "o_tc", "o_z_done", "o_z_copied", "o_sgu", "o_bias",
                             "o_four"))

        block = ctx.enter_context(nc.Block())

        def slot(u):
            return u % RING

        def half(tile, u, h):
            return tile[:, slot(u), h * HALF:(h + 1) * HALF]

        def ffn_of(s):
            return (0, 0) if s == 0 else (0, 1) if s == 2 else (1, 0) if s == 3 else (1, 1)

        @block.sync
        def _(sp):
            def load_unit(u, i, halves):
                sp.wait_ge(lo_done, u + 1 + RING * i)
                for h, src in enumerate(halves):
                    dst = half(w_raw, u, h).rearrange("p (a b) -> p a b", a=src.shape[1])
                    sp.dma_start(dst, src).then_inc(raw_in[slot(u)], 16)

            def cols(w, start, n=P):
                return w.rearrange("(k p) n -> p k n", p=P)[:, :, bass.ds(start, n)]

            def load_pair(group, b, i, layer):
                sp.wait_ge(mod_used, MRING * group + b + 1 + MRING * i)
                start = (group - layer * LAYER_GROUPS) * MRING * PAIR + b * PAIR + i * MRING * PAIR
                sp.dma_start(m_raw[:, b, :].rearrange("p (a n) -> p a n", a=KT),
                             cols(w_mod[layer], start, PAIR)).then_inc(mod_in[b], 16)

            def load_ffn(s):
                layer, which = ffn_of(s)
                win, wout = ffn_w_in[layer, which], ffn_w_out[layer, which]
                u0, g0 = UNIT0[s], GROUP0[s]

                def in_unit(u, t, i):
                    load_unit(u, i, [cols(win, h * FFN + t * P + i * RING * P) for h in range(2)])

                def out_unit(u, t, i):
                    load_unit(u, i, [wout[bass.ds((2 * t + h) * P + i * 2 * RING * P, P), :]
                                     .rearrange("p (a n) -> p a n", a=1) for h in range(2)])

                if s == 0:
                    for pair in range(MRING, MRING * GROUPS_FIRST):
                        if pair == MRING * GROUPS_FIRST - 2:
                            in_unit(u0, 0, 0)
                        load_pair(pair // MRING, pair % MRING, 0, 0)
                else:
                    in_unit(u0, 0, 0)
                in_unit(u0 + 1, 1, 0)
                in_unit(u0 + 2, 2, 0)
                mods = MOD_LOOPS[s]
                rounds = min(mods, LOOPS - 1)
                first = max(0, min(rounds, LAYER_GROUPS - g0))
                parts = [(first, 0), (rounds - first, 1), (LOOPS - 1 - rounds, None)]
                done = 0
                for n, mod_layer in parts:
                    if n > 0:
                        with sp.Fori(0, n) as i:
                            for b in range(RING):
                                t = 1 + RING * done + b
                                in_unit(u0 + t + 2, t + 2, i)
                                if mod_layer is not None:
                                    load_pair(g0 + done, b, i, mod_layer)
                        done += n
                for b in range(RING):
                    t = 1 + RING * done + b
                    if t + 2 < FT:
                        in_unit(u0 + t + 2, t + 2, 0)
                    else:
                        out_unit(u0 + t + 2, t + 2 - FT, 0)
                    if mods == LOOPS:
                        load_pair(g0 + done, b, 0, (g0 + done) // LAYER_GROUPS)
                if MOD_EXTRA[s]:
                    for b in range(MRING):
                        load_pair(g0 + mods, b, 0, (g0 + mods) // LAYER_GROUPS)
                with sp.Fori(0, (FFN_OUT_UNITS - 2) // RING) as i:
                    for b in range(RING):
                        out_unit(u0 + FT + 2 + b, 2 + b, i)

            def load_proj_out(u, w, kt0, d0):
                load_unit(u, 0, [w[(kt0 + 2 * h) * P:(kt0 + 2 * h + 2) * P, d0 * P:(d0 + 4) * P]
                                 .rearrange("(k p) n -> p k n", p=P) for h in range(2)])

            sp.dma_start(ident[:], k_ident).then_inc(const_in, 16)
            sp.dma_start(cond_rows[0:KT, :], c_ctx.rearrange("(r n) -> r n", n=P)).then_inc(cond_in, 16)
            sp.dma_start(cond_rows[KT:2 * KT, :], c[0].rearrange("(r n) -> r n", n=P)).then_inc(cond_in, 16)
            for b in range(MRING):
                load_pair(0, b, 0, 0)
            sp.dma_start(x_nat[:, 0, :], x_prompt[0]).then_inc(x_in, 16)
            sp.dma_start(x_nat[:, 1:TT, :], x_sample[0].rearrange("(a p) n -> p a n", p=P)).then_inc(x_in, 16)
            load_ffn(0)
            u = UNIT0[1]
            a0 = (HEADS + 2 * KV_HEADS) * HD

            def glu_unit(n, j):
                load_unit(u + n, 0, [cols(ev_w_in[0], a0 + h * CONV_CH + j * P) for h in range(2)])

            glu_unit(0, 0)
            glu_unit(1, 1)
            for n, tile in ((2, 4), (3, 0), (4, 2)):
                load_unit(u + n, 0, [cols(ev_w_in[0], (tile + h) * P) for h in range(2)])
            sp.wait_ge(a_ready, 2 * KT)
            sp.wait_ge(unit_done, RING + UNIT0[1])
            for dst, src in ((rope[:], k_rope), (ck_nat[:], cache_k[0, 0].rearrange("t g d -> t (g d)")),
                             (v_nat[:, TT, :], cache_v[0, 0].rearrange("t g d -> t (g d)"))):
                sp.dma_start(dst, src).then_inc(e_in, 16)
            for j in range(2, CT):
                glu_unit(3 + j, j)
            for j, (kt0, d0) in enumerate(((0, 0), (0, 4), (4, 0), (4, 4))):
                load_proj_out(u + CT + 3 + j, ev_w_out[0], kt0, d0)
            load_ffn(2)
            load_ffn(3)
            u = UNIT0[4]
            for j, base in enumerate((8, 10, 0, 2, 4, 6)):
                load_unit(u + j, 0, [cols(od_w_in[0], (base + h) * P) for h in range(2)])
                if j == 3:
                    sp.wait_ge(a_ready, 5 * KT)
                    sp.wait_ge(unit_done, RING + u)
                    for dst, src in ((fourier[:], k_fourier), (ws_nat[:], sgu_w[0].rearrange("g p q -> p g q"))):
                        sp.dma_start(dst, src).then_inc(o_in, 16)
                    for g in range(CT):
                        sp.dma_start(bs[:, g, :], sgu_b[0, g:g + 1, :].to_broadcast([P, P])).then_inc(o_in, 16)
            for j, (kt0, d0) in enumerate(((0, 4), (0, 0), (4, 0), (4, 4))):
                load_proj_out(u + 6 + j, od_w_out[0], kt0, d0)
            load_ffn(5)
            for tt in range(TT):
                sp.wait_ge(out_c, tt + 1)
                dst = y_prompt[0] if tt == 0 else y_sample[0, (tt - 1) * P:tt * P, :]
                sp.dma_start(dst, x_nat[:, tt, :]).then_inc(out_done, 16)
            sp.wait_ge(out_done, 16 * TT)
            sp.wait_ge(cache_out, 32)

        @block.gpsimd
        def _(pool):
            nc.gpsimd.memset(cond[:], 0.0).then_inc(setup, 1)
            nc.gpsimd.memset(ones[:], 1.0).then_inc(setup, 1)
            nc.gpsimd.memset(ones_mean[:], 1.0 / CONV_CH).then_inc(setup, 1)

            def add_squares(n):
                for d in range(1, ADDED):
                    pool.wait_ge(sq_done, KT * n + d + 1)
                    if n or d > 1:
                        pool.wait_ge(acc_done, (ADDED - 1) * n + d - 1)
                    first = n_sq[:, 0, :] if d == 1 else n_acc[:]
                    nc.gpsimd.tensor_tensor(n_acc[:], first, n_sq[:, d, :], ALU.add).then_inc(acc_done, 1)

            add_squares(0)
            add_squares(1)
            pool.wait_ge(unit_done, RING + UNIT0[1])
            pool.wait_ge(a_ready, 2 * KT)
            nc.gpsimd.memset(padded[:], 0.0).then_inc(e_zero, 1)
            nc.gpsimd.memset(pick_half[:], 0.0).then_inc(e_zero, 1)
            pool.wait_ge(e_zero, 2)
            nc.gpsimd.memset(pick_half[0:HD, 0:1], 1.0).then_inc(e_zero, 1)
            nc.gpsimd.memset(pick_half[HD:P, 1:2], 1.0).then_inc(e_zero, 1)
            pool.wait_ge(e_zero, 4)
            for m, j in enumerate(POOL_TILES):
                acc = conv[:, j, :]
                for k in range(1, CONV_K):
                    n = m * (CONV_K - 1) + k - 1
                    pool.wait_ge(tap_ready, m * CONV_K + k + 1)
                    if n:
                        pool.wait_ge(tap_added, n)
                    nc.gpsimd.tensor_tensor(acc, acc, taps_buf[:, n % TAP_BUFS, :], ALU.add).then_inc(tap_added, 1)
            pool.wait_ge(tap_added, len(POOL_TILES) * (CONV_K - 1))
            for n in range(2, N_SUB):
                add_squares(n)

        @block.scalar
        def _(act):
            act.wait_ge(setup, 2)
            nc.scalar.activation(warm[:, 15:16], ones[:, 0:1], ACT.Silu)
            act.wait_ge(cond_t, 1)
            for i in range(2):
                nc.scalar.activation(cond[:, :, COND_AT + i:COND_AT + i + 1], ps[:, 0, i * KT:(i + 1) * KT].unsqueeze(2),
                                     ACT.Silu).then_inc(cond_ready, 1)
            for dst, src in (
                    (rows[0:MODT, 0, :], b_mod[0].rearrange("(r n) -> r n", n=P)),
                    (rows[A_NORM_G:A_ROWS, 0, :], norm_g.rearrange("l s (r n) -> (l s r) n", n=P)),
                    (rows[0:MODT, 1, :], b_mod[1].rearrange("(r n) -> r n", n=P)),
                    (rows[B_CONV_B:B_CONV_B + CT, 1, :], conv_b[0].rearrange("(r n) -> r n", n=P)),
                    (rows[B_CN_G:B_CN_G + CT, 1, :], conv_norm_g[0].rearrange("(r n) -> r n", n=P)),
                    (rows[B_CN_B:B_CN_B + CT, 1, :], conv_norm_b[0].rearrange("(r n) -> r n", n=P)),
                    (rows[B_SN_G:B_SN_G + CT, 1, :], sgu_norm_g[0].rearrange("(r n) -> r n", n=P)),
                    (rows[B_SN_B:B_SN_B + CT, 1, :], sgu_norm_b[0].rearrange("(r n) -> r n", n=P)),
                    (rows[B_QG:B_QG + 1, 1, 0:HD], q_norm_g), (rows[B_QG:B_QG + 1, 1, HD:P], q_norm_g),
                    (rows[B_KG:B_KG + 1, 1, 0:HD], k_norm_g), (rows[B_KG:B_KG + 1, 1, HD:P], k_norm_g),
                    (conv_rows[:, :], conv_w[0])):
                act.dma_start(dst, src).then_inc(vectors_in, 16)

            def split(u, i=0):
                act.wait_ge(raw_in[slot(u)], 32 * (u // RING + 1) + 32 * i)
                act.wait_ge(unit_done, u + 1 + RING * i)
                nc.scalar.activation(w_hi[:, slot(u), :], w_raw[:, slot(u), :], ACT.Copy).then_inc(hi_done, 1)

            def preload(n, func):
                nc.scalar.activation(warm[:, n:n + 1], ones[:, 0:1], func)

            def norm_stats(n):
                preload(n, ACT.Sqrt)
                for d in range(KT):
                    act.wait_ge(x_ready, KT * n + d + 1)
                    nc.scalar.activation(n_sq[:, d, :], x[:, d, :], ACT.Square).then_inc(sq_done, 1)
                act.wait_ge(ms_done, n + 1)
                nc.scalar.activation(stat[:, 4:4 + TT], stat[:, 0:TT], ACT.Sqrt).then_inc(root_done, 1)

            def norm(n):
                for d in range(KT):
                    act.wait_ge(full_done, KT * n + d + 1)
                    for cnd, lo, hi in SEGS:
                        ins = nc.scalar.activation(a_hi[:, d, lo:hi], n_full[:, d, lo:hi], ACT.Identity,
                                                   bias=m_shift[:, n, d, cnd:cnd + 1])
                    ins.then_inc(a_hi_done, 1)

            def ffn(s):
                u0, f = UNIT0[s], FFN_AT[s]

                def step(t, b, i):
                    split(u0 + t + 2, i)
                    act.wait_ge(unit_done, RING + u0 + t + 1 + RING * i)
                    act.wait_ge(h_ready, FT * f + t + 1 + RING * i)
                    nc.scalar.activation(glu[:, 0, :], ps[:, 2 * b, 0:TOK], ACT.Silu).then_inc(silu_done, 1)
                    act.wait_ge(prod_done, RING + FT * f + t + 1 + RING * i)
                    nc.scalar.activation(h_hi[:, bass.ds(t + RING * i, 1), :], glu[:],
                                         ACT.Copy).then_inc(h_hi_done, 1)

                step(0, 0, 0)
                with act.Fori(0, LOOPS) as i:
                    for b in range(RING):
                        step(1 + b, (1 + b) % RING, i)
                split(u0 + FT + 2)
                ahead = min(FFN_UNITS - FT - 2, UNITS - (u0 + FT + 3))
                with act.Fori(0, ahead // RING) as i:
                    for b in range(RING):
                        split(u0 + FT + 3 + b, i)
                for b in range(ahead // RING * RING, ahead):
                    split(u0 + FT + 3 + b)
                if s < 5:
                    split(u0 + FFN_UNITS + 1)

            norm_stats(0)
            for v in range(2):
                act.wait_ge(rows_t, v + 1)
                nc.scalar.activation((vec_a, vec_b)[v][:], ps[:, 1 + v, 0:(A_ROWS, B_ROWS)[v]], ACT.Copy).then_inc(rows_c, 1)
            act.wait_ge(rows_t, 3)
            nc.scalar.activation(conv_wt[:], ps[:, 3, 0:CT * CONV_K].rearrange("p (a b) -> p a b", a=CT),
                                 ACT.Copy).then_inc(rows_c, 1)
            split(0)
            norm(0)
            split(1)
            ffn(0)

            norm_stats(1)
            norm(1)
            u = UNIT0[1]

            def sigmoid(n, j):
                act.wait_ge(unit_done, RING + u + n + 1)
                if j >= 2:
                    act.wait_ge(glu_done, j - 1)
                nc.scalar.activation(e_sig[:, j % 2, :], ps[:, GLU_BANK[j] + 1, 0:TOK], ACT.Sigmoid).then_inc(sig_done, 1)

            def tap_products(m, k0, k1):
                j = POOL_TILES[m]
                for k in range(k0, k1):
                    w = conv_wt[:, j, k:k + 1]
                    src = padded[:, j, k:k + CONV_N]
                    if k == 0:
                        act.wait_ge(glu_done, j + 1)
                        nc.scalar.activation(conv[:, j, :], src, ACT.Identity, scale=w,
                                             bias=vec_b[:, B_CONV_B + j:B_CONV_B + j + 1]).then_inc(tap_ready, 1)
                        continue
                    n = m * (CONV_K - 1) + k - 1
                    if n >= TAP_BUFS:
                        act.wait_ge(tap_added, n + 1 - TAP_BUFS)
                    nc.scalar.activation(taps_buf[:, n % TAP_BUFS, :], src, ACT.Copy, scale=w).then_inc(tap_ready, 1)

            split(u + 2)
            sigmoid(0, 0)
            split(u + 3)
            tap_products(0, 0, 4)
            sigmoid(1, 1)
            for n in range(2, 5):
                split(u + n + 2)
                tap_products(0, 6 * n - 8, 6 * n - 2)
                act.wait_ge(unit_done, RING + u + n + 1)
                for h in range(2):
                    m = 2 * (n - 2) + h
                    tile = (QT, None, 0, 1, 2, 3)[m]
                    dst = v_raw[:] if tile is None else qk[:, tile, :]
                    nc.scalar.activation(dst, ps[:, QKV_BANK[n] + h, 0:TOK], ACT.Copy).then_inc(qk_copied, 1)
                    if tile is not None:
                        act.wait_ge(qk_copied, m + 1)
                        nc.scalar.activation(qk_sq[:, tile, :], dst, ACT.Square).then_inc(qk_sq_done, 1)
            act.wait_ge(e_t, 1)
            nc.scalar.activation(v_nat[:, 0:TT, :], ps[:, 3, 0:TOK].rearrange("p (a b) -> p a b", a=TT),
                                 ACT.Copy).then_inc(e_tc, 1)
            for g in range(KV_HEADS):
                for o in range(2):
                    nc.scalar.activation(kdup[o * HD:(o + 1) * HD, g, TOK:], ps[g * HD:(g + 1) * HD, 2, 0:PAST],
                                         ACT.Copy).then_inc(kdup_done, 1)
            act.wait_ge(qk_ms, 1)
            nc.scalar.activation(stat_row[:, 0:30], stat[:, 0:30], ACT.Sqrt).then_inc(qk_root, 1)
            split(u + 7)
            tap_products(0, 22, 26)
            sigmoid(5, 2)
            split(u + 8)
            tap_products(0, 26, CONV_K)
            act.wait_ge(e_t, 2)
            nc.scalar.activation(k_nat[:], ps[:, 3, 0:P], ACT.Copy).then_inc(e_tc, 1)
            sigmoid(6, 3)
            preload(6, ACT.Exp)
            act.wait_ge(e_tc, 2)
            act.dma_start(new_cache_k[0, 0].rearrange("t g d -> t (g d)"), k_nat[:]).then_inc(cache_out, 16)
            act.dma_start(new_cache_v[0, 0].rearrange("t g d -> t (g d)"), v_nat[:, 0, :]).then_inc(cache_out, 16)
            N = HEADS * TT
            for n in range(N + 1):
                if n < N:
                    width = CTX if n % TT == 0 else LAT + PAST
                    act.wait_ge(max_done, n + 1)
                    if n >= 2:
                        act.wait_ge(pt_done, n - 1)
                    nc.scalar.activation(prob[:, n % 2, 0:width], ps[:, 4 + n % 2, 0:width], ACT.Exp,
                                         bias=smaxn[:, n:n + 1], scale=HD ** -0.5,
                                         accum_out=ssum[:, n:n + 1]).then_inc(exp_done, 1)
                if n >= 1:
                    m = n - 1
                    width = CTX if m % TT == 0 else LAT + PAST
                    act.wait_ge(pt_done, m + 1)
                    if m >= 2:
                        act.wait_ge(pv_done, m - 1)
                    nc.scalar.activation(prob_t[:, m % 2, 0:width], ps[:, 6 + m % 2, 0:width], ACT.Copy).then_inc(pt_copied, 1)
                if n < N:
                    double = CONV_K - N
                    tap_products(1, n + min(n, double), n + 1 + min(n + 1, double))
            preload(7, ACT.Sqrt)
            act.wait_ge(pv_done, N)
            for j in range(QT):
                nc.scalar.activation(a_hi[:, j, :], ps[:, j, 0:TOK], ACT.Copy).then_inc(mix_hi, 1)
            split(u + 9)

            def layer_norm_root(m, src):
                for j in range(CT):
                    act.wait_ge(ln_xc, CT * m + j + 1)
                    nc.scalar.activation(qk_sq[:, j, :] if m == 0 else o_sq[:, j, :], src[:, j, :],
                                         ACT.Square).then_inc(ln_sq, 1)
                act.wait_ge(ln_ms, m + 1)
                nc.scalar.activation(stat_row[:, 0:TT], stat[:, 0:TT], ACT.Sqrt).then_inc(ln_root, 1)

            layer_norm_root(0, qk)
            preload(8, ACT.Silu)
            split(u + 10)
            for j in range(CT):
                act.wait_ge(ln_y, j + 1)
                nc.scalar.activation(qk[:, j, :], qk_sq[:, j, :], ACT.Silu, bias=vec_b[:, B_CN_B + j:B_CN_B + j + 1],
                                     scale=vec_b[:, B_CN_G + j:B_CN_G + j + 1]).then_inc(ln_out, 1)
                act.wait_ge(ln_out, j + 1)
                nc.scalar.activation(a_hi[:, QT + j, :], qk[:, j, :], ACT.Copy).then_inc(mix_hi, 1)
            split(u + 11)
            split(u + 12)
            act.wait_ge(cache_out, 32)
            norm_stats(2)
            norm(2)
            ffn(2)
            norm_stats(3)
            norm(3)
            ffn(3)

            norm_stats(4)
            norm(4)
            u = UNIT0[4]
            for j in range(6):
                split(u + j + 2)
                act.wait_ge(unit_done, RING + u + j + 1)
                for h in range(2):
                    n = 2 * j + h
                    dst = (o_v, o_f, o_u)[n // CT][:, n % CT, :]
                    nc.scalar.activation(dst, ps[:, O_BANK[j] + h, 0:TOK], ACT.Copy).then_inc(o_copied, 1)
                if j == 2:
                    for k in range(CT):
                        act.wait_ge(ln_xc, CT + k + 1)
                        nc.scalar.activation(o_sq[:, k, :], o_v[:, k, :], ACT.Square).then_inc(ln_sq, 1)
                if j == 4:
                    act.wait_ge(ln_ms, 2)
                    nc.scalar.activation(stat_row[:, 0:TT], stat[:, 0:TT], ACT.Sqrt).then_inc(ln_root, 1)
            for j in range(CT):
                act.wait_ge(ln_y, CT + j + 1)
                nc.scalar.activation(o_v[:, j, :], o_sq[:, j, :], ACT.Identity, bias=vec_b[:, B_SN_B + j:B_SN_B + j + 1],
                                     scale=vec_b[:, B_SN_G + j:B_SN_G + j + 1]).then_inc(ln_out, 1)
            for n in range(2 * TT):
                act.wait_ge(o_z_done, n + 1)
                nc.scalar.activation(o_z[:, n // 2, (n % 2) * 512:(n % 2 + 1) * 512], ps[:, O_ZBANK[n], :],
                                     ACT.Copy).then_inc(o_z_copied, 1)
            act.wait_ge(o_t, 1)
            nc.scalar.activation(ws_t[:], ps[:, 6, :].rearrange("p (a b) -> p a b", a=CT), ACT.Copy).then_inc(o_tc, 1)
            for tt in range(TT):
                act.wait_ge(o_t, tt + 2)
                nc.scalar.activation(o_vn[:, tt, :], ps[:, O_VBANK[tt], :], ACT.Copy).then_inc(o_tc, 1)
            split(u + 8)
            for g in range(CT):
                act.wait_ge(o_four, g + 1)
                for _, lo, hi in SEGS:
                    nc.scalar.activation(a_hi[:, g, lo:hi], ps[:, 4 + g, lo:hi], ACT.Copy,
                                         scale=float((hi - lo) * P) ** -0.5).then_inc(mix_hi, 1)
            for g in range(CT):
                act.wait_ge(o_bias, g + 1)
                nc.scalar.activation(a_hi[:, CT + g, :], o_sq[:, g, :], ACT.Copy).then_inc(mix_hi, 1)
            split(u + 9)
            split(u + 10)
            split(u + 11)
            norm_stats(5)
            norm(5)
            ffn(5)
            for tt in range(TT):
                act.wait_ge(out_t, tt + 1)
                nc.scalar.activation(x_nat[:, tt, :].rearrange("p (a b) -> p a b", a=2), ps[:, 2 * tt:2 * tt + 2, :],
                                     ACT.Copy).then_inc(out_c, 1)

        @block.vector
        def _(dve):
            self_n = [0]

            def mark(ins):
                ins.then_inc(dve_self, 1)
                self_n[0] += 1
                return self_n[0]

            def split(u, i=0):
                dve.wait_ge(hi_done, u + 1 + RING * i)
                nc.vector.tensor_tensor(w_lo[:, slot(u), :], w_raw[:, slot(u), :], w_hi[:, slot(u), :].bitcast(FP32),
                                        ALU.subtract).then_inc(lo_done, 1)

            def part_copy(g, i=0):
                dve.wait_ge(mod_used, MRING * (g + 2) + MRING * i)
                if g:
                    dve.wait_ge(cols_done, g + i)
                nc.vector.tensor_copy(mod_part[:], ps[:, 6, 0:PAIR]).then_inc(part_copied, 1)

            def cols_copy(g, i=0):
                dve.wait_ge(cols_done, g + 1 + i)
                n = MRING * PAIR_TILES
                dst = mod_cols[:, bass.ds(n * g + n * i, n), :].rearrange("p (a q) c -> p q a c", a=MRING)
                nc.vector.tensor_copy(dst, ps[:, 7, 0:2 * n].rearrange("p (q a c) -> p q a c", q=PAIR_TILES, a=MRING)
                                      ).then_inc(cols_copied, 1)

            def groups(tiles):
                return -(-tiles // (MRING * PAIR_TILES))

            def bias(s, which):
                layer, m = s // 3, 3 * (s % 3) + which
                v, base = (vec_a, A_BMOD) if layer == 0 else (vec_b, B_BMOD)
                return v[:, base + m * KT:base + (m + 1) * KT].unsqueeze(2).to_broadcast([P, KT, 2])

            def raw_mod(s, which):
                t = (s // 3) * MODT + (3 * (s % 3) + which) * KT
                return mod_cols[:, t:t + KT, :]

            def modulation_in(s):
                dve.wait_ge(rows_c, 2)
                dve.wait_ge(cols_copied, 1 + groups((3 * s + 2) * KT))
                mark(nc.vector.tensor_tensor(m_shift[:, s], raw_mod(s, 0), bias(s, 0), ALU.add))
                dve.wait_ge(dve_self, mark(nc.vector.tensor_tensor(m_scale[:, s], raw_mod(s, 1), bias(s, 1), ALU.add)))
                g = vec_a[:, A_NORM_G + s * KT:A_NORM_G + (s + 1) * KT].unsqueeze(2).to_broadcast([P, KT, 2])
                dve.wait_ge(dve_self, mark(nc.vector.scalar_tensor_tensor(
                    m_scale[:, s], m_scale[:, s], 1.0, g, ALU.add, ALU.mult)))

            def modulation_gate(s):
                dve.wait_ge(cols_copied, 1 + groups(3 * (s + 1) * KT))
                n = mark(nc.vector.tensor_tensor(m_gate[:, s], raw_mod(s, 2), bias(s, 2), ALU.add))
                dve.wait_ge(dve_self, n)
                if s % 3 != 1:
                    dve.wait_ge(dve_self, mark(nc.vector.tensor_scalar(m_gate[:, s], m_gate[:, s], 0.5, None, ALU.mult)))

            def residual(s, d):
                for cnd, lo, hi in SEGS:
                    ins = nc.vector.scalar_tensor_tensor(x[:, d, lo:hi], ps[:, d, lo:hi], m_gate[:, s, d, cnd:cnd + 1],
                                                         x[:, d, lo:hi], ALU.mult, ALU.add)
                ins.then_inc(x_ready, 1)

            def norm_stats(n, unit=None):
                if unit is not None:
                    split(unit)
                dve.wait_ge(stat_done, n + 1)
                nc.vector.tensor_scalar(stat[:, 0:TT], ps[:, 0, 0:TT], 1.0 / D_MODEL, RMS_EPS,
                                        ALU.mult, ALU.add).then_inc(ms_done, 1)
                dve.wait_ge(root_done, n + 1)
                dve.wait_ge(dve_self, mark(nc.vector.reciprocal(stat[:, 8:8 + TT], stat[:, 4:4 + TT])))
                nc.vector.tensor_tensor(n_diag[:], ident[:].unsqueeze(1).to_broadcast([P, TT, P]),
                                        stat[:, 8:8 + TT].unsqueeze(2).to_broadcast([P, TT, P]), ALU.mult).then_inc(diag_done, 1)

            def norm(n):
                bank = BC_BANK[n]
                dve.wait_ge(bc_done, n + 1)
                for d in range(KT + 1):
                    if d < KT:
                        for cnd, lo, hi in SEGS:
                            ins = nc.vector.scalar_tensor_tensor(n_full[:, d, lo:hi], ps[:, bank, lo:hi],
                                                                 m_scale[:, n, d, cnd:cnd + 1], x[:, d, lo:hi],
                                                                 ALU.mult, ALU.mult)
                        ins.then_inc(full_done, 1)
                    if d >= 1:
                        e = d - 1
                        dve.wait_ge(a_hi_done, KT * n + e + 1)
                        for cnd, lo, hi in SEGS:
                            ins = nc.vector.scalar_tensor_tensor(a_lo[:, e, lo:hi], n_full[:, e, lo:hi],
                                                                 m_shift[:, n, e, cnd:cnd + 1],
                                                                 a_hi[:, e, lo:hi].bitcast(FP32), ALU.add, ALU.subtract)
                        ins.then_inc(a_ready, 1)

            def ffn(s):
                u0, f, g0 = UNIT0[s], FFN_AT[s], GROUP0[s]

                def step(t, b, i, group):
                    split(u0 + t + 2, i)
                    if group is not None:
                        part_copy(group, i)
                    dve.wait_ge(silu_done, FT * f + t + 1 + RING * i)
                    nc.vector.tensor_tensor(glu[:, 0, :], glu[:, 0, :], ps[:, 2 * b + 1, 0:TOK],
                                            ALU.mult).then_inc(prod_done, 1)
                    dve.wait_ge(h_hi_done, FT * f + t + 1 + RING * i)
                    nc.vector.tensor_tensor(h_lo[:, bass.ds(t + RING * i, 1), :], glu[:],
                                            h_hi[:, bass.ds(t + RING * i, 1), :].bitcast(FP32),
                                            ALU.subtract).then_inc(h_ready, 1)
                    if group is not None:
                        cols_copy(group, i)

                step(0, 0, 0, None)
                done = 0
                for n, mod in ((MOD_LOOPS[s], True), (LOOPS - MOD_LOOPS[s], False)):
                    if n:
                        with dve.Fori(0, n) as i:
                            for b in range(RING):
                                t = 1 + RING * done + b
                                step(t, (1 + b) % RING, i, g0 if mod and b == RING - 1 else None)
                        done += n
                for g in range(g0 + MOD_LOOPS[s], g0 + MOD_LOOPS[s] + MOD_EXTRA[s]):
                    part_copy(g)
                    cols_copy(g)
                split(u0 + FT + 2)
                ahead = min(FFN_UNITS - FT - 2, UNITS - (u0 + FT + 3))
                with dve.Fori(0, ahead // RING) as i:
                    for b in range(RING):
                        split(u0 + FT + 3 + b, i)
                for b in range(ahead // RING * RING, ahead):
                    split(u0 + FT + 3 + b)
                modulation_gate(s)
                for d in range(KT):
                    if d < KT - 1:
                        dve.wait_ge(y_done, (KT - 1) * f + M_Y[s] + d + 1)
                    else:
                        dve.wait_ge(unit_done, RING + u0 + FFN_UNITS)
                    residual(s, d)
                if s < 5:
                    modulation_in(s + 1)

            dve.sem_inc(lo_done, RING)
            dve.sem_inc(part_copied, 1)
            dve.sem_inc(cols_copied, 1)
            dve.sem_inc(prod_done, RING)
            dve.sem_inc(h_ready, 1)
            dve.wait_ge(const_in, 16)
            nc.vector.tensor_reduce(mod_pick[:], ident[:].rearrange("p (a b) -> p b a", a=4)[:, 0:2 * MRING, :], axis=AX.X,
                                    op=ALU.add).then_inc(pick_ready, 1)
            part_copy(0)
            for d in range(KT):
                dve.wait_ge(x_t, d + 1)
                nc.vector.tensor_copy(x[:, d, :], ps[:, d % 6, 0:TOK]).then_inc(x_ready, 1)
            cols_copy(0)
            norm_stats(0)
            part_copy(1)
            cols_copy(1)
            split(0)
            part_copy(2)
            cols_copy(2)
            modulation_in(0)
            norm(0)
            split(1)
            ffn(0)

            norm_stats(1, UNIT0[1] + 1)
            norm(1)
            u = UNIT0[1]
            tap_at = {}

            def taps(j, k0, k1):
                for k in range(k0, k1):
                    if k == 0:
                        ins = nc.vector.tensor_scalar(conv[:, j, :], padded[:, j, 0:CONV_N], conv_wt[:, j, 0:1],
                                                      vec_b[:, B_CONV_B + j:B_CONV_B + j + 1], ALU.mult, ALU.add)
                    else:
                        dve.wait_ge(dve_self, tap_at[j])
                        ins = nc.vector.scalar_tensor_tensor(conv[:, j, :], padded[:, j, k:k + CONV_N],
                                                             conv_wt[:, j, k:k + 1], conv[:, j, :], ALU.mult, ALU.add)
                    if k < CONV_K - 1:
                        tap_at[j] = mark(ins)
                    else:
                        ins.then_inc(conv_done, 1)

            def glu_mul(j):
                dve.wait_ge(sig_done, j + 1)
                dve.wait_ge(e_zero, 1)
                for sgm, lo, hi in SEGS:
                    ins = nc.vector.tensor_tensor(padded[:, j, PAD_AT[sgm]:PAD_AT[sgm] + hi - lo],
                                                  e_sig[:, j % 2, lo:hi], ps[:, GLU_BANK[j], lo:hi], ALU.mult)
                ins.then_inc(glu_done, 1)

            split(u + 2)
            glu_mul(0)
            dve.wait_ge(rows_c, 3)
            split(u + 3)
            glu_mul(1)
            dve.wait_ge(glu_done, 2)
            taps(1, 0, 8)
            split(u + 4)
            taps(1, 8, 18)
            split(u + 5)
            taps(1, 18, 28)
            split(u + 6)
            NS = 2 * TT * (QT + 1)
            dve.wait_ge(qk_stat, 1)
            nc.vector.tensor_scalar(stat[:, 0:NS], ps[:, 6, 0:NS], 1.0 / HD, RMS_EPS, ALU.mult, ALU.add).then_inc(qk_ms, 1)
            dve.wait_ge(qk_root, 1)
            dve.wait_ge(dve_self, mark(nc.vector.reciprocal(stat_row[:, 0:NS], stat_row[:, 0:NS])))
            nc.vector.tensor_copy(qk_wide[:], stat_row[:, 0:NS].unsqueeze(2).to_broadcast([P, NS, HD])).then_inc(qk_wide_done, 1)
            split(u + 7)
            taps(1, 28, CONV_K)
            glu_mul(2)
            for j in range(QT + 1):
                dve.wait_ge(qk_bc, j + 1)
                col = B_QG if j < QT else B_KG
                nc.vector.scalar_tensor_tensor(qk[:, j, :], qk[:, j, :], vec_b[:, col:col + 1], ps[:, BC_BANKS[j], 0:TOK],
                                               ALU.mult, ALU.mult).then_inc(qk_normed, 1)
            dve.wait_ge(e_in, 48)
            dve.wait_ge(qk_normed, QT + 1)
            a = mark(nc.vector.tensor_tensor(rot[:], qk[:, :, CTX:], rope[:, R_COS:R_COS + LAT].unsqueeze(1)
                                             .to_broadcast([P, QT + 1, LAT]), ALU.mult))
            dve.wait_ge(dve_self, a)
            dve.wait_ge(swap_done, 1)
            for lo, hi, bank in SWAP_BANKS:
                n = hi - lo
                a = mark(nc.vector.tensor_tensor(qk[:, lo:hi, CTX:], ps[:, bank, 0:n * LAT].rearrange("p (c b) -> p c b", c=n),
                                                 rope[:, R_SIN:R_SIN + LAT].unsqueeze(1).to_broadcast([P, n, LAT]), ALU.mult))
            dve.wait_ge(dve_self, a)
            nc.vector.tensor_tensor(qk[:, :, CTX:], qk[:, :, CTX:], rot[:], ALU.add).then_inc(roped, 1)
            dve.wait_ge(roped, 1)
            for g in range(KV_HEADS):
                for o in range(2):
                    nc.vector.tensor_copy(kdup[o * HD:(o + 1) * HD, g, 0:TOK], qk[g * HD:(g + 1) * HD, QT, :]).then_inc(roped, 1)

            def attention(n):
                width = CTX if n % TT == 0 else LAT + PAST
                dve.wait_ge(score_done, n + 1)
                a = mark(nc.vector.tensor_reduce(smax[:, n:n + 1], ps[:, 4 + n % 2, 0:width], axis=AX.X, op=ALU.max))
                dve.wait_ge(dve_self, a)
                nc.vector.tensor_scalar(smaxn[:, n:n + 1], smax[:, n:n + 1], -(HD ** -0.5), None, ALU.mult).then_inc(max_done, 1)

            def normalize(n):
                width = CTX if n % TT == 0 else LAT + PAST
                dve.wait_ge(exp_done, n + 1)
                dve.wait_ge(dve_self, mark(nc.vector.reciprocal(srec[:, n:n + 1], ssum[:, n:n + 1])))
                nc.vector.tensor_scalar(prob[:, n % 2, 0:width], prob[:, n % 2, 0:width], srec[:, n:n + 1], None,
                                        ALU.mult).then_inc(prob_done, 1)

            N = HEADS * TT
            split(u + 8)
            dve.wait_ge(glu_done, 3)
            taps(2, 0, EARLY_TAPS)
            glu_mul(3)
            attention(0)
            for n in range(N):
                if n + 1 < N:
                    attention(n + 1)
                normalize(n)
                taps(2, EARLY_TAPS + n, EARLY_TAPS + n + 1)

            def layer_norm(m, src, dst, sq, at):
                dve.wait_ge(ln_mean_done, m + 1)
                for j in range(CT):
                    for sgm, lo, hi in SEGS:
                        ins = nc.vector.tensor_tensor(dst[:, j, lo:hi], src[:, j, at[sgm]:at[sgm] + hi - lo],
                                                      ps[:, 4, lo:hi], ALU.subtract)
                    ins.then_inc(ln_xc, 1)

            def layer_norm_scale(m, bank, diag):
                dve.wait_ge(ln_stat, m + 1)
                nc.vector.tensor_scalar(stat[:, 0:TT], ps[:, bank, 0:TT], 1.0 / CONV_CH, LN_EPS, ALU.mult, ALU.add).then_inc(ln_ms, 1)
                dve.wait_ge(ln_root, m + 1)
                dve.wait_ge(dve_self, mark(nc.vector.reciprocal(stat[:, 8:8 + TT], stat_row[:, 0:TT])))
                for tt in range(TT):
                    ins = nc.vector.tensor_scalar(diag[:, tt, :], ident[:], stat[:, 8 + tt:9 + tt], None, ALU.mult)
                ins.then_inc(ln_diag, 1)

            def mix_low(j, src):
                dve.wait_ge(mix_hi, j + 1)
                nc.vector.tensor_tensor(a_lo[:, j, :], src, a_hi[:, j, :].bitcast(FP32), ALU.subtract).then_inc(mix_ready, 1)

            for j in range(QT):
                mix_low(j, ps[:, j, 0:TOK])
            layer_norm(0, conv, qk, qk_sq, CONV_AT)
            split(u + 9)
            layer_norm_scale(0, 7, e_diag)
            split(u + 10)
            modulation_gate(1)
            dve.wait_ge(ln_bc, 1)
            for j in range(CT):
                nc.vector.tensor_tensor(qk_sq[:, j, :].rearrange("p (a b) -> p a b", a=TT),
                                        qk[:, j, :].rearrange("p (a b) -> p a b", a=TT),
                                        ps[:, 4:4 + TT, TOK:], ALU.mult).then_inc(ln_y, 1)
            for j in range(CT):
                mix_low(QT + j, qk[:, j, :])
            split(u + 11)
            for d in range(KT):
                if d % 4 < 3:
                    dve.wait_ge(y_done, (KT - 1) + (d // 4) * 3 + d % 4 + 1)
                else:
                    dve.wait_ge(unit_done, RING + u + 10 + d // 4)
                residual(1, d)
            modulation_in(2)
            norm_stats(2, UNIT0[2] + 1)
            norm(2)
            ffn(2)
            norm_stats(3, UNIT0[3] + 1)
            norm(3)
            ffn(3)

            norm_stats(4, UNIT0[4] + 1)
            norm(4)
            u = UNIT0[4]
            split(u + 2)
            split(u + 3)
            split(u + 4)
            layer_norm(1, o_v, o_v, o_sq, [0, CTX])
            split(u + 5)
            split(u + 6)
            layer_norm_scale(1, 5, o_diag)
            split(u + 7)
            dve.wait_ge(ln_bc, 2)
            for j in range(CT):
                nc.vector.tensor_tensor(o_sq[:, j, :], o_v[:, j, :], ps[:, 4, 0:TOK], ALU.mult).then_inc(ln_y, 1)
            split(u + 8)
            for g in range(CT):
                dve.wait_ge(mix_hi, 2 * QT + 2 * g + 2)
                for _, lo, hi in SEGS:
                    ins = nc.vector.scalar_tensor_tensor(a_lo[:, g, lo:hi], ps[:, 4 + g, lo:hi], float((hi - lo) * P) ** -0.5,
                                                         a_hi[:, g, lo:hi].bitcast(FP32), ALU.mult, ALU.subtract)
                ins.then_inc(mix_ready, 1)
            dve.wait_ge(o_in, 16 * (2 + CT))
            dve.wait_ge(ln_out, 2 * CT)
            for g in range(CT):
                dve.wait_ge(o_sgu, g + 1)
                a = mark(nc.vector.tensor_tensor(o_sq[:, g, :].rearrange("p (a b) -> p a b", a=TT),
                                                 ps[:, g, 0:TOK].rearrange("p (a b) -> p a b", a=TT),
                                                 bs[:, g:g + 1, :].to_broadcast([P, TT, P]), ALU.add))
                dve.wait_ge(dve_self, a)
                dve.wait_ge(o_copied, 12)
                nc.vector.tensor_tensor(o_sq[:, g, :], o_sq[:, g, :], o_u[:, g, :], ALU.mult).then_inc(o_bias, 1)
            for g in range(CT):
                dve.wait_ge(mix_hi, 2 * QT + 2 * CT + g + 1)
                nc.vector.tensor_tensor(a_lo[:, CT + g, :], o_sq[:, g, :], a_hi[:, CT + g, :].bitcast(FP32),
                                        ALU.subtract).then_inc(mix_ready, 1)
            modulation_gate(4)
            split(u + 9)
            split(u + 10)
            for d in range(KT):
                if d % 4 < 3:
                    dve.wait_ge(y_done, 3 * (KT - 1) + 6 + (d // 4) * 3 + d % 4 + 1)
                else:
                    dve.wait_ge(unit_done, RING + u + 9 + d // 4)
                residual(4, d)
            modulation_in(5)
            norm_stats(5, UNIT0[5] + 1)
            norm(5)
            ffn(5)

        @block.tensor
        def _(pe):
            mm = nc.tensor.matmul

            def three(out, whi, wlo, mhi, mlo, start, stop):
                mm(out, whi, mhi, start=start, stop=False)
                mm(out, whi, mlo, start=False, stop=False)
                return mm(out, wlo, mhi, start=False, stop=stop)

            def tile_of(w, u, n):
                return w[:, slot(u), n * P:(n + 1) * P]

            def in_unit(u, banks, n=None, i=0):
                pe.wait_ge(lo_done, RING + u + 1 + RING * i)
                for k in range(KT):
                    if n is not None:
                        pe.wait_ge(a_ready, KT * n + k + 1)
                    for h in range(2):
                        ins = three(ps[:, banks + h, 0:TOK], tile_of(w_hi, u, h * KT + k), tile_of(w_lo, u, h * KT + k),
                                    a_hi[:, k, :], a_lo[:, k, :], k == 0, k == KT - 1)
                ins.then_inc(unit_done, 1)

            def mod_sums(g, b, i=0):
                pe.wait_ge(mod_in[b], 16 * (g + 1) + 16 * i)
                for k in range(KT):
                    j = k % 4
                    ins = mm(ps[32 * j:32 * j + 32, 6, 0:PAIR], cond[:, k, COND_AT - 2 * b:COND_AT - 2 * b + COND_ROWS],
                             m_raw[:, b, k * PAIR:(k + 1) * PAIR], start=b == 0 and k < 4, stop=b == MRING - 1 and k >= 4)
                ins.then_inc(mod_used, 1)

            def mod_columns(g, i=0):
                pe.wait_ge(part_copied, g + 2 + i)
                pe.wait_ge(cols_copied, g + 1 + i)
                n = 2 * MRING
                for q in range(PAIR_TILES):
                    ins = mm(ps[:, 7, q * n:(q + 1) * n], mod_part[:, q * P:(q + 1) * P], mod_pick[:], start=True, stop=True)
                ins.then_inc(cols_done, 1)

            def token_sums(out, src, k, last):
                for tt in range(TT):
                    ins = mm(out[:, tt:tt + 1], src[:, tt * P:(tt + 1) * P], ones[:, 0:1], start=(k == 0 and tt == 0),
                             stop=last, skip_group_check=True)
                return ins

            def spread(bank, diag):
                for tt in range(TT):
                    ins = mm(ps[:, bank, tt * P:(tt + 1) * P], ones[:], diag[:, tt, :], start=True, stop=True)
                return ins

            def norm_sums(n):
                for d in range(ADDED, KT):
                    pe.wait_ge(sq_done, KT * n + d + 1)
                    token_sums(ps[:, 0, :], n_sq[:, d, :], d - ADDED, False)
                pe.wait_ge(acc_done, (ADDED - 1) * (n + 1))
                token_sums(ps[:, 0, :], n_acc[:], 1, True).then_inc(stat_done, 1)

            def norm_spread(n):
                pe.wait_ge(diag_done, n + 1)
                spread(BC_BANK[n], n_diag).then_inc(bc_done, 1)

            def norm(n):
                norm_sums(n)
                norm_spread(n)

            def ffn(s):
                u0, f, g0 = UNIT0[s], FFN_AT[s], GROUP0[s]

                def step(t, b, i, pair, n=None):
                    if pair is not None:
                        mod_sums(*pair, i)
                    pe.wait_ge(prod_done, FT * f + t + 1 + RING * i)
                    in_unit(u0 + t, 2 * b, n, i)
                    if pair is not None and pair[1] == MRING - 1:
                        mod_columns(pair[0], i)

                step(0, 0, 0, None, s)
                done = 0
                for n, mod in ((MOD_LOOPS[s], True), (LOOPS - MOD_LOOPS[s], False)):
                    if n:
                        with pe.Fori(0, n) as i:
                            for b in range(RING):
                                t = 1 + RING * done + b
                                step(t, (1 + b) % RING, i, (g0, b) if mod else None)
                        done += n
                for g in range(g0 + MOD_LOOPS[s], g0 + MOD_LOOPS[s] + MOD_EXTRA[s]):
                    for b in range(MRING):
                        mod_sums(g, b)
                    mod_columns(g)

                def out_unit(u, t, i, first=False):
                    pe.wait_ge(lo_done, RING + u + 1 + RING * i)
                    for h in range(2):
                        fm = bass.ds(2 * t + h + 2 * RING * i, 1)
                        mhi, mlo = h_hi[:, fm, :], h_lo[:, fm, :]
                        for d in (6, 7, 2, 3, 4, 5, 0, 1) if first else range(KT):
                            if first and h == 0 and d in (2, 4, 0):
                                pe.wait_ge(prod_done, RING + FT * f + FT - {2: 2, 4: 1, 0: 0}[d])
                            ins = three(ps[:, d:d + 1, 0:TOK], tile_of(w_hi, u, h * KT + d), tile_of(w_lo, u, h * KT + d),
                                        mhi, mlo, first and h == 0, False)
                    ins.then_inc(unit_done, 1)

                pe.wait_ge(h_ready, 1 + FT * f + 2)
                if MOD_LOOPS[s]:
                    pe.wait_ge(cols_copied, 1 + g0 + MOD_LOOPS[s] + MOD_EXTRA[s])
                out_unit(u0 + FT, 0, 0, True)
                pe.wait_ge(h_ready, 1 + FT * (f + 1))
                with pe.Fori(0, (FFN_OUT_UNITS - 2) // RING) as i:
                    for b in range(RING):
                        out_unit(u0 + FT + 1 + b, 1 + b, i)
                u = u0 + FFN_UNITS - 1
                pe.wait_ge(lo_done, RING + u + 1)
                for d in range(KT):
                    for h in range(2):
                        ft = FT - 2 + h
                        ins = three(ps[:, d, 0:TOK], tile_of(w_hi, u, h * KT + d), tile_of(w_lo, u, h * KT + d),
                                    h_hi[:, ft, :], h_lo[:, ft, :], False, h == 1)
                    ins.then_inc(y_done if d < KT - 1 else unit_done, 1)

            def proj_out(u, kt0, d0, last, ready):
                pe.wait_ge(lo_done, RING + u + 1)
                for d in range(4):
                    for k in range(4):
                        if d == 0:
                            pe.wait_ge(mix_ready, ready + k + 1)
                        at = k * 4 + d
                        ins = three(ps[:, d0 + d, 0:TOK], tile_of(w_hi, u, at), tile_of(w_lo, u, at),
                                    a_hi[:, kt0 + k, :], a_lo[:, kt0 + k, :], not last and k == 0, last and k == 3)
                    if last:
                        ins.then_inc(y_done if d < 3 else unit_done, 1)
                if not last:
                    ins.then_inc(unit_done, 1)

            pe.sem_inc(unit_done, RING)
            pe.sem_inc(mod_used, MRING)

            pe.wait_ge(const_in, 16)
            pe.wait_ge(cond_in, 32)
            nc.tensor.transpose(ps[:, 0, 0:2 * KT], cond_rows[:], ident[0:2 * KT, 0:2 * KT]).then_inc(cond_t, 1)
            pe.wait_ge(cond_ready, 2)
            for b in range(MRING):
                mod_sums(0, b)
            pe.wait_ge(x_in, 32)
            for d in range(KT):
                if d >= 6:
                    pe.wait_ge(x_ready, d - 5)
                for tt in range(TT):
                    ins = nc.tensor.transpose(ps[:, d % 6, tt * P:(tt + 1) * P], x_nat[:, tt, d * P:(d + 1) * P], ident[:])
                ins.then_inc(x_t, 1)
            pe.wait_ge(pick_ready, 1)
            mod_columns(0)
            mod_sums(1, 0)
            pe.wait_ge(x_ready, KT)
            norm_sums(0)
            pe.wait_ge(vectors_in, 16 * 13)
            for v in range(2):
                n = (A_ROWS, B_ROWS)[v]
                nc.tensor.transpose(ps[:, 1 + v, 0:n], rows[0:n, v, :], ident[0:n, 0:n]).then_inc(rows_t, 1)
            for j in range(CT):
                ins = nc.tensor.transpose(ps[:, 3, j * CONV_K:(j + 1) * CONV_K], conv_rows[:, j * P:(j + 1) * P],
                                          ident[0:CONV_K, 0:CONV_K])
            ins.then_inc(rows_t, 1)
            norm_spread(0)
            for b in range(1, MRING):
                mod_sums(1, b)
            mod_columns(1)
            pe.wait_ge(rows_c, 3)
            for b in range(MRING):
                mod_sums(2, b)
            mod_columns(2)
            ffn(0)

            norm(1)
            u = UNIT0[1]
            in_unit(u, GLU_BANK[0], 1)
            in_unit(u + 1, GLU_BANK[1])
            in_unit(u + 2, QKV_BANK[2])
            in_unit(u + 3, QKV_BANK[3])

            def qk_sums(j):
                pe.wait_ge(qk_sq_done, (j + 1) % (QT + 1) + 1)
                for tt in range(TT):
                    n = 2 * (TT * j + tt)
                    ins = mm(ps[:, 6, n:n + 2], qk_sq[:, j, tt * P:(tt + 1) * P], pick_half[:], start=True, stop=True)
                return ins

            pe.wait_ge(e_zero, 4)
            pe.wait_ge(glu_done, 2)
            qk_sums(QT)
            in_unit(u + 4, QKV_BANK[4])
            qk_sums(0)
            qk_sums(1)
            pe.wait_ge(e_in, 48)
            pe.wait_ge(qk_copied, 4)
            nc.tensor.transpose(ps[:, 2, 0:P], ck_nat[:], ident[:])
            for tt in range(TT):
                ins = nc.tensor.transpose(ps[:, 3, tt * P:(tt + 1) * P], v_raw[:, tt * P:(tt + 1) * P], ident[:])
            ins.then_inc(e_t, 1)
            qk_sums(2)
            qk_sums(3).then_inc(qk_stat, 1)
            in_unit(u + 5, GLU_BANK[2])
            pe.wait_ge(qk_copied, QT + 2)
            pe.wait_ge(qk_wide_done, 1)
            pe.wait_ge(kdup_done, 4)
            for j in range(QT + 1):
                for tt in range(TT):
                    n = 2 * (TT * j + tt)
                    ins = mm(ps[:, BC_BANKS[j], tt * P:(tt + 1) * P], qk_wide[:, n:n + 2, :].rearrange("p a b -> p (a b)"),
                             ident[:], start=True, stop=True)
                ins.then_inc(qk_bc, 1)
            pe.wait_ge(qk_normed, 3)
            for lo, hi, bank in SWAP_BANKS:
                for j in range(lo, hi):
                    pe.wait_ge(qk_normed, j + 1)
                    ins = mm(ps[:, bank, (j - lo) * LAT:(j - lo + 1) * LAT], rope[:, R_SWAP:R_SWAP + P], qk[:, j, CTX:],
                             start=True, stop=True)
            ins.then_inc(swap_done, 1)
            nc.tensor.transpose(ps[:, 3, 0:P], qk[:, QT, 0:CTX], ident[:]).then_inc(e_t, 1)
            in_unit(u + 6, GLU_BANK[3])
            pe.wait_ge(glu_done, 3)
            pe.wait_ge(roped, 5)
            pe.wait_ge(kdup_done, 4)
            pe.wait_ge(e_tc, 2)
            N = HEADS * TT

            def scores(n):
                head, tt = n // TT, n % TT
                j, o, g = head // 2, (head % 2) * HD, head // (HEADS // KV_HEADS)
                keys = slice(0, CTX) if tt == 0 else slice(CTX, TOK + PAST)
                if n >= 2:
                    pe.wait_ge(exp_done, n - 1)
                mm(ps[:, 4 + n % 2, 0:keys.stop - keys.start], qk[o:o + HD, j, tt * P:(tt + 1) * P],
                   kdup[o:o + HD, g, keys], start=True, stop=True).then_inc(score_done, 1)

            def flip(n):
                pe.wait_ge(prob_done, n + 1)
                if n == 0:
                    pe.wait_ge(glu_done, CT)
                if n >= 2:
                    pe.wait_ge(pt_copied, n - 1)
                for k in range(1 if n % TT == 0 else 3):
                    ins = nc.tensor.transpose(ps[:, 6 + n % 2, k * P:(k + 1) * P], prob[:, n % 2, k * P:(k + 1) * P], ident[:])
                ins.then_inc(pt_done, 1)

            def values(n):
                head, tt = n // TT, n % TT
                j, o, g = head // 2, (head % 2) * HD, head // (HEADS // KV_HEADS)
                tiles = [0] if tt == 0 else [1, 2, 3]
                pe.wait_ge(pt_copied, n + 1)
                for k, v in enumerate(tiles):
                    ins = mm(ps[o:o + HD, j, tt * P:(tt + 1) * P], v_nat[:, v, g * HD:(g + 1) * HD],
                             prob_t[:, n % 2, k * P:(k + 1) * P], start=k == 0, stop=k == len(tiles) - 1)
                ins.then_inc(pv_done, 1)

            scores(0)
            scores(1)
            for n in range(N):
                if n + 2 < N:
                    scores(n + 2)
                flip(n)
                if n:
                    values(n - 1)
            values(N - 1)

            def means(m, src, at, ready):
                for sgm, lo, hi in SEGS:
                    for j in range(CT):
                        ins = mm(ps[:, 4, lo:hi], ones_mean[:], src[:, j, at[sgm]:at[sgm] + hi - lo],
                                 start=j == 0, stop=j == CT - 1)
                ins.then_inc(ln_mean_done, 1)

            def variances(m, sq, bank):
                for j in range(CT):
                    pe.wait_ge(ln_sq, CT * m + j + 1)
                    ins = token_sums(ps[:, bank, :], sq[:, j, :], j, j == CT - 1)
                ins.then_inc(ln_stat, 1)

            pe.wait_ge(conv_done, len(DVE_TILES))
            pe.wait_ge(tap_added, len(POOL_TILES) * (CONV_K - 1))
            means(0, conv, CONV_AT, 0)
            proj_out(u + 7, 0, 0, False, 0)
            variances(0, qk_sq, 7)
            pe.wait_ge(ln_ms, 1)
            proj_out(u + 8, 0, 4, False, 0)
            pe.wait_ge(ln_diag, 1)
            for tt in range(TT):
                ins = mm(ps[:, 4 + tt, TOK:], ones[:], e_diag[:, tt, :], start=False, stop=False, skip_group_check=True)
            ins.then_inc(ln_bc, 1)
            pe.wait_ge(ln_y, CT)
            proj_out(u + 9, 4, 0, True, QT)
            proj_out(u + 10, 4, 4, True, QT)
            norm(2)
            ffn(2)
            norm(3)
            ffn(3)

            norm(4)
            u = UNIT0[4]
            in_unit(u, O_BANK[0], 4)
            in_unit(u + 1, O_BANK[1])
            in_unit(u + 2, O_BANK[2])
            pe.wait_ge(o_copied, 4)
            means(1, o_v, [0, CTX], 0)
            in_unit(u + 3, O_BANK[3])
            in_unit(u + 4, O_BANK[4])
            variances(1, o_sq, 5)
            pe.wait_ge(o_copied, 6)
            in_unit(u + 5, O_BANK[5])
            pe.wait_ge(ln_diag, 2)
            spread(4, o_diag).then_inc(ln_bc, 1)
            pe.wait_ge(o_in, 16 * (2 + CT))
            for n in range(2 * TT):
                tt, h = n // 2, n % 2
                if n < 5:
                    pe.wait_ge(o_copied, (8, 8, 10, 10, 10)[n])
                else:
                    pe.wait_ge(o_z_copied, 1)
                for gg in range(2):
                    ins = mm(ps[:, O_ZBANK[n], gg * 2 * P:(gg + 1) * 2 * P], o_f[:, 2 * h + gg, tt * P:(tt + 1) * P],
                             fourier[:, F_CH:F_CH + 2 * P], start=True, stop=True)
                ins.then_inc(o_z_done, 1)
            pe.wait_ge(o_copied, 12)
            for g in range(CT):
                ins = nc.tensor.transpose(ps[:, 6, g * P:(g + 1) * P], ws_nat[:, g, :], ident[:])
            ins.then_inc(o_t, 1)
            pe.wait_ge(ln_out, 2 * CT)
            pe.wait_ge(o_z_copied, 3)
            for tt in range(TT):
                for j in range(CT):
                    ins = nc.tensor.transpose(ps[:, O_VBANK[tt], j * P:(j + 1) * P], o_v[:, j, tt * P:(tt + 1) * P], ident[:])
                ins.then_inc(o_t, 1)
            pe.wait_ge(o_z_copied, 6)
            pe.wait_ge(o_tc, 2)
            for g in range(CT):
                for cs in range(2):
                    z = slice(g * 2 * P + cs * P, g * 2 * P + (cs + 1) * P)
                    mm(ps[:, 4 + g, 0:CTX], o_z[:, 0, z], fourier[:, F_CTX + cs * P:F_CTX + (cs + 1) * P],
                       start=cs == 0, stop=cs == 1)
                for cs in range(2):
                    z = slice(g * 2 * P + cs * P, g * 2 * P + (cs + 1) * P)
                    for lt in range(2):
                        at = F_LAT + (2 * lt + cs) * LAT
                        ins = mm(ps[:, 4 + g, CTX:TOK], o_z[:, 1 + lt, z], fourier[:, at:at + LAT],
                                 start=cs == 0 and lt == 0, stop=cs == 1 and lt == 1)
                ins.then_inc(o_four, 1)
            pe.wait_ge(o_tc, 1 + TT)
            for g in range(CT):
                for tt in range(TT):
                    ins = mm(ps[:, g, tt * P:(tt + 1) * P], o_vn[:, tt, g * P:(g + 1) * P], ws_t[:, g, :], start=True, stop=True)
                ins.then_inc(o_sgu, 1)
            proj_out(u + 6, 0, 4, False, 2 * QT)
            pe.wait_ge(o_bias, CT)
            proj_out(u + 7, 0, 0, False, 2 * QT)
            proj_out(u + 8, 4, 0, True, 3 * QT)
            proj_out(u + 9, 4, 4, True, 3 * QT)
            norm(5)
            ffn(5)
            pe.wait_ge(x_ready, KT * (N_SUB + 1))
            for tt in range(TT):
                for d in range(KT):
                    ins = nc.tensor.transpose(ps[:, 2 * tt + d // 4, (d % 4) * P:(d % 4 + 1) * P],
                                              x[:, d, tt * P:(tt + 1) * P], ident[:])
                ins.then_inc(out_t, 1)


FFN_AT = {0: 0, 2: 1, 3: 2, 5: 3}
M_Y = {0: 0, 2: 6, 3: 6, 5: 12}
O_BANK = [0, 2, 6, 0, 2, 6]
O_ZBANK = [0, 1, 2, 3, 5, 0]
O_VBANK = [7, 1, 2]
GLU_BANK = [0, 6, 4, 6]
QKV_BANK = {2: 2, 3: 4, 4: 0}
BC_BANKS = [0, 1, 2, 3, 7]
SWAP_BANKS = [(0, 2, 2), (2, 4, 0), (4, 5, 1)]
ADDED = KT - 2
BC_BANK = [5, 7, 7, 7, 7, 7]

_INS = ["x_prompt", "x_sample", "cache_k", "cache_v", "c", "c_ctx", "w_mod", "b_mod", "norm_g", "ffn_w_in",
        "ffn_w_out", "ev_w_in", "ev_w_out", "q_norm_g", "k_norm_g", "conv_w", "conv_b", "conv_norm_g",
        "conv_norm_b", "od_w_in", "od_w_out", "sgu_norm_g", "sgu_norm_b", "sgu_w", "sgu_b"]
_OUTS = [(1, CTX, D_MODEL), (1, LAT, D_MODEL), (1, 1, CTX, KV_HEADS, HD), (1, 1, CTX, KV_HEADS, HD)]


def kernel(**inputs):
    import concourse.bacc as bacc
    from concourse.bass_utils import run_bass_kernel_spmd

    nc = bacc.Bacc("TRN2", target_bir_lowering=False, num_devices=1)
    named = {n: np.ascontiguousarray(inputs[n]) for n in _INS}
    named.update(zip(("k_ident", "k_rope", "k_fourier"), shape_constants()))
    arrays, args = {}, []
    for name, a in named.items():
        arrays[f"in_{name}"] = a
        args.append(nc.dram_tensor(f"in_{name}", a.shape, mybir.dt.from_np(a.dtype), kind="ExternalInput").ap())
    for i, shape in enumerate(_OUTS):
        args.append(nc.dram_tensor(f"out_{i}", shape, FP32, kind="ExternalOutput").ap())
    build(nc, *args)
    result = run_bass_kernel_spmd(nc, [arrays], core_ids=[0])
    return tuple(result.results[0][f"out_{i}"] for i in range(len(_OUTS)))
```

```python
from contextlib import ExitStack

import numpy as np

import concourse.bass as bass
import concourse.mybir as mybir

FP32 = mybir.dt.float32
F32R = mybir.dt.float32r
ALU = mybir.AluOpType
ACT = mybir.ActivationFunctionType
AX = mybir.AxisListType

P = 128
D_MODEL, CTX, LAT, PAST = 1024, 128, 256, 128
TOK = CTX + LAT
TT = TOK // P
SEGS = [(0, 0, CTX), (1, CTX, TOK)]
KT = D_MODEL // P
FFN = 2816
FT = FFN // P
HEADS, KV_HEADS, HD = 8, 2, 64
QT = HEADS * HD // P
GRID_W, THETA = 64, 10000.0
CONV_CH, CONV_K = 512, 31
CT = CONV_CH // P
PADW = CONV_K // 2
PAD_AT = [PADW, 2 * PADW + CTX]
PAD_N = 3 * PADW + TOK
CONV_N = PAD_N - (CONV_K - 1)
CONV_AT = [0, CTX + PADW]
N_MOD = 9
N_SUB = 6
MODT = N_MOD * KT
RMS_EPS, LN_EPS = 1e-6, 1e-5
EARLY_TAPS = 3
POOL_TILES, TAP_BUFS = [0, 3], 2
DVE_TILES = [1, 2]

RING = 3
MRING = 3
UNIT = 2048
HALF = UNIT // 2
FFN_OUT_UNITS = FT // 2
FFN_UNITS = FT + FFN_OUT_UNITS
M0_UNITS, M1_UNITS = 11, 10
_sizes = [FFN_UNITS, M0_UNITS, FFN_UNITS, FFN_UNITS, M1_UNITS, FFN_UNITS]
UNIT0 = [sum(_sizes[:i]) for i in range(6)]
UNITS = sum(_sizes)

PAIR = 2 * P
PAIR_TILES = 2
GROUPS_FIRST = 3
LOOPS = (FT - 1) // RING
MOD_LOOPS = {0: LOOPS, 2: LOOPS, 3: LOOPS - 1, 5: 0}
MOD_EXTRA = {0: 1, 2: 0, 3: 0, 5: 0}
GROUP0, _p = {}, GROUPS_FIRST
for _s in (0, 2, 3, 5):
    GROUP0[_s] = _p
    _p += MOD_LOOPS[_s] + MOD_EXTRA[_s]
assert _p * MRING == 2 * MODT // PAIR_TILES
LAYER_PAIRS = MODT // PAIR_TILES
LAYER_GROUPS = LAYER_PAIRS // MRING
COND_ROWS = 32
COND_AT = 2 * (MRING - 1)

A_BMOD, A_NORM_G, A_ROWS = 0, MODT, MODT + N_SUB * KT
B_BMOD, B_CONV_B = 0, MODT
B_CN_G, B_CN_B, B_SN_G, B_SN_B = (B_CONV_B + CT * i for i in range(1, 5))
B_QG = B_CONV_B + 5 * CT
B_KG, B_ROWS = B_QG + 1, B_QG + 2

R_SWAP, R_COS, R_SIN, R_N = 0, P, P + LAT, P + 2 * LAT
F_CH, F_LAT, F_CTX, F_N = 0, 2 * P, 2 * P + 4 * LAT, 2 * P + 4 * LAT + 2 * P


def shape_constants():
    ident = np.eye(P, dtype=np.float32)
    swap = ident.reshape(P // 2, 2, P)[:, ::-1].reshape(P, P)
    t = np.arange(LAT)
    row, col = (t // GRID_W).astype(np.float32), (t % GRID_W).astype(np.float32)
    half = HD // 2
    freq = (1.0 / np.float32(THETA) ** (np.arange(0, half, 2, dtype=np.float32) / np.float32(half))).astype(np.float32)
    ang = np.concatenate([row[:, None] * freq, col[:, None] * freq], axis=-1)
    cos = np.repeat(np.cos(ang), 2, axis=1).T
    sin = np.repeat(np.sin(ang), 2, axis=1).T * np.tile([-1.0, 1.0], half)[:, None]
    rope = np.concatenate([swap, np.tile(cos, (2, 1)), np.tile(sin, (2, 1))], axis=1)

    def dft(n):
        a = 2 * np.pi * (np.outer(np.arange(n), np.arange(n)) % n) / n
        return np.cos(a), np.sin(a)

    cc, cs = dft(P)
    lc, ls = dft(LAT)
    lat = np.concatenate([lc[0:P], -ls[0:P], lc[P:], -ls[P:]], axis=1)
    fourier = np.concatenate([cc, cs, lat, cc, -cs], axis=1)
    return (ident, np.ascontiguousarray(rope, dtype=np.float32), np.ascontiguousarray(fourier, dtype=np.float32))


def build(nc, x_prompt, x_sample, cache_k, cache_v, c, c_ctx, w_mod, b_mod, norm_g, ffn_w_in, ffn_w_out,
          ev_w_in, ev_w_out, q_norm_g, k_norm_g, conv_w, conv_b, conv_norm_g, conv_norm_b, od_w_in, od_w_out,
          sgu_norm_g, sgu_norm_b, sgu_w, sgu_b, k_ident, k_rope, k_fourier,
          y_prompt, y_sample, new_cache_k, new_cache_v):
    ctx = ExitStack()
    with ctx:
        def sb(name, shape, dt=FP32, stack=ctx):
            return stack.enter_context(nc.sbuf_tensor(name, shape, dt))

        def sem(name):
            return ctx.enter_context(nc.semaphore(name))

        w_raw = sb("w_raw", [P, RING, UNIT])
        w_hi = sb("w_hi", [P, RING, UNIT], F32R)
        w_lo = sb("w_lo", [P, RING, UNIT], F32R)
        m_raw = sb("m_raw", [P, MRING, UNIT])
        x = sb("x", [P, KT, TOK])
        a_hi = sb("a_hi", [P, KT, TOK], F32R)
        a_lo = sb("a_lo", [P, KT, TOK], F32R)
        ident = sb("ident", [P, P])
        ones = sb("ones", [P, P])
        ones_mean = sb("ones_mean", [P, P])
        vec_a = sb("vec_a", [P, A_ROWS])
        vec_b = sb("vec_b", [P, B_ROWS])
        conv_wt = sb("conv_wt", [P, CT, CONV_K])
        cond = sb("cond", [P, KT, COND_AT + COND_ROWS])
        mod_pick = sb("mod_pick", [P, 2 * MRING])
        mod_part = sb("mod_part", [P, PAIR])
        mod_cols = sb("mod_cols", [P, 2 * MODT, 2])
        m_shift = sb("m_shift", [P, N_SUB, KT, 2])
        m_scale = sb("m_scale", [P, N_SUB, KT, 2])
        m_gate = sb("m_gate", [P, N_SUB, KT, 2])
        stat = sb("stat", [P, 32])
        stat_row = sb("stat_row", [P, 32])
        warm = sb("warm", [P, 16])
        glu = sb("glu", [P, 1, TOK])

        r = ExitStack()
        h_hi = sb("h_hi", [P, FT, TOK], F32R, r)
        h_lo = sb("h_lo", [P, FT, TOK], F32R, r)
        r.close()
        r = ExitStack()
        n_sq = sb("n_sq", [P, KT, TOK], stack=r)
        n_diag = sb("n_diag", [P, TT, P], stack=r)
        n_acc = sb("n_acc", [P, TOK], stack=r)
        n_full = sb("n_full", [P, KT, TOK], stack=r)
        cond_rows = sb("cond_rows", [2 * KT, P], stack=r)
        rows = sb("rows", [P, 2, P], stack=r)
        conv_rows = sb("conv_rows", [CONV_K, CONV_CH], stack=r)
        x_nat = sb("x_nat", [P, TT, D_MODEL], stack=r)
        r.close()
        r = ExitStack()
        e_diag = sb("e_diag", [P, TT, P], stack=r)
        taps_buf = sb("taps_buf", [P, TAP_BUFS, CONV_N], stack=r)
        padded = sb("padded", [P, CT, PAD_N], stack=r)
        conv = sb("conv", [P, CT, CONV_N], stack=r)
        e_sig = sb("e_sig", [P, 2, TOK], stack=r)
        qk = sb("qk", [P, QT + 1, TOK], stack=r)
        qk_sq = sb("qk_sq", [P, QT + 1, TOK], stack=r)
        qk_wide = sb("qk_wide", [P, 2 * TT * (QT + 1), HD], stack=r)
        v_raw = sb("v_raw", [P, TOK], stack=r)
        rope = sb("rope", [P, R_N], stack=r)
        pick_half = sb("pick_half", [P, 2], stack=r)
        rot = sb("rot", [P, QT + 1, LAT], stack=r)
        kdup = sb("kdup", [P, KV_HEADS, TOK + PAST], stack=r)
        ck_nat = sb("ck_nat", [P, P], stack=r)
        v_nat = sb("v_nat", [P, TT + 1, P], stack=r)
        k_nat = sb("k_nat", [P, P], stack=r)
        prob = sb("prob", [P, 2, TOK], stack=r)
        prob_t = sb("prob_t", [P, 2, TOK], stack=r)
        smax = sb("smax", [P, HEADS * TT], stack=r)
        smaxn = sb("smaxn", [P, HEADS * TT], stack=r)
        ssum = sb("ssum", [P, HEADS * TT], stack=r)
        srec = sb("srec", [P, HEADS * TT], stack=r)
        r.close()
        r = ExitStack()
        o_diag = sb("o_diag", [P, TT, P], stack=r)
        o_v = sb("o_v", [P, CT, TOK], stack=r)
        o_f = sb("o_f", [P, CT, TOK], stack=r)
        o_u = sb("o_u", [P, CT, TOK], stack=r)
        o_sq = sb("o_sq", [P, CT, TOK], stack=r)
        o_vn = sb("o_vn", [P, TT, CONV_CH], stack=r)
        o_z = sb("o_z", [P, TT, 2 * CONV_CH], stack=r)
        fourier = sb("fourier", [P, F_N], stack=r)
        ws_nat = sb("ws_nat", [P, CT, P], stack=r)
        ws_t = sb("ws_t", [P, CT, P], stack=r)
        bs = sb("bs", [P, CT, P], stack=r)
        r.close()

        ps = ctx.enter_context(nc.psum_tensor("ps", [P, 8, 512], FP32))

        raw_in = [sem(f"raw_in{i}") for i in range(RING)]
        hi_done = sem("hi_done")
        lo_done = sem("lo_done")
        unit_done = sem("unit_done")
        mod_in = [sem(f"mod_in{i}") for i in range(MRING)]
        mod_used = sem("mod_used")
        part_copied = sem("part_copied")
        cols_done = sem("cols_done")
        cols_copied = sem("cols_copied")
        const_in, cond_in, x_in = sem("const_in"), sem("cond_in"), sem("x_in")
        cond_t = sem("cond_t")
        vectors_in = sem("vectors_in")
        setup = sem("setup")
        pick_ready = sem("pick_ready")
        rows_t, rows_c = sem("rows_t"), sem("rows_c")
        cond_ready = sem("cond_ready")
        x_t = sem("x_t")
        x_ready = sem("x_ready")
        y_done = sem("y_done")
        sq_done, stat_done, ms_done, root_done, diag_done, bc_done = (
            sem(n) for n in ("sq_done", "stat_done", "ms_done", "root_done", "diag_done", "bc_done"))
        full_done, a_hi_done, a_ready = sem("full_done"), sem("a_hi_done"), sem("a_ready")
        dve_self = sem("dve_self")
        acc_done = sem("acc_done")
        silu_done, h_hi_done = sem("silu_done"), sem("h_hi_done")
        prod_done, h_ready = sem("prod_done"), sem("h_ready")
        out_in, out_t, out_c, out_done = sem("out_in"), sem("out_t"), sem("out_c"), sem("out_done")
        e_in, e_zero, sig_done, glu_done, conv_done = (
            sem(n) for n in ("e_in", "e_zero", "sig_done", "glu_done", "conv_done"))
        qk_copied, qk_sq_done, qk_stat, qk_ms, qk_root, qk_wide_done, qk_bc, qk_normed = (
            sem(n) for n in ("qk_copied", "qk_sq_done", "qk_stat", "qk_ms", "qk_root", "qk_wide_done",
                             "qk_bc", "qk_normed"))
        swap_done, roped, e_t, e_tc, kdup_done, cache_out = (
            sem(n) for n in ("swap_done", "roped", "e_t", "e_tc", "kdup_done", "cache_out"))
        score_done, max_done, exp_done, prob_done, pt_done, pt_copied, pv_done = (
            sem(n) for n in ("score_done", "max_done", "exp_done", "prob_done", "pt_done", "pt_copied", "pv_done"))
        mix_hi, mix_ready = sem("mix_hi"), sem("mix_ready")
        tap_ready, tap_added = sem("tap_ready"), sem("tap_added")
        ln_mean_done, ln_xc, ln_sq, ln_stat, ln_ms, ln_root, ln_diag, ln_bc, ln_y = (
            sem(n) for n in ("ln_mean_done", "ln_xc", "ln_sq", "ln_stat", "ln_ms", "ln_root",
                             "ln_diag", "ln_bc", "ln_y"))
        ln_out = sem("ln_out")
        conv_summed, v_summed = sem("conv_summed"), sem("v_summed")
        ln_added = sem("ln_added")
        o_in, o_copied, o_t, o_tc, o_z_done, o_z_copied, o_sgu, o_bias, o_four = (
            sem(n) for n in ("o_in", "o_copied", "o_t", "o_tc", "o_z_done", "o_z_copied", "o_sgu", "o_bias",
                             "o_four"))

        block = ctx.enter_context(nc.Block())

        def slot(u):
            return u % RING

        def half(tile, u, h):
            return tile[:, slot(u), h * HALF:(h + 1) * HALF]

        def ffn_of(s):
            return (0, 0) if s == 0 else (0, 1) if s == 2 else (1, 0) if s == 3 else (1, 1)

        def probs(m):
            return e_sig if m % 2 else prob

        def conv_sum():
            return rot[:].rearrange("p a b -> p (a b)")[:, 0:CONV_N]

        @block.sync
        def _(sp):
            def load_unit(u, i, halves):
                sp.wait_ge(lo_done, u + 1 + RING * i)
                for h, src in enumerate(halves):
                    dst = half(w_raw, u, h).rearrange("p (a b) -> p a b", a=src.shape[1])
                    sp.dma_start(dst, src).then_inc(raw_in[slot(u)], 16)

            def cols(w, start, n=P):
                return w.rearrange("(k p) n -> p k n", p=P)[:, :, bass.ds(start, n)]

            def load_pair(group, b, i, layer):
                sp.wait_ge(mod_used, MRING * group + b + 1 + MRING * i)
                start = (group - layer * LAYER_GROUPS) * MRING * PAIR + b * PAIR + i * MRING * PAIR
                sp.dma_start(m_raw[:, b, :].rearrange("p (a n) -> p a n", a=KT),
                             cols(w_mod[layer], start, PAIR)).then_inc(mod_in[b], 16)

            def load_ffn(s):
                layer, which = ffn_of(s)
                win, wout = ffn_w_in[layer, which], ffn_w_out[layer, which]
                u0, g0 = UNIT0[s], GROUP0[s]

                def in_unit(u, t, i):
                    load_unit(u, i, [cols(win, h * FFN + t * P + i * RING * P) for h in range(2)])

                def out_unit(u, t, i):
                    load_unit(u, i, [wout[bass.ds((2 * t + h) * P + i * 2 * RING * P, P), :]
                                     .rearrange("p (a n) -> p a n", a=1) for h in range(2)])

                if s == 0:
                    for pair in range(MRING, MRING * GROUPS_FIRST):
                        if pair == MRING * GROUPS_FIRST - 2:
                            in_unit(u0, 0, 0)
                        load_pair(pair // MRING, pair % MRING, 0, 0)
                else:
                    in_unit(u0, 0, 0)
                in_unit(u0 + 1, 1, 0)
                in_unit(u0 + 2, 2, 0)
                mods = MOD_LOOPS[s]
                rounds = min(mods, LOOPS - 1)
                first = max(0, min(rounds, LAYER_GROUPS - g0))
                parts = [(first, 0), (rounds - first, 1), (LOOPS - 1 - rounds, None)]
                done = 0
                for n, mod_layer in parts:
                    if n > 0:
                        with sp.Fori(0, n) as i:
                            for b in range(RING):
                                t = 1 + RING * done + b
                                in_unit(u0 + t + 2, t + 2, i)
                                if mod_layer is not None:
                                    load_pair(g0 + done, b, i, mod_layer)
                        done += n
                for b in range(RING):
                    t = 1 + RING * done + b
                    if t + 2 < FT:
                        in_unit(u0 + t + 2, t + 2, 0)
                    else:
                        out_unit(u0 + t + 2, t + 2 - FT, 0)
                    if mods == LOOPS:
                        load_pair(g0 + done, b, 0, (g0 + done) // LAYER_GROUPS)
                if MOD_EXTRA[s]:
                    for b in range(MRING):
                        load_pair(g0 + mods, b, 0, (g0 + mods) // LAYER_GROUPS)
                with sp.Fori(0, (FFN_OUT_UNITS - 2) // RING) as i:
                    for b in range(RING):
                        out_unit(u0 + FT + 2 + b, 2 + b, i)

            def load_proj_out(u, w, kt0, d0):
                load_unit(u, 0, [w[(kt0 + 2 * h) * P:(kt0 + 2 * h + 2) * P, d0 * P:(d0 + 4) * P]
                                 .rearrange("(k p) n -> p k n", p=P) for h in range(2)])

            sp.dma_start(ident[:], k_ident).then_inc(const_in, 16)
            sp.dma_start(cond_rows[0:KT, :], c_ctx.rearrange("(r n) -> r n", n=P)).then_inc(cond_in, 16)
            sp.dma_start(cond_rows[KT:2 * KT, :], c[0].rearrange("(r n) -> r n", n=P)).then_inc(cond_in, 16)
            for b in range(MRING):
                load_pair(0, b, 0, 0)
            sp.dma_start(x_nat[:, 0, :], x_prompt[0]).then_inc(x_in, 16)
            sp.dma_start(x_nat[:, 1:TT, :], x_sample[0].rearrange("(a p) n -> p a n", p=P)).then_inc(x_in, 16)
            load_ffn(0)
            u = UNIT0[1]
            a0 = (HEADS + 2 * KV_HEADS) * HD

            def glu_unit(n, j):
                load_unit(u + n, 0, [cols(ev_w_in[0], a0 + h * CONV_CH + j * P) for h in range(2)])

            glu_unit(0, 0)
            glu_unit(1, 1)
            for n, tile in ((2, 4), (3, 0), (4, 2)):
                load_unit(u + n, 0, [cols(ev_w_in[0], (tile + h) * P) for h in range(2)])
            sp.wait_ge(a_ready, 2 * KT)
            sp.wait_ge(unit_done, RING + UNIT0[1])
            for dst, src in ((rope[:], k_rope), (ck_nat[:], cache_k[0, 0].rearrange("t g d -> t (g d)")),
                             (v_nat[:, TT, :], cache_v[0, 0].rearrange("t g d -> t (g d)"))):
                sp.dma_start(dst, src).then_inc(e_in, 16)
            for j in range(2, CT):
                glu_unit(3 + j, j)
            for j, (kt0, d0) in enumerate(((0, 0), (0, 4), (4, 0), (4, 4))):
                load_proj_out(u + CT + 3 + j, ev_w_out[0], kt0, d0)
            load_ffn(2)
            load_ffn(3)
            u = UNIT0[4]
            for j, base in enumerate((8, 10, 0, 2, 4, 6)):
                load_unit(u + j, 0, [cols(od_w_in[0], (base + h) * P) for h in range(2)])
                if j == 3:
                    sp.wait_ge(a_ready, 5 * KT)
                    sp.wait_ge(unit_done, RING + u)
                    for dst, src in ((fourier[:], k_fourier), (ws_nat[:], sgu_w[0].rearrange("g p q -> p g q"))):
                        sp.dma_start(dst, src).then_inc(o_in, 16)
                    for g in range(CT):
                        sp.dma_start(bs[:, g, :], sgu_b[0, g:g + 1, :].to_broadcast([P, P])).then_inc(o_in, 16)
            for j, (kt0, d0) in enumerate(((0, 4), (0, 0), (4, 0), (4, 4))):
                load_proj_out(u + 6 + j, od_w_out[0], kt0, d0)
            load_ffn(5)
            for tt in range(TT):
                sp.wait_ge(out_c, tt + 1)
                dst = y_prompt[0] if tt == 0 else y_sample[0, (tt - 1) * P:tt * P, :]
                sp.dma_start(dst, x_nat[:, tt, :]).then_inc(out_done, 16)
            sp.wait_ge(out_done, 16 * TT)
            sp.wait_ge(cache_out, 32)

        @block.gpsimd
        def _(pool):
            nc.gpsimd.memset(cond[:], 0.0).then_inc(setup, 1)
            nc.gpsimd.memset(ones[:], 1.0).then_inc(setup, 1)
            nc.gpsimd.memset(ones_mean[:], 1.0 / CONV_CH).then_inc(setup, 1)

            def add_squares(n):
                for d in range(1, ADDED):
                    pool.wait_ge(sq_done, KT * n + d + 1)
                    if n or d > 1:
                        pool.wait_ge(acc_done, (ADDED - 1) * n + d - 1)
                    first = n_sq[:, 0, :] if d == 1 else n_acc[:]
                    nc.gpsimd.tensor_tensor(n_acc[:], first, n_sq[:, d, :], ALU.add).then_inc(acc_done, 1)

            add_squares(0)
            add_squares(1)
            pool.wait_ge(unit_done, RING + UNIT0[1])
            pool.wait_ge(a_ready, 2 * KT)
            nc.gpsimd.memset(padded[:], 0.0).then_inc(e_zero, 1)
            nc.gpsimd.memset(pick_half[:], 0.0).then_inc(e_zero, 1)
            pool.wait_ge(e_zero, 2)
            nc.gpsimd.memset(pick_half[0:HD, 0:1], 1.0).then_inc(e_zero, 1)
            nc.gpsimd.memset(pick_half[HD:P, 1:2], 1.0).then_inc(e_zero, 1)
            pool.wait_ge(e_zero, 4)
            for m, j in enumerate(POOL_TILES):
                acc = conv[:, j, :]
                for k in range(1, CONV_K):
                    n = m * (CONV_K - 1) + k - 1
                    pool.wait_ge(tap_ready, m * CONV_K + k + 1)
                    if n:
                        pool.wait_ge(tap_added, n)
                    nc.gpsimd.tensor_tensor(acc, acc, taps_buf[:, n % TAP_BUFS, :], ALU.add).then_inc(tap_added, 1)
            pool.wait_ge(tap_added, len(POOL_TILES) * (CONV_K - 1))

            def add_channel_squares(m, sq):
                for j in range(1, CT):
                    pool.wait_ge(ln_sq, CT * m + j + 1)
                    if m or j > 1:
                        pool.wait_ge(ln_added, (CT - 1) * m + j - 1)
                    nc.gpsimd.tensor_tensor(sq[:, 0, :], sq[:, 0, :], sq[:, j, :], ALU.add).then_inc(ln_added, 1)

            add_channel_squares(0, qk_sq)
            pool.wait_ge(ln_added, CT - 1)
            for n in range(2, 5):
                add_squares(n)
            pool.wait_ge(acc_done, (ADDED - 1) * 5)
            for j in range(1, CT):
                pool.wait_ge(o_copied, j + 1)
                if j > 1:
                    pool.wait_ge(v_summed, j - 1)
                nc.gpsimd.tensor_tensor(o_vn[:, 0, 0:TOK], o_v[:, 0, :] if j == 1 else o_vn[:, 0, 0:TOK], o_v[:, j, :],
                                        ALU.add).then_inc(v_summed, 1)
            pool.wait_ge(v_summed, CT - 1)
            add_channel_squares(1, o_sq)
            pool.wait_ge(ln_added, 2 * (CT - 1))
            add_squares(5)

        @block.scalar
        def _(act):
            act.wait_ge(setup, 2)
            nc.scalar.activation(warm[:, 15:16], ones[:, 0:1], ACT.Silu)
            act.wait_ge(cond_t, 1)
            for i in range(2):
                nc.scalar.activation(cond[:, :, COND_AT + i:COND_AT + i + 1], ps[:, 0, i * KT:(i + 1) * KT].unsqueeze(2),
                                     ACT.Silu).then_inc(cond_ready, 1)
            for dst, src in (
                    (rows[0:MODT, 0, :], b_mod[0].rearrange("(r n) -> r n", n=P)),
                    (rows[A_NORM_G:A_ROWS, 0, :], norm_g.rearrange("l s (r n) -> (l s r) n", n=P)),
                    (rows[0:MODT, 1, :], b_mod[1].rearrange("(r n) -> r n", n=P)),
                    (rows[B_CONV_B:B_CONV_B + CT, 1, :], conv_b[0].rearrange("(r n) -> r n", n=P)),
                    (rows[B_CN_G:B_CN_G + CT, 1, :], conv_norm_g[0].rearrange("(r n) -> r n", n=P)),
                    (rows[B_CN_B:B_CN_B + CT, 1, :], conv_norm_b[0].rearrange("(r n) -> r n", n=P)),
                    (rows[B_SN_G:B_SN_G + CT, 1, :], sgu_norm_g[0].rearrange("(r n) -> r n", n=P)),
                    (rows[B_SN_B:B_SN_B + CT, 1, :], sgu_norm_b[0].rearrange("(r n) -> r n", n=P)),
                    (rows[B_QG:B_QG + 1, 1, 0:HD], q_norm_g), (rows[B_QG:B_QG + 1, 1, HD:P], q_norm_g),
                    (rows[B_KG:B_KG + 1, 1, 0:HD], k_norm_g), (rows[B_KG:B_KG + 1, 1, HD:P], k_norm_g),
                    (conv_rows[:, :], conv_w[0])):
                act.dma_start(dst, src).then_inc(vectors_in, 16)

            def split(u, i=0):
                act.wait_ge(raw_in[slot(u)], 32 * (u // RING + 1) + 32 * i)
                act.wait_ge(unit_done, u + 1 + RING * i)
                nc.scalar.activation(w_hi[:, slot(u), :], w_raw[:, slot(u), :], ACT.Copy).then_inc(hi_done, 1)

            def preload(n, func):
                nc.scalar.activation(warm[:, n:n + 1], ones[:, 0:1], func)

            def norm_stats(n):
                preload(n, ACT.Sqrt)
                for d in range(KT):
                    act.wait_ge(x_ready, KT * n + d + 1)
                    nc.scalar.activation(n_sq[:, d, :], x[:, d, :], ACT.Square).then_inc(sq_done, 1)
                act.wait_ge(ms_done, n + 1)
                nc.scalar.activation(stat[:, 4:4 + TT], stat[:, 0:TT], ACT.Sqrt).then_inc(root_done, 1)

            def norm(n):
                for d in range(KT):
                    for cnd, lo, hi in SEGS:
                        act.wait_ge(full_done, 2 * (KT * n + d) + cnd + 1)
                        nc.scalar.activation(a_hi[:, d, lo:hi], n_full[:, d, lo:hi], ACT.Identity,
                                             bias=m_shift[:, n, d, cnd:cnd + 1]).then_inc(a_hi_done, 1)

            def ffn(s):
                u0, f = UNIT0[s], FFN_AT[s]

                def step(t, b, i):
                    split(u0 + t + 2, i)
                    act.wait_ge(unit_done, RING + u0 + t + 1 + RING * i)
                    act.wait_ge(h_ready, FT * f + t + 1 + RING * i)
                    nc.scalar.activation(glu[:, 0, :], ps[:, 2 * b, 0:TOK], ACT.Silu).then_inc(silu_done, 1)
                    act.wait_ge(prod_done, RING + FT * f + t + 1 + RING * i)
                    nc.scalar.activation(h_hi[:, bass.ds(t + RING * i, 1), :], glu[:],
                                         ACT.Copy).then_inc(h_hi_done, 1)

                step(0, 0, 0)
                with act.Fori(0, LOOPS) as i:
                    for b in range(RING):
                        step(1 + b, (1 + b) % RING, i)
                split(u0 + FT + 2)
                ahead = min(FFN_UNITS - FT - 2, UNITS - (u0 + FT + 3))
                with act.Fori(0, ahead // RING) as i:
                    for b in range(RING):
                        split(u0 + FT + 3 + b, i)
                for b in range(ahead // RING * RING, ahead):
                    split(u0 + FT + 3 + b)
                if s < 5:
                    split(u0 + FFN_UNITS + 1)

            norm_stats(0)
            for v in range(2):
                act.wait_ge(rows_t, v + 1)
                nc.scalar.activation((vec_a, vec_b)[v][:], ps[:, 1 + v, 0:(A_ROWS, B_ROWS)[v]], ACT.Copy).then_inc(rows_c, 1)
            act.wait_ge(rows_t, 3)
            nc.scalar.activation(conv_wt[:], ps[:, 3, 0:CT * CONV_K].rearrange("p (a b) -> p a b", a=CT),
                                 ACT.Copy).then_inc(rows_c, 1)
            split(0)
            norm(0)
            split(1)
            ffn(0)

            norm_stats(1)
            norm(1)
            u = UNIT0[1]

            def sigmoid(n, j):
                act.wait_ge(unit_done, RING + u + n + 1)
                if j >= 2:
                    act.wait_ge(glu_done, j - 1)
                nc.scalar.activation(e_sig[:, j % 2, :], ps[:, GLU_BANK[j] + 1, 0:TOK], ACT.Sigmoid).then_inc(sig_done, 1)

            def tap_products(m, k0, k1):
                j = POOL_TILES[m]
                for k in range(k0, k1):
                    w = conv_wt[:, j, k:k + 1]
                    src = padded[:, j, k:k + CONV_N]
                    if k == 0:
                        act.wait_ge(glu_done, j + 1)
                        nc.scalar.activation(conv[:, j, :], src, ACT.Identity, scale=w,
                                             bias=vec_b[:, B_CONV_B + j:B_CONV_B + j + 1]).then_inc(tap_ready, 1)
                        continue
                    n = m * (CONV_K - 1) + k - 1
                    if n >= TAP_BUFS:
                        act.wait_ge(tap_added, n + 1 - TAP_BUFS)
                    nc.scalar.activation(taps_buf[:, n % TAP_BUFS, :], src, ACT.Copy, scale=w).then_inc(tap_ready, 1)

            split(u + 2)
            sigmoid(0, 0)
            split(u + 3)
            tap_products(0, 0, 4)
            sigmoid(1, 1)
            for n in range(2, 5):
                split(u + n + 2)
                tap_products(0, 6 * n - 8, 6 * n - 2)
                act.wait_ge(unit_done, RING + u + n + 1)
                for h in range(2):
                    m = 2 * (n - 2) + h
                    tile = (QT, None, 0, 1, 2, 3)[m]
                    dst = v_raw[:] if tile is None else qk[:, tile, :]
                    nc.scalar.activation(dst, ps[:, QKV_BANK[n] + h, 0:TOK], ACT.Copy).then_inc(qk_copied, 1)
                    if tile is not None:
                        act.wait_ge(qk_copied, m + 1)
                        nc.scalar.activation(qk_sq[:, tile, :], dst, ACT.Square).then_inc(qk_sq_done, 1)
            act.wait_ge(e_t, 1)
            nc.scalar.activation(v_nat[:, 0:TT, :], ps[:, 3, 0:TOK].rearrange("p (a b) -> p a b", a=TT),
                                 ACT.Copy).then_inc(e_tc, 1)
            for g in range(KV_HEADS):
                for o in range(2):
                    nc.scalar.activation(kdup[o * HD:(o + 1) * HD, g, TOK:], ps[g * HD:(g + 1) * HD, 2, 0:PAST],
                                         ACT.Copy).then_inc(kdup_done, 1)
            act.wait_ge(qk_ms, 1)
            nc.scalar.activation(stat_row[:, 0:30], stat[:, 0:30], ACT.Sqrt).then_inc(qk_root, 1)
            split(u + 7)
            tap_products(0, 22, 26)
            sigmoid(5, 2)
            split(u + 8)
            tap_products(0, 26, CONV_K)
            act.wait_ge(e_t, 2)
            nc.scalar.activation(k_nat[:], ps[:, 3, 0:P], ACT.Copy).then_inc(e_tc, 1)
            sigmoid(6, 3)
            preload(6, ACT.Exp)
            act.wait_ge(e_tc, 2)
            act.dma_start(new_cache_k[0, 0].rearrange("t g d -> t (g d)"), k_nat[:]).then_inc(cache_out, 16)
            act.dma_start(new_cache_v[0, 0].rearrange("t g d -> t (g d)"), v_nat[:, 0, :]).then_inc(cache_out, 16)

            def mix_high(j):
                nc.scalar.activation(a_hi[:, j, :], ps[:, j % 2, 0:TOK], ACT.Copy).then_inc(mix_hi, 1)

            tap = 0
            for m in range(PAIR_STEPS + 1):
                if m < PAIR_STEPS:
                    width = CTX if m % TT == 0 else LAT + PAST
                    act.wait_ge(max_done, m + 1)
                    if m >= 2:
                        act.wait_ge(pt_done, 2 * (m - 1))
                    if m == 1:
                        act.wait_ge(glu_done, CT)
                    for h in range(2):
                        n = 2 * m + h
                        ins = nc.scalar.activation(probs(m)[:, h, 0:width], ps[:, SCORE_BANK[m % 2] + h, 0:width], ACT.Exp,
                                                   bias=smaxn[:, n:n + 1], scale=HD ** -0.5, accum_out=ssum[:, n:n + 1])
                    ins.then_inc(exp_done, 1)
                    more = 2 if m == 0 else 1
                    tap_products(1, tap, tap + more)
                    tap += more
                if m >= 1:
                    width = CTX if (m - 1) % TT == 0 else LAT + PAST
                    if m >= 2:
                        act.wait_ge(pv_done, m - 1)
                    for h in range(2):
                        act.wait_ge(pt_done, 2 * (m - 1) + h + 1)
                        nc.scalar.activation(prob_t[:, h, 0:width], ps[:, 6 + h, 0:width], ACT.Copy).then_inc(pt_copied, 1)
                if m < PAIR_STEPS:
                    more = 2 - m % 2
                    tap_products(1, tap, tap + more)
                    tap += more
                if m >= 4 and (m - 4) % TT == 0:
                    mix_high((m - 4) // TT)
            preload(7, ACT.Sqrt)
            act.wait_ge(pv_done, PAIR_STEPS)
            mix_high(QT - 1)
            split(u + 9)

            def layer_norm_root(m, src):
                for j in range(CT):
                    act.wait_ge(ln_xc, CT * m + j + 1)
                    nc.scalar.activation(qk_sq[:, j, :] if m == 0 else o_sq[:, j, :], src[:, j, :],
                                         ACT.Square).then_inc(ln_sq, 1)
                act.wait_ge(ln_ms, m + 1)
                nc.scalar.activation(stat_row[:, 0:TT], stat[:, 0:TT], ACT.Sqrt).then_inc(ln_root, 1)

            layer_norm_root(0, qk)
            preload(8, ACT.Silu)
            split(u + 10)
            for j in range(CT):
                act.wait_ge(ln_y, j + 1)
                nc.scalar.activation(qk[:, j, :], qk_sq[:, j, :], ACT.Silu, bias=vec_b[:, B_CN_B + j:B_CN_B + j + 1],
                                     scale=vec_b[:, B_CN_G + j:B_CN_G + j + 1]).then_inc(ln_out, 1)
                act.wait_ge(ln_out, j + 1)
                nc.scalar.activation(a_hi[:, QT + j, :], qk[:, j, :], ACT.Copy).then_inc(mix_hi, 1)
            split(u + 11)
            split(u + 12)
            act.wait_ge(cache_out, 32)
            norm_stats(2)
            norm(2)
            ffn(2)
            norm_stats(3)
            norm(3)
            ffn(3)

            norm_stats(4)
            norm(4)
            u = UNIT0[4]
            for j in range(6):
                split(u + j + 2)
                act.wait_ge(unit_done, RING + u + j + 1)
                for h in range(2):
                    n = 2 * j + h
                    dst = (o_v, o_f, o_u)[n // CT][:, n % CT, :]
                    nc.scalar.activation(dst, ps[:, O_BANK[j] + h, 0:TOK], ACT.Copy).then_inc(o_copied, 1)
                if j == 2:
                    for k in range(CT):
                        act.wait_ge(ln_xc, CT + k + 1)
                        nc.scalar.activation(o_sq[:, k, :], o_v[:, k, :], ACT.Square).then_inc(ln_sq, 1)
                if j == 4:
                    act.wait_ge(ln_ms, 2)
                    nc.scalar.activation(stat_row[:, 0:TT], stat[:, 0:TT], ACT.Sqrt).then_inc(ln_root, 1)
            for j in range(CT):
                act.wait_ge(ln_y, CT + j + 1)
                nc.scalar.activation(o_v[:, j, :], o_sq[:, j, :], ACT.Identity, bias=vec_b[:, B_SN_B + j:B_SN_B + j + 1],
                                     scale=vec_b[:, B_SN_G + j:B_SN_G + j + 1]).then_inc(ln_out, 1)
            for n in range(2 * TT):
                act.wait_ge(o_z_done, n + 1)
                nc.scalar.activation(o_z[:, n // 2, (n % 2) * 512:(n % 2 + 1) * 512], ps[:, O_ZBANK[n], :],
                                     ACT.Copy).then_inc(o_z_copied, 1)
            act.wait_ge(o_t, 1)
            nc.scalar.activation(ws_t[:], ps[:, 6, :].rearrange("p (a b) -> p a b", a=CT), ACT.Copy).then_inc(o_tc, 1)
            for tt in range(TT):
                act.wait_ge(o_t, tt + 2)
                nc.scalar.activation(o_vn[:, tt, :], ps[:, O_VBANK[tt], :], ACT.Copy).then_inc(o_tc, 1)
            split(u + 8)
            for g in range(CT):
                act.wait_ge(o_four, g + 1)
                for _, lo, hi in SEGS:
                    nc.scalar.activation(a_hi[:, g, lo:hi], ps[:, 4 + g, lo:hi], ACT.Copy,
                                         scale=float((hi - lo) * P) ** -0.5).then_inc(mix_hi, 1)
            for g in range(CT):
                act.wait_ge(o_bias, g + 1)
                nc.scalar.activation(a_hi[:, CT + g, :], o_sq[:, g, :], ACT.Copy).then_inc(mix_hi, 1)
            split(u + 9)
            split(u + 10)
            split(u + 11)
            norm_stats(5)
            norm(5)
            ffn(5)
            for tt in range(TT):
                act.wait_ge(out_t, tt + 1)
                nc.scalar.activation(x_nat[:, tt, :].rearrange("p (a b) -> p a b", a=2), ps[:, 2 * tt:2 * tt + 2, :],
                                     ACT.Copy).then_inc(out_c, 1)

        @block.vector
        def _(dve):
            self_n = [0]

            def mark(ins):
                ins.then_inc(dve_self, 1)
                self_n[0] += 1
                return self_n[0]

            def split(u, i=0):
                dve.wait_ge(hi_done, u + 1 + RING * i)
                nc.vector.tensor_tensor(w_lo[:, slot(u), :], w_raw[:, slot(u), :], w_hi[:, slot(u), :].bitcast(FP32),
                                        ALU.subtract).then_inc(lo_done, 1)

            def part_copy(g, i=0):
                dve.wait_ge(mod_used, MRING * (g + 2) + MRING * i)
                if g:
                    dve.wait_ge(cols_done, g + i)
                nc.vector.tensor_copy(mod_part[:], ps[:, 6, 0:PAIR]).then_inc(part_copied, 1)

            def cols_copy(g, i=0):
                dve.wait_ge(cols_done, g + 1 + i)
                n = MRING * PAIR_TILES
                dst = mod_cols[:, bass.ds(n * g + n * i, n), :].rearrange("p (a q) c -> p q a c", a=MRING)
                nc.vector.tensor_copy(dst, ps[:, 7, 0:2 * n].rearrange("p (q a c) -> p q a c", q=PAIR_TILES, a=MRING)
                                      ).then_inc(cols_copied, 1)

            def groups(tiles):
                return -(-tiles // (MRING * PAIR_TILES))

            def bias(s, which):
                layer, m = s // 3, 3 * (s % 3) + which
                v, base = (vec_a, A_BMOD) if layer == 0 else (vec_b, B_BMOD)
                return v[:, base + m * KT:base + (m + 1) * KT].unsqueeze(2).to_broadcast([P, KT, 2])

            def raw_mod(s, which):
                t = (s // 3) * MODT + (3 * (s % 3) + which) * KT
                return mod_cols[:, t:t + KT, :]

            def modulation_in(s):
                dve.wait_ge(rows_c, 2)
                dve.wait_ge(cols_copied, 1 + groups((3 * s + 2) * KT))
                mark(nc.vector.tensor_tensor(m_shift[:, s], raw_mod(s, 0), bias(s, 0), ALU.add))
                dve.wait_ge(dve_self, mark(nc.vector.tensor_tensor(m_scale[:, s], raw_mod(s, 1), bias(s, 1), ALU.add)))
                g = vec_a[:, A_NORM_G + s * KT:A_NORM_G + (s + 1) * KT].unsqueeze(2).to_broadcast([P, KT, 2])
                dve.wait_ge(dve_self, mark(nc.vector.scalar_tensor_tensor(
                    m_scale[:, s], m_scale[:, s], 1.0, g, ALU.add, ALU.mult)))

            def modulation_gate(s):
                dve.wait_ge(cols_copied, 1 + groups(3 * (s + 1) * KT))
                n = mark(nc.vector.tensor_tensor(m_gate[:, s], raw_mod(s, 2), bias(s, 2), ALU.add))
                dve.wait_ge(dve_self, n)
                if s % 3 != 1:
                    dve.wait_ge(dve_self, mark(nc.vector.tensor_scalar(m_gate[:, s], m_gate[:, s], 0.5, None, ALU.mult)))

            def residual(s, d):
                for cnd, lo, hi in SEGS:
                    ins = nc.vector.scalar_tensor_tensor(x[:, d, lo:hi], ps[:, d, lo:hi], m_gate[:, s, d, cnd:cnd + 1],
                                                         x[:, d, lo:hi], ALU.mult, ALU.add)
                ins.then_inc(x_ready, 1)

            def norm_stats(n, unit=None):
                if unit is not None:
                    split(unit)
                dve.wait_ge(stat_done, n + 1)
                nc.vector.tensor_scalar(stat[:, 0:TT], ps[:, 0, 0:TT], 1.0 / D_MODEL, RMS_EPS,
                                        ALU.mult, ALU.add).then_inc(ms_done, 1)
                dve.wait_ge(root_done, n + 1)
                dve.wait_ge(dve_self, mark(nc.vector.reciprocal(stat[:, 8:8 + TT], stat[:, 4:4 + TT])))
                nc.vector.tensor_tensor(n_diag[:], ident[:].unsqueeze(1).to_broadcast([P, TT, P]),
                                        stat[:, 8:8 + TT].unsqueeze(2).to_broadcast([P, TT, P]), ALU.mult).then_inc(diag_done, 1)

            def norm(n):
                bank = BC_BANK[n]
                dve.wait_ge(bc_done, n + 1)
                for d in range(KT + 1):
                    if d < KT:
                        for cnd, lo, hi in SEGS:
                            nc.vector.scalar_tensor_tensor(n_full[:, d, lo:hi], ps[:, bank, lo:hi],
                                                           m_scale[:, n, d, cnd:cnd + 1], x[:, d, lo:hi],
                                                           ALU.mult, ALU.mult).then_inc(full_done, 1)
                    if d >= 1:
                        e = d - 1
                        for cnd, lo, hi in SEGS:
                            dve.wait_ge(a_hi_done, 2 * (KT * n + e) + cnd + 1)
                            ins = nc.vector.scalar_tensor_tensor(a_lo[:, e, lo:hi], n_full[:, e, lo:hi],
                                                                 m_shift[:, n, e, cnd:cnd + 1],
                                                                 a_hi[:, e, lo:hi].bitcast(FP32), ALU.add, ALU.subtract)
                        ins.then_inc(a_ready, 1)

            def ffn(s):
                u0, f, g0 = UNIT0[s], FFN_AT[s], GROUP0[s]

                def step(t, b, i, group):
                    split(u0 + t + 2, i)
                    if group is not None:
                        part_copy(group, i)
                    dve.wait_ge(silu_done, FT * f + t + 1 + RING * i)
                    nc.vector.tensor_tensor(glu[:, 0, :], glu[:, 0, :], ps[:, 2 * b + 1, 0:TOK],
                                            ALU.mult).then_inc(prod_done, 1)
                    dve.wait_ge(h_hi_done, FT * f + t + 1 + RING * i)
                    nc.vector.tensor_tensor(h_lo[:, bass.ds(t + RING * i, 1), :], glu[:],
                                            h_hi[:, bass.ds(t + RING * i, 1), :].bitcast(FP32),
                                            ALU.subtract).then_inc(h_ready, 1)
                    if group is not None:
                        cols_copy(group, i)

                step(0, 0, 0, None)
                done = 0
                for n, mod in ((MOD_LOOPS[s], True), (LOOPS - MOD_LOOPS[s], False)):
                    if n:
                        with dve.Fori(0, n) as i:
                            for b in range(RING):
                                t = 1 + RING * done + b
                                step(t, (1 + b) % RING, i, g0 if mod and b == RING - 1 else None)
                        done += n
                for g in range(g0 + MOD_LOOPS[s], g0 + MOD_LOOPS[s] + MOD_EXTRA[s]):
                    part_copy(g)
                    cols_copy(g)
                split(u0 + FT + 2)
                ahead = min(FFN_UNITS - FT - 2, UNITS - (u0 + FT + 3))
                with dve.Fori(0, ahead // RING) as i:
                    for b in range(RING):
                        split(u0 + FT + 3 + b, i)
                for b in range(ahead // RING * RING, ahead):
                    split(u0 + FT + 3 + b)
                modulation_gate(s)
                for d in range(KT):
                    if d < KT - 1:
                        dve.wait_ge(y_done, (KT - 1) * f + M_Y[s] + d + 1)
                    else:
                        dve.wait_ge(unit_done, RING + u0 + FFN_UNITS)
                    residual(s, d)
                if s < 5:
                    modulation_in(s + 1)

            dve.sem_inc(lo_done, RING)
            dve.sem_inc(part_copied, 1)
            dve.sem_inc(cols_copied, 1)
            dve.sem_inc(prod_done, RING)
            dve.sem_inc(h_ready, 1)
            dve.wait_ge(const_in, 16)
            nc.vector.tensor_reduce(mod_pick[:], ident[:].rearrange("p (a b) -> p b a", a=4)[:, 0:2 * MRING, :], axis=AX.X,
                                    op=ALU.add).then_inc(pick_ready, 1)
            part_copy(0)
            for d in range(KT):
                dve.wait_ge(x_t, d + 1)
                nc.vector.tensor_copy(x[:, d, :], ps[:, d % 6, 0:TOK]).then_inc(x_ready, 1)
            cols_copy(0)
            norm_stats(0)
            part_copy(1)
            cols_copy(1)
            split(0)
            part_copy(2)
            cols_copy(2)
            modulation_in(0)
            norm(0)
            split(1)
            ffn(0)

            norm_stats(1, UNIT0[1] + 1)
            norm(1)
            u = UNIT0[1]
            tap_at = {}

            def taps(j, k0, k1):
                for k in range(k0, k1):
                    if k == 0:
                        ins = nc.vector.tensor_scalar(conv[:, j, :], padded[:, j, 0:CONV_N], conv_wt[:, j, 0:1],
                                                      vec_b[:, B_CONV_B + j:B_CONV_B + j + 1], ALU.mult, ALU.add)
                    else:
                        dve.wait_ge(dve_self, tap_at[j])
                        ins = nc.vector.scalar_tensor_tensor(conv[:, j, :], padded[:, j, k:k + CONV_N],
                                                             conv_wt[:, j, k:k + 1], conv[:, j, :], ALU.mult, ALU.add)
                    if k < CONV_K - 1:
                        tap_at[j] = mark(ins)
                    else:
                        ins.then_inc(conv_done, 1)

            def glu_mul(j):
                dve.wait_ge(sig_done, j + 1)
                dve.wait_ge(e_zero, 1)
                for sgm, lo, hi in SEGS:
                    ins = nc.vector.tensor_tensor(padded[:, j, PAD_AT[sgm]:PAD_AT[sgm] + hi - lo],
                                                  e_sig[:, j % 2, lo:hi], ps[:, GLU_BANK[j], lo:hi], ALU.mult)
                ins.then_inc(glu_done, 1)

            split(u + 2)
            glu_mul(0)
            dve.wait_ge(rows_c, 3)
            split(u + 3)
            glu_mul(1)
            dve.wait_ge(glu_done, 2)
            taps(1, 0, 8)
            split(u + 4)
            taps(1, 8, 18)
            split(u + 5)
            taps(1, 18, 28)
            split(u + 6)
            NS = 2 * TT * (QT + 1)
            dve.wait_ge(qk_stat, 1)
            nc.vector.tensor_scalar(stat[:, 0:NS], ps[:, 6, 0:NS], 1.0 / HD, RMS_EPS, ALU.mult, ALU.add).then_inc(qk_ms, 1)
            dve.wait_ge(qk_root, 1)
            dve.wait_ge(dve_self, mark(nc.vector.reciprocal(stat_row[:, 0:NS], stat_row[:, 0:NS])))
            nc.vector.tensor_copy(qk_wide[:], stat_row[:, 0:NS].unsqueeze(2).to_broadcast([P, NS, HD])).then_inc(qk_wide_done, 1)
            split(u + 7)
            taps(1, 28, CONV_K)
            glu_mul(2)
            for j in range(QT + 1):
                dve.wait_ge(qk_bc, j + 1)
                col = B_QG if j < QT else B_KG
                nc.vector.scalar_tensor_tensor(qk[:, j, :], qk[:, j, :], vec_b[:, col:col + 1], ps[:, BC_BANKS[j], 0:TOK],
                                               ALU.mult, ALU.mult).then_inc(qk_normed, 1)
            dve.wait_ge(e_in, 48)
            dve.wait_ge(qk_normed, QT + 1)
            a = mark(nc.vector.tensor_tensor(rot[:], qk[:, :, CTX:], rope[:, R_COS:R_COS + LAT].unsqueeze(1)
                                             .to_broadcast([P, QT + 1, LAT]), ALU.mult))
            dve.wait_ge(dve_self, a)
            dve.wait_ge(swap_done, 1)
            for lo, hi, bank in SWAP_BANKS:
                n = hi - lo
                a = mark(nc.vector.tensor_tensor(qk[:, lo:hi, CTX:], ps[:, bank, 0:n * LAT].rearrange("p (c b) -> p c b", c=n),
                                                 rope[:, R_SIN:R_SIN + LAT].unsqueeze(1).to_broadcast([P, n, LAT]), ALU.mult))
            dve.wait_ge(dve_self, a)
            nc.vector.tensor_tensor(qk[:, :, CTX:], qk[:, :, CTX:], rot[:], ALU.add).then_inc(roped, 1)
            dve.wait_ge(roped, 1)
            for g in range(KV_HEADS):
                for o in range(2):
                    nc.vector.tensor_copy(kdup[o * HD:(o + 1) * HD, g, 0:TOK], qk[g * HD:(g + 1) * HD, QT, :]).then_inc(roped, 1)

            def attention(m):
                width = CTX if m % TT == 0 else LAT + PAST
                at = slice(2 * m, 2 * m + 2)
                bank = SCORE_BANK[m % 2]
                dve.wait_ge(score_done, m + 1)
                a = mark(nc.vector.tensor_reduce(smax[:, at], ps[:, bank:bank + 2, 0:width], axis=AX.X, op=ALU.max))
                dve.wait_ge(dve_self, a)
                nc.vector.tensor_scalar(smaxn[:, at], smax[:, at], -(HD ** -0.5), None, ALU.mult).then_inc(max_done, 1)

            def normalize(m):
                width = CTX if m % TT == 0 else LAT + PAST
                dve.wait_ge(exp_done, m + 1)
                dve.wait_ge(dve_self, mark(nc.vector.reciprocal(srec[:, 2 * m:2 * m + 2], ssum[:, 2 * m:2 * m + 2])))
                for h in range(2):
                    buf = probs(m)[:, h, 0:width]
                    ins = nc.vector.tensor_scalar(buf, buf, srec[:, 2 * m + h:2 * m + h + 1], None, ALU.mult)
                ins.then_inc(prob_done, 1)

            def mix_low(j, src):
                dve.wait_ge(mix_hi, j + 1)
                nc.vector.tensor_tensor(a_lo[:, j, :], src, a_hi[:, j, :].bitcast(FP32), ALU.subtract).then_inc(mix_ready, 1)

            split(u + 8)
            dve.wait_ge(glu_done, 3)
            taps(2, 0, EARLY_TAPS)
            attention(0)
            glu_mul(3)
            tap = EARLY_TAPS
            for m in range(PAIR_STEPS):
                if m + 1 < PAIR_STEPS:
                    attention(m + 1)
                normalize(m)
                more = 3 if m % TT == 0 else 2
                taps(2, tap, tap + more)
                tap += more
                if m >= 4 and (m - 4) % TT == 0:
                    j = (m - 4) // TT
                    mix_low(j, ps[:, j % 2, 0:TOK])
            dve.wait_ge(conv_done, len(DVE_TILES))
            dve.wait_ge(tap_added, CONV_K - 1)
            dve.wait_ge(dve_self, mark(nc.vector.tensor_tensor(conv_sum(), conv[:, 0, :], conv[:, 1, :], ALU.add)))
            dve.wait_ge(dve_self, mark(nc.vector.tensor_tensor(conv_sum(), conv_sum(), conv[:, 2, :], ALU.add)))
            dve.wait_ge(tap_added, len(POOL_TILES) * (CONV_K - 1))
            nc.vector.tensor_tensor(conv_sum(), conv_sum(), conv[:, 3, :], ALU.add).then_inc(conv_summed, 1)

            def layer_norm(m, src, dst, sq, at):
                dve.wait_ge(ln_mean_done, m + 1)
                for j in range(CT):
                    for sgm, lo, hi in SEGS:
                        ins = nc.vector.tensor_tensor(dst[:, j, lo:hi], src[:, j, at[sgm]:at[sgm] + hi - lo],
                                                      ps[:, 4, lo:hi], ALU.subtract)
                    ins.then_inc(ln_xc, 1)

            def layer_norm_scale(m, bank, diag):
                dve.wait_ge(ln_stat, m + 1)
                nc.vector.tensor_scalar(stat[:, 0:TT], ps[:, bank, 0:TT], 1.0 / CONV_CH, LN_EPS, ALU.mult, ALU.add).then_inc(ln_ms, 1)
                dve.wait_ge(ln_root, m + 1)
                dve.wait_ge(dve_self, mark(nc.vector.reciprocal(stat[:, 8:8 + TT], stat_row[:, 0:TT])))
                for tt in range(TT):
                    ins = nc.vector.tensor_scalar(diag[:, tt, :], ident[:], stat[:, 8 + tt:9 + tt], None, ALU.mult)
                ins.then_inc(ln_diag, 1)

            mix_low(QT - 1, ps[:, (QT - 1) % 2, 0:TOK])
            layer_norm(0, conv, qk, qk_sq, CONV_AT)
            split(u + 9)
            layer_norm_scale(0, 7, e_diag)
            split(u + 10)
            modulation_gate(1)
            dve.wait_ge(ln_bc, 1)
            for j in range(CT):
                nc.vector.tensor_tensor(qk_sq[:, j, :].rearrange("p (a b) -> p a b", a=TT),
                                        qk[:, j, :].rearrange("p (a b) -> p a b", a=TT),
                                        ps[:, 4:4 + TT, TOK:], ALU.mult).then_inc(ln_y, 1)
            for j in range(CT):
                mix_low(QT + j, qk[:, j, :])
            split(u + 11)
            for d in range(KT):
                if d % 4 < 3:
                    dve.wait_ge(y_done, (KT - 1) + (d // 4) * 3 + d % 4 + 1)
                else:
                    dve.wait_ge(unit_done, RING + u + 10 + d // 4)
                residual(1, d)
            modulation_in(2)
            norm_stats(2, UNIT0[2] + 1)
            norm(2)
            ffn(2)
            norm_stats(3, UNIT0[3] + 1)
            norm(3)
            ffn(3)

            norm_stats(4, UNIT0[4] + 1)
            norm(4)
            u = UNIT0[4]
            split(u + 2)
            split(u + 3)
            split(u + 4)
            layer_norm(1, o_v, o_v, o_sq, [0, CTX])
            split(u + 5)
            split(u + 6)
            layer_norm_scale(1, 5, o_diag)
            split(u + 7)
            dve.wait_ge(ln_bc, 2)
            for j in range(CT):
                nc.vector.tensor_tensor(o_sq[:, j, :], o_v[:, j, :], ps[:, 4, 0:TOK], ALU.mult).then_inc(ln_y, 1)
            split(u + 8)
            for g in range(CT):
                dve.wait_ge(mix_hi, 2 * QT + 2 * g + 2)
                for _, lo, hi in SEGS:
                    ins = nc.vector.scalar_tensor_tensor(a_lo[:, g, lo:hi], ps[:, 4 + g, lo:hi], float((hi - lo) * P) ** -0.5,
                                                         a_hi[:, g, lo:hi].bitcast(FP32), ALU.mult, ALU.subtract)
                ins.then_inc(mix_ready, 1)
            dve.wait_ge(o_in, 16 * (2 + CT))
            dve.wait_ge(ln_out, 2 * CT)
            for g in range(CT):
                dve.wait_ge(o_sgu, g + 1)
                a = mark(nc.vector.tensor_tensor(o_sq[:, g, :].rearrange("p (a b) -> p a b", a=TT),
                                                 ps[:, g, 0:TOK].rearrange("p (a b) -> p a b", a=TT),
                                                 bs[:, g:g + 1, :].to_broadcast([P, TT, P]), ALU.add))
                dve.wait_ge(dve_self, a)
                dve.wait_ge(o_copied, 12)
                nc.vector.tensor_tensor(o_sq[:, g, :], o_sq[:, g, :], o_u[:, g, :], ALU.mult).then_inc(o_bias, 1)
            for g in range(CT):
                dve.wait_ge(mix_hi, 2 * QT + 2 * CT + g + 1)
                nc.vector.tensor_tensor(a_lo[:, CT + g, :], o_sq[:, g, :], a_hi[:, CT + g, :].bitcast(FP32),
                                        ALU.subtract).then_inc(mix_ready, 1)
            modulation_gate(4)
            split(u + 9)
            split(u + 10)
            for d in range(KT):
                if d % 4 < 3:
                    dve.wait_ge(y_done, 3 * (KT - 1) + 6 + (d // 4) * 3 + d % 4 + 1)
                else:
                    dve.wait_ge(unit_done, RING + u + 9 + d // 4)
                residual(4, d)
            modulation_in(5)
            norm_stats(5, UNIT0[5] + 1)
            norm(5)
            ffn(5)

        @block.tensor
        def _(pe):
            mm = nc.tensor.matmul

            def three(out, whi, wlo, mhi, mlo, start, stop):
                mm(out, whi, mhi, start=start, stop=False)
                mm(out, whi, mlo, start=False, stop=False)
                return mm(out, wlo, mhi, start=False, stop=stop)

            def tile_of(w, u, n):
                return w[:, slot(u), n * P:(n + 1) * P]

            def in_unit(u, banks, i=0):
                pe.wait_ge(lo_done, RING + u + 1 + RING * i)
                for k in range(KT):
                    for h in range(2):
                        ins = three(ps[:, banks + h, 0:TOK], tile_of(w_hi, u, h * KT + k), tile_of(w_lo, u, h * KT + k),
                                    a_hi[:, k, :], a_lo[:, k, :], k == 0, k == KT - 1)
                ins.then_inc(unit_done, 1)

            def first_units(u, banks, n, together=True, between=None):
                if not together:
                    for k in range(KT):
                        pe.wait_ge(a_ready, KT * n + k + 1)
                        if k == 0:
                            pe.wait_ge(lo_done, RING + u + 1)
                        for h in range(2):
                            ins = three(ps[:, banks[0] + h, 0:TOK], tile_of(w_hi, u, h * KT + k),
                                        tile_of(w_lo, u, h * KT + k), a_hi[:, k, :], a_lo[:, k, :], k == 0, k == KT - 1)
                    ins.then_inc(unit_done, 1)
                    if between is not None:
                        between()
                    in_unit(u + 1, banks[1])
                    return
                for m in range(2):
                    pe.wait_ge(lo_done, RING + u + m + 1)
                for k in range(KT):
                    pe.wait_ge(a_ready, KT * n + k + 1)
                    for m in range(2):
                        for h in range(2):
                            ins = three(ps[:, banks[m] + h, 0:TOK], tile_of(w_hi, u + m, h * KT + k),
                                        tile_of(w_lo, u + m, h * KT + k), a_hi[:, k, :], a_lo[:, k, :], k == 0, k == KT - 1)
                        if k == KT - 1:
                            ins.then_inc(unit_done, 1)

            def mod_sums(g, b, i=0):
                pe.wait_ge(mod_in[b], 16 * (g + 1) + 16 * i)
                for k in range(KT):
                    j = k % 4
                    ins = mm(ps[32 * j:32 * j + 32, 6, 0:PAIR], cond[:, k, COND_AT - 2 * b:COND_AT - 2 * b + COND_ROWS],
                             m_raw[:, b, k * PAIR:(k + 1) * PAIR], start=b == 0 and k < 4, stop=b == MRING - 1 and k >= 4)
                ins.then_inc(mod_used, 1)

            def mod_columns(g, i=0):
                pe.wait_ge(part_copied, g + 2 + i)
                pe.wait_ge(cols_copied, g + 1 + i)
                n = 2 * MRING
                for q in range(PAIR_TILES):
                    ins = mm(ps[:, 7, q * n:(q + 1) * n], mod_part[:, q * P:(q + 1) * P], mod_pick[:], start=True, stop=True)
                ins.then_inc(cols_done, 1)

            def token_sums(out, src, k, last):
                for tt in range(TT):
                    ins = mm(out[:, tt:tt + 1], src[:, tt * P:(tt + 1) * P], ones[:, 0:1], start=(k == 0 and tt == 0),
                             stop=last, skip_group_check=True)
                return ins

            def spread(bank, diag):
                for tt in range(TT):
                    ins = mm(ps[:, bank, tt * P:(tt + 1) * P], ones[:], diag[:, tt, :], start=True, stop=True)
                return ins

            def norm_sums(n):
                for d in range(ADDED, KT):
                    pe.wait_ge(sq_done, KT * n + d + 1)
                    token_sums(ps[:, 0, :], n_sq[:, d, :], d - ADDED, False)
                pe.wait_ge(acc_done, (ADDED - 1) * (n + 1))
                token_sums(ps[:, 0, :], n_acc[:], 1, True).then_inc(stat_done, 1)

            def norm_spread(n):
                pe.wait_ge(diag_done, n + 1)
                spread(BC_BANK[n], n_diag).then_inc(bc_done, 1)

            def norm(n):
                norm_sums(n)
                norm_spread(n)

            def ffn(s):
                u0, f, g0 = UNIT0[s], FFN_AT[s], GROUP0[s]

                mods = MOD_LOOPS[s]

                def step(t, i, pair):
                    if pair is not None:
                        mod_sums(*pair, i)
                    pe.wait_ge(prod_done, FT * f + t + 1 + RING * i)
                    in_unit(u0 + t, 2 * (t % RING), i)
                    if pair is not None and pair[1] == MRING - 1:
                        mod_columns(pair[0], i)

                if s == 0:
                    first_units(u0, (0, 2), s, False, lambda: mod_sums(g0, 0))
                else:
                    if mods:
                        mod_sums(g0, 0)
                    first_units(u0, (0, 2), s)
                rounds = LOOPS - 1 if mods in (0, LOOPS) else mods - 1
                with pe.Fori(0, rounds) as i:
                    step(2, i, (g0, 1) if mods else None)
                    step(3, i, (g0, 2) if mods else None)
                    step(4, i, (g0 + 1, 0) if mods else None)
                for r in range(rounds, LOOPS):
                    step(2 + RING * r, 0, (g0 + r, 1) if r < mods else None)
                    step(3 + RING * r, 0, (g0 + r, 2) if r < mods else None)
                    if r < LOOPS - 1:
                        step(4 + RING * r, 0, (g0 + r + 1, 0) if r + 1 < mods else None)
                for g in range(g0 + MOD_LOOPS[s], g0 + MOD_LOOPS[s] + MOD_EXTRA[s]):
                    for b in range(MRING):
                        mod_sums(g, b)
                    mod_columns(g)

                def out_unit(u, t, i, first=False):
                    pe.wait_ge(lo_done, RING + u + 1 + RING * i)
                    for h in range(2):
                        fm = bass.ds(2 * t + h + 2 * RING * i, 1)
                        mhi, mlo = h_hi[:, fm, :], h_lo[:, fm, :]
                        for d in (2, 3, 4, 5, 6, 7, 0, 1) if first else range(KT):
                            if first and h == 0 and d in (2, 4, 0):
                                pe.wait_ge(prod_done, RING + FT * f + FT - {2: 2, 4: 1, 0: 0}[d])
                            if first and h == 0 and d == 6 and mods:
                                pe.wait_ge(cols_copied, 1 + g0 + mods + MOD_EXTRA[s])
                            ins = three(ps[:, d:d + 1, 0:TOK], tile_of(w_hi, u, h * KT + d), tile_of(w_lo, u, h * KT + d),
                                        mhi, mlo, first and h == 0, False)
                    ins.then_inc(unit_done, 1)

                pe.wait_ge(h_ready, 1 + FT * f + 2)
                out_unit(u0 + FT, 0, 0, True)
                pe.wait_ge(h_ready, 1 + FT * (f + 1))
                with pe.Fori(0, (FFN_OUT_UNITS - 2) // RING) as i:
                    for b in range(RING):
                        out_unit(u0 + FT + 1 + b, 1 + b, i)
                u = u0 + FFN_UNITS - 1
                pe.wait_ge(lo_done, RING + u + 1)
                for d in range(KT):
                    for h in range(2):
                        ft = FT - 2 + h
                        ins = three(ps[:, d, 0:TOK], tile_of(w_hi, u, h * KT + d), tile_of(w_lo, u, h * KT + d),
                                    h_hi[:, ft, :], h_lo[:, ft, :], False, h == 1)
                    ins.then_inc(y_done if d < KT - 1 else unit_done, 1)

            def proj_out(u, kt0, d0, last, ready, beside=None):
                pe.wait_ge(lo_done, RING + u + 1)
                for d in range(4):
                    for k in range(4):
                        if d == 0:
                            pe.wait_ge(mix_ready, ready + k + 1)
                        at = k * 4 + d
                        ins = three(ps[:, d0 + d, 0:TOK], tile_of(w_hi, u, at), tile_of(w_lo, u, at),
                                    a_hi[:, kt0 + k, :], a_lo[:, kt0 + k, :], not last and k == 0, last and k == 3)
                    if last:
                        ins.then_inc(y_done if d < 3 else unit_done, 1)
                    if d == 2 and beside is not None:
                        beside()
                if not last:
                    ins.then_inc(unit_done, 1)

            pe.sem_inc(unit_done, RING)
            pe.sem_inc(mod_used, MRING)

            pe.wait_ge(const_in, 16)
            pe.wait_ge(cond_in, 32)
            nc.tensor.transpose(ps[:, 0, 0:2 * KT], cond_rows[:], ident[0:2 * KT, 0:2 * KT]).then_inc(cond_t, 1)
            pe.wait_ge(cond_ready, 2)
            for b in range(MRING):
                mod_sums(0, b)
            pe.wait_ge(x_in, 32)
            for d in range(KT):
                if d >= 6:
                    pe.wait_ge(x_ready, d - 5)
                for tt in range(TT):
                    ins = nc.tensor.transpose(ps[:, d % 6, tt * P:(tt + 1) * P], x_nat[:, tt, d * P:(d + 1) * P], ident[:])
                ins.then_inc(x_t, 1)
            pe.wait_ge(pick_ready, 1)
            mod_columns(0)
            mod_sums(1, 0)
            pe.wait_ge(x_ready, KT)
            norm_sums(0)
            pe.wait_ge(vectors_in, 16 * 13)
            for v in range(2):
                n = (A_ROWS, B_ROWS)[v]
                nc.tensor.transpose(ps[:, 1 + v, 0:n], rows[0:n, v, :], ident[0:n, 0:n]).then_inc(rows_t, 1)
            for j in range(CT):
                ins = nc.tensor.transpose(ps[:, 3, j * CONV_K:(j + 1) * CONV_K], conv_rows[:, j * P:(j + 1) * P],
                                          ident[0:CONV_K, 0:CONV_K])
            ins.then_inc(rows_t, 1)
            norm_spread(0)
            for b in range(1, MRING):
                mod_sums(1, b)
            mod_columns(1)
            pe.wait_ge(rows_c, 3)
            for b in range(MRING):
                mod_sums(2, b)
            mod_columns(2)
            ffn(0)

            norm(1)
            u = UNIT0[1]
            first_units(u, GLU_BANK, 1, False)
            in_unit(u + 2, QKV_BANK[2])
            in_unit(u + 3, QKV_BANK[3])

            def qk_sums(j):
                pe.wait_ge(qk_sq_done, (j + 1) % (QT + 1) + 1)
                for tt in range(TT):
                    n = 2 * (TT * j + tt)
                    ins = mm(ps[:, 6, n:n + 2], qk_sq[:, j, tt * P:(tt + 1) * P], pick_half[:], start=True, stop=True)
                return ins

            pe.wait_ge(e_zero, 4)
            pe.wait_ge(glu_done, 2)
            qk_sums(QT)
            in_unit(u + 4, QKV_BANK[4])
            qk_sums(0)
            qk_sums(1)
            pe.wait_ge(e_in, 48)
            pe.wait_ge(qk_copied, 4)
            nc.tensor.transpose(ps[:, 2, 0:P], ck_nat[:], ident[:])
            for tt in range(TT):
                ins = nc.tensor.transpose(ps[:, 3, tt * P:(tt + 1) * P], v_raw[:, tt * P:(tt + 1) * P], ident[:])
            ins.then_inc(e_t, 1)
            qk_sums(2)
            qk_sums(3).then_inc(qk_stat, 1)
            in_unit(u + 5, GLU_BANK[2])
            pe.wait_ge(qk_copied, QT + 2)
            pe.wait_ge(qk_wide_done, 1)
            pe.wait_ge(kdup_done, 4)
            for j in range(QT + 1):
                for tt in range(TT):
                    n = 2 * (TT * j + tt)
                    ins = mm(ps[:, BC_BANKS[j], tt * P:(tt + 1) * P], qk_wide[:, n:n + 2, :].rearrange("p a b -> p (a b)"),
                             ident[:], start=True, stop=True)
                ins.then_inc(qk_bc, 1)
            pe.wait_ge(qk_normed, 3)
            for lo, hi, bank in SWAP_BANKS:
                for j in range(lo, hi):
                    pe.wait_ge(qk_normed, j + 1)
                    ins = mm(ps[:, bank, (j - lo) * LAT:(j - lo + 1) * LAT], rope[:, R_SWAP:R_SWAP + P], qk[:, j, CTX:],
                             start=True, stop=True)
            ins.then_inc(swap_done, 1)
            nc.tensor.transpose(ps[:, 3, 0:P], qk[:, QT, 0:CTX], ident[:]).then_inc(e_t, 1)
            in_unit(u + 6, GLU_BANK[3])
            pe.wait_ge(glu_done, 3)
            pe.wait_ge(roped, 5)
            pe.wait_ge(kdup_done, 4)
            pe.wait_ge(e_tc, 2)
            def scores(m):
                j, tt = m // TT, m % TT
                keys = slice(0, CTX) if tt == 0 else slice(CTX, TOK + PAST)
                if m >= 2:
                    pe.wait_ge(exp_done, m - 1)
                for h in range(2):
                    o = h * HD
                    ins = mm(ps[:, SCORE_BANK[m % 2] + h, 0:keys.stop - keys.start], qk[o:o + HD, j, tt * P:(tt + 1) * P],
                             kdup[o:o + HD, j // 2, keys], start=True, stop=True)
                ins.then_inc(score_done, 1)

            def flip(m):
                pe.wait_ge(prob_done, m + 1)
                if m == 0:
                    pe.wait_ge(glu_done, CT)
                for h in range(2):
                    if m:
                        pe.wait_ge(pt_copied, 2 * m + h - 1)
                    for k in range(1 if m % TT == 0 else 3):
                        ins = nc.tensor.transpose(ps[:, 6 + h, k * P:(k + 1) * P], probs(m)[:, h, k * P:(k + 1) * P], ident[:])
                    ins.then_inc(pt_done, 1)

            def values(m):
                j, tt = m // TT, m % TT
                tiles = [0] if tt == 0 else [1, 2, 3]
                pe.wait_ge(pt_copied, 2 * m + 2)
                if tt == 0 and j >= 2:
                    pe.wait_ge(mix_ready, j - 1)
                for k, v in enumerate(tiles):
                    for h in range(2):
                        ins = mm(ps[h * HD:(h + 1) * HD, j % 2, tt * P:(tt + 1) * P],
                                 v_nat[:, v, (j // 2) * HD:(j // 2 + 1) * HD], prob_t[:, h, k * P:(k + 1) * P],
                                 start=k == 0, stop=k == len(tiles) - 1)
                ins.then_inc(pv_done, 1)

            scores(0)
            scores(1)
            for m in range(PAIR_STEPS):
                if m + 2 < PAIR_STEPS:
                    scores(m + 2)
                if m:
                    values(m - 1)
                flip(m)
            values(PAIR_STEPS - 1)

            def means(src, at):
                for sgm, lo, hi in SEGS:
                    ins = mm(ps[:, 4, lo:hi], ones_mean[:], src[:, at[sgm]:at[sgm] + hi - lo], start=True, stop=True)
                ins.then_inc(ln_mean_done, 1)

            def variances(m, sq, bank):
                pe.wait_ge(ln_added, (CT - 1) * (m + 1))
                token_sums(ps[:, bank, :], sq[:, 0, :], 0, True).then_inc(ln_stat, 1)

            pe.wait_ge(conv_summed, 1)
            means(conv_sum(), CONV_AT)
            proj_out(u + 7, 0, 0, False, 0)
            variances(0, qk_sq, 7)
            pe.wait_ge(ln_ms, 1)

            def spread_beside():
                pe.wait_ge(ln_diag, 1)
                for tt in range(TT):
                    ins = mm(ps[:, 4 + tt, TOK:], ones[:], e_diag[:, tt, :], start=False, stop=False, skip_group_check=True)
                ins.then_inc(ln_bc, 1)

            proj_out(u + 8, 0, 4, False, 0, spread_beside)
            pe.wait_ge(ln_y, CT)
            proj_out(u + 9, 4, 0, True, QT)
            proj_out(u + 10, 4, 4, True, QT)
            norm(2)
            ffn(2)
            norm(3)
            ffn(3)

            norm(4)
            u = UNIT0[4]
            first_units(u, O_BANK, 4)
            in_unit(u + 2, O_BANK[2])
            pe.wait_ge(v_summed, CT - 1)
            means(o_vn[:, 0, 0:TOK], [0, CTX])
            in_unit(u + 3, O_BANK[3])
            in_unit(u + 4, O_BANK[4])
            variances(1, o_sq, 5)
            pe.wait_ge(o_copied, 6)
            in_unit(u + 5, O_BANK[5])
            pe.wait_ge(ln_diag, 2)
            spread(4, o_diag).then_inc(ln_bc, 1)
            pe.wait_ge(o_in, 16 * (2 + CT))
            for n in range(2 * TT):
                tt, h = n // 2, n % 2
                if n < 5:
                    pe.wait_ge(o_copied, (8, 8, 10, 10, 10)[n])
                else:
                    pe.wait_ge(o_z_copied, 1)
                for gg in range(2):
                    ins = mm(ps[:, O_ZBANK[n], gg * 2 * P:(gg + 1) * 2 * P], o_f[:, 2 * h + gg, tt * P:(tt + 1) * P],
                             fourier[:, F_CH:F_CH + 2 * P], start=True, stop=True)
                ins.then_inc(o_z_done, 1)
            pe.wait_ge(o_copied, 12)
            for g in range(CT):
                ins = nc.tensor.transpose(ps[:, 6, g * P:(g + 1) * P], ws_nat[:, g, :], ident[:])
            ins.then_inc(o_t, 1)
            pe.wait_ge(ln_out, 2 * CT)
            pe.wait_ge(o_z_copied, 3)
            for tt in range(TT):
                for j in range(CT):
                    ins = nc.tensor.transpose(ps[:, O_VBANK[tt], j * P:(j + 1) * P], o_v[:, j, tt * P:(tt + 1) * P], ident[:])
                ins.then_inc(o_t, 1)
            pe.wait_ge(o_z_copied, 6)
            pe.wait_ge(o_tc, 2)
            for g in range(CT):
                for cs in range(2):
                    z = slice(g * 2 * P + cs * P, g * 2 * P + (cs + 1) * P)
                    mm(ps[:, 4 + g, 0:CTX], o_z[:, 0, z], fourier[:, F_CTX + cs * P:F_CTX + (cs + 1) * P],
                       start=cs == 0, stop=cs == 1)
                for cs in range(2):
                    z = slice(g * 2 * P + cs * P, g * 2 * P + (cs + 1) * P)
                    for lt in range(2):
                        at = F_LAT + (2 * lt + cs) * LAT
                        ins = mm(ps[:, 4 + g, CTX:TOK], o_z[:, 1 + lt, z], fourier[:, at:at + LAT],
                                 start=cs == 0 and lt == 0, stop=cs == 1 and lt == 1)
                ins.then_inc(o_four, 1)
            pe.wait_ge(o_tc, 1 + TT)
            for g in range(CT):
                for tt in range(TT):
                    ins = mm(ps[:, g, tt * P:(tt + 1) * P], o_vn[:, tt, g * P:(g + 1) * P], ws_t[:, g, :], start=True, stop=True)
                ins.then_inc(o_sgu, 1)
            proj_out(u + 6, 0, 4, False, 2 * QT)
            pe.wait_ge(o_bias, CT)
            proj_out(u + 7, 0, 0, False, 2 * QT)
            proj_out(u + 8, 4, 0, True, 3 * QT)
            proj_out(u + 9, 4, 4, True, 3 * QT)
            norm(5)
            ffn(5)
            pe.wait_ge(x_ready, KT * (N_SUB + 1))
            for tt in range(TT):
                for d in range(KT):
                    ins = nc.tensor.transpose(ps[:, 2 * tt + d // 4, (d % 4) * P:(d % 4 + 1) * P],
                                              x[:, d, tt * P:(tt + 1) * P], ident[:])
                ins.then_inc(out_t, 1)


FFN_AT = {0: 0, 2: 1, 3: 2, 5: 3}
M_Y = {0: 0, 2: 6, 3: 6, 5: 12}
O_BANK = [0, 2, 6, 0, 2, 6]
O_ZBANK = [0, 1, 2, 3, 5, 0]
O_VBANK = [7, 1, 2]
GLU_BANK = [0, 6, 4, 6]
QKV_BANK = {2: 2, 3: 4, 4: 0}
BC_BANKS = [0, 1, 2, 3, 7]
SWAP_BANKS = [(0, 2, 2), (2, 4, 0), (4, 5, 1)]
ADDED = KT - 2
SCORE_BANK = [4, 2]
PAIR_STEPS = QT * TT
BC_BANK = [5, 5, 7, 7, 7, 7]

_INS = ["x_prompt", "x_sample", "cache_k", "cache_v", "c", "c_ctx", "w_mod", "b_mod", "norm_g", "ffn_w_in",
        "ffn_w_out", "ev_w_in", "ev_w_out", "q_norm_g", "k_norm_g", "conv_w", "conv_b", "conv_norm_g",
        "conv_norm_b", "od_w_in", "od_w_out", "sgu_norm_g", "sgu_norm_b", "sgu_w", "sgu_b"]
_OUTS = [(1, CTX, D_MODEL), (1, LAT, D_MODEL), (1, 1, CTX, KV_HEADS, HD), (1, 1, CTX, KV_HEADS, HD)]


def kernel(**inputs):
    import concourse.bacc as bacc
    from concourse.bass_utils import run_bass_kernel_spmd

    nc = bacc.Bacc("TRN2", target_bir_lowering=False, num_devices=1)
    named = {n: np.ascontiguousarray(inputs[n]) for n in _INS}
    named.update(zip(("k_ident", "k_rope", "k_fourier"), shape_constants()))
    arrays, args = {}, []
    for name, a in named.items():
        arrays[f"in_{name}"] = a
        args.append(nc.dram_tensor(f"in_{name}", a.shape, mybir.dt.from_np(a.dtype), kind="ExternalInput").ap())
    for i, shape in enumerate(_OUTS):
        args.append(nc.dram_tensor(f"out_{i}", shape, FP32, kind="ExternalOutput").ap())
    build(nc, *args)
    result = run_bass_kernel_spmd(nc, [arrays], core_ids=[0])
    return tuple(result.results[0][f"out_{i}"] for i in range(len(_OUTS)))
```
